# Optimizing a Trainium2 kernel written in Bass

```python
import math, functools
import jax, jax.numpy as jnp
from jax import lax
import numpy as np

D_MODEL = 1024
BATCH = 1
SEQ = 256
DEPTH = 1
DEC_BATCH = 1
DEC_SEQ = 2048
PAST_LEN = 512

GRID_W = 64
D_MIX = D_MODEL
D_A = D_MIX // 4
A_HEADS = 4
A_HEAD_DIM = D_A // A_HEADS
CHUNK = 128
D_B = D_MIX // 4
B_GROUPS = 4
B_GROUP_DIM = D_B // B_GROUPS
D_C = D_MIX - D_A - D_B
C_HEAD_DIM = 64
C_HEADS = D_C // C_HEAD_DIM
P_IN = 2 * D_A + D_B + 3 * D_C
NA_ROWS = 8
NA_KW = 16
NA_QB = 16
NA_BAND = NA_QB + NA_KW
ATTN_QBLK = 128
D_FF = 2816
CONV_W = 3
ALPHA = (2 * DEPTH) ** 0.25
BETA = (8 * DEPTH) ** -0.25
LN_EPS = 1e-6

kernel_name = "hybrid_gmlp_fnet_natten_diffusion_step"

def _norm(x):
    xf = x.astype(jnp.float32)
    mu = xf.mean(-1, keepdims=True)
    var = jnp.square(xf - mu).mean(-1, keepdims=True)
    return ((xf - mu) * lax.rsqrt(var + LN_EPS)).astype(x.dtype)

def _affine_ln(x, g, b):
    return _norm(x) * g + b

def _chunk_gmlp(z, ws, bs):
    B, L, _ = z.shape
    z = jax.nn.gelu(z)
    u, v = jnp.split(z, 2, axis=-1)
    v = _norm(v).reshape(B, L // CHUNK, CHUNK, A_HEADS, A_HEAD_DIM)
    v = jnp.einsum('hpq,bnqhd->bnphd', ws, v) + bs.T[None, None, :, :, None]
    return u * v.reshape(B, L, D_A)

def _fourier(z, fw):
    B, L, _ = z.shape
    zg = z.reshape(B, L, B_GROUPS, B_GROUP_DIM).astype(jnp.float32)
    zf = jnp.fft.fft2(zg, axes=(1, 3), norm='ortho').real.astype(z.dtype)
    return jnp.einsum('blgc,gcd->blgd', zf, fw).reshape(B, L, D_B)

def _conv_ffn(h, w_gu, conv_w, conv_b, w_down):
    g, u = jnp.split(h @ w_gu, 2, axis=-1)
    L = g.shape[1]
    pad = CONV_W // 2
    gp = jnp.pad(g, ((0, 0), (pad, pad), (0, 0)))
    gc = conv_b
    for t in range(CONV_W):
        gc = gc + gp[:, t:t + L] * conv_w[t]
    return (jax.nn.silu(gc) * u) @ w_down

def _context_attention(q, k, v):
    B, L, H, d = q.shape
    scale = d ** -0.5
    qb = q.reshape(B, L // ATTN_QBLK, ATTN_QBLK, H, d).transpose(1, 0, 2, 3, 4)

    def blk(qi):
        s = jnp.einsum('bqhd,bkhd->bhqk', qi, k).astype(jnp.float32) * scale
        p = jax.nn.softmax(s, axis=-1).astype(v.dtype)
        return jnp.einsum('bhqk,bkhd->bqhd', p, v)

    o = lax.map(blk, qb)
    return o.transpose(1, 0, 2, 3, 4).reshape(B, L, H * d)

def _neighbourhood_attention(q, k, v, kc, vc, rpb):
    B, L, H, d = q.shape
    R = L // GRID_W
    kh = min(NA_ROWS, R)
    scale = d ** -0.5
    nb = GRID_W // NA_QB
    cols = np.arange(GRID_W)
    col_start = np.clip(cols - NA_KW // 2, 0, GRID_W - NA_KW).reshape(nb, NA_QB)
    band_start = np.clip(np.arange(nb) * NA_QB - NA_KW // 2, 0, GRID_W - NA_BAND)
    band_cols = band_start[:, None] + np.arange(NA_BAND)
    qcols = cols.reshape(nb, NA_QB)
    kcols = band_cols[:, None, :]
    in_win = (kcols >= col_start[:, :, None]) & (kcols < col_start[:, :, None] + NA_KW)
    col_idx = np.clip(kcols - qcols[:, :, None] + NA_KW - 1, 0, 2 * NA_KW - 2)
    mask = in_win[:, :, None, :]
    qg = q.reshape(B, R, GRID_W, H, d)
    kg = k.reshape(B, R, GRID_W, H, d)
    vg = v.reshape(B, R, GRID_W, H, d)
    n_loc = kh * NA_BAND

    def row(r):
        rs = jnp.clip(r - kh // 2, 0, R - kh)
        kr = lax.dynamic_slice_in_dim(kg, rs, kh, axis=1)
        vr = lax.dynamic_slice_in_dim(vg, rs, kh, axis=1)
        kb = kr[:, :, band_cols]
        vb = vr[:, :, band_cols]
        qr = lax.dynamic_index_in_dim(qg, r, axis=1, keepdims=False).reshape(B, nb, NA_QB, H, d)
        row_idx = rs + jnp.arange(kh) - r + NA_ROWS - 1
        bias = rpb[:, row_idx][:, :, col_idx].transpose(0, 2, 3, 1, 4)
        s_loc = jnp.einsum('bjqhd,bkjwhd->bhjqkw', qr, kb).astype(jnp.float32) * scale
        s_loc = jnp.where(mask, s_loc + bias.astype(jnp.float32)[None], -jnp.inf)
        s_loc = s_loc.reshape(B, H, nb, NA_QB, n_loc)
        s_ctx = jnp.einsum('bjqhd,bchd->bhjqc', qr, kc).astype(jnp.float32) * scale
        p = jax.nn.softmax(jnp.concatenate([s_loc, s_ctx], axis=-1), axis=-1).astype(v.dtype)
        p_loc = p[..., :n_loc].reshape(B, H, nb, NA_QB, kh, NA_BAND)
        p_ctx = p[..., n_loc:]
        o = (jnp.einsum('bhjqkw,bkjwhd->bjqhd', p_loc, vb)
             + jnp.einsum('bhjqc,bchd->bjqhd', p_ctx, vc))
        return o.reshape(B, GRID_W, H * d)

    o = lax.map(row, jnp.arange(R))
    return o.transpose(1, 0, 2, 3).reshape(B, L, H * d)

def _layer(x, mod, w_in, a_ws, a_bs, f_w, w_out, ln1_g, ln1_b,
           w_gu, conv_w, conv_b, w_down, ln2_g, ln2_b, attend):
    shift1, scale1, gate1, shift2, scale2, gate2 = jnp.split(mod, 6, axis=-1)
    B, L, _ = x.shape
    h = _norm(x) * (1 + scale1) + shift1
    z = h @ w_in
    o1 = 2 * D_A
    o2 = o1 + D_B
    o3 = o2 + D_C
    o4 = o3 + D_C
    za, zb, q, k, v = jnp.split(z, [o1, o2, o3, o4], axis=-1)
    q = q.reshape(B, L, C_HEADS, C_HEAD_DIM)
    k = k.reshape(B, L, C_HEADS, C_HEAD_DIM)
    v = v.reshape(B, L, C_HEADS, C_HEAD_DIM)
    y = jnp.concatenate([_chunk_gmlp(za, a_ws, a_bs), _fourier(zb, f_w), attend(q, k, v)], axis=-1) @ w_out
    x = _affine_ln(ALPHA * x + gate1 * y, ln1_g, ln1_b)
    h = _norm(x) * (1 + scale2) + shift2
    x = _affine_ln(ALPHA * x + gate2 * _conv_ffn(h, w_gu, conv_w, conv_b, w_down), ln2_g, ln2_b)
    return x, k, v

def setup_inputs(seed: int = 0) -> dict:
    key = jax.random.key(seed)
    ks = jax.random.split(key, 24)
    n = lambda i, shape, s=1.0: jax.random.normal(ks[i], shape, jnp.float32) * s
    return {
        'x_prompt': n(0, (BATCH, SEQ, D_MODEL)),
        'x_sample': n(1, (DEC_BATCH, DEC_SEQ, D_MODEL)),
        'cache_k': n(2, (DEC_BATCH, DEPTH, PAST_LEN, C_HEADS, C_HEAD_DIM)),
        'cache_v': n(3, (DEC_BATCH, DEPTH, PAST_LEN, C_HEADS, C_HEAD_DIM)),
        'c': n(4, (DEC_BATCH, D_MODEL)),
        'c_ctx': n(5, (D_MODEL,)),
        'w_ada': n(6, (DEPTH, D_MODEL, 6 * D_MODEL), 0.5 * D_MODEL ** -0.5),
        'b_ada': n(7, (DEPTH, 6 * D_MODEL), 0.01),
        'w_in': n(8, (DEPTH, D_MODEL, P_IN), D_MODEL ** -0.5),
        'a_ws': n(9, (DEPTH, A_HEADS, CHUNK, CHUNK), CHUNK ** -0.5),
        'a_bs': 1.0 + n(10, (DEPTH, A_HEADS, CHUNK), 0.1),
        'f_w': n(11, (DEPTH, B_GROUPS, B_GROUP_DIM, B_GROUP_DIM), B_GROUP_DIM ** -0.5),
        'rpb': n(12, (DEPTH, C_HEADS, 2 * NA_ROWS - 1, 2 * NA_KW - 1), 0.5),
        'w_out': n(13, (DEPTH, D_MIX, D_MODEL), BETA * D_MIX ** -0.5),
        'ln1_g': 1.0 + n(14, (DEPTH, D_MODEL), 0.05),
        'ln1_b': n(15, (DEPTH, D_MODEL), 0.01),
        'w_gu': n(16, (DEPTH, D_MODEL, 2 * D_FF), D_MODEL ** -0.5),
        'conv_w': n(17, (DEPTH, CONV_W, D_FF), CONV_W ** -0.5),
        'conv_b': n(18, (DEPTH, D_FF), 0.01),
        'w_down': n(19, (DEPTH, D_FF, D_MODEL), BETA * D_FF ** -0.5),
        'ln2_g': 1.0 + n(20, (DEPTH, D_MODEL), 0.05),
        'ln2_b': n(21, (DEPTH, D_MODEL), 0.01),
    }

def reference(x_prompt, x_sample, cache_k, cache_v, c, c_ctx, w_ada, b_ada, w_in, a_ws, a_bs,
              f_w, rpb, w_out, ln1_g, ln1_b, w_gu, conv_w, conv_b, w_down, ln2_g, ln2_b):
    xp = x_prompt
    xs = x_sample
    new_ks = []
    new_vs = []
    for l in range(DEPTH):
        shared = (w_in[l], a_ws[l], a_bs[l], f_w[l], w_out[l], ln1_g[l], ln1_b[l],
                  w_gu[l], conv_w[l], conv_b[l], w_down[l], ln2_g[l], ln2_b[l])
        mod_ctx = (jax.nn.silu(c_ctx) @ w_ada[l] + b_ada[l])[None, None, :]
        xp, k_l, v_l = _layer(xp, mod_ctx, *shared, attend=_context_attention)
        new_ks.append(k_l)
        new_vs.append(v_l)
        mod_lat = (jax.nn.silu(c) @ w_ada[l] + b_ada[l])[:, None, :]
        attend_lat = functools.partial(_neighbourhood_attention, kc=cache_k[:, l], vc=cache_v[:, l], rpb=rpb[l])
        xs, _, _ = _layer(xs, mod_lat, *shared, attend=attend_lat)
    new_k = jnp.stack(new_ks, axis=1)
    new_v = jnp.stack(new_vs, axis=1)
    return (xp, xs, new_k, new_v)


_drawn_inputs = setup_inputs


def setup_inputs(seed=0):
    import zlib

    import numpy as np

    out = dict(_drawn_inputs(seed))
    spreads = {}
    factors = {'cache_k': 64.0,
     'cache_v': 64.0,
     'b_ada': 4.319,
     'a_bs': 8.0,
     'rpb': 64.0,
     'ln1_b': 5.684,
     'conv_b': 52.964,
     'ln2_b': 5.511}
    for name, (base, spread) in spreads.items():
        noise = np.random.default_rng([zlib.crc32(name.encode()), seed]).standard_normal(out[name].shape)
        drawn = base * np.exp(spread * noise) if base else spread * noise
        out[name] = __import__('jax').numpy.asarray(drawn.astype(out[name].dtype))
    for name, factor in factors.items():
        out[name] = (out[name] * factor).astype(out[name].dtype)
    return out
```

```python
from contextlib import ExitStack

import concourse.bass as bass
from concourse import mybir

F32 = mybir.dt.float32
F32R = mybir.dt.float32r
FP16 = mybir.dt.float16
BF16 = mybir.dt.bfloat16
ALU = mybir.AluOpType
ACT = mybir.ActivationFunctionType
AX_X = mybir.AxisListType.X

P = 128
D = 1024
KT = D // P
T_LAT, T_CTX, T_PAST = 2048, 256, 512
T_ALL = T_LAT + T_CTX
D_A, D_B, D_C = 256, 256, 512
HEADS, HD = 8, 64
A_HEADS = 4
GRID = 64
P_IN = 2 * D_A + D_B + 3 * D_C
COL_ZA, COL_ZB, COL_Q, COL_K, COL_V = 0, 512, 768, 1280, 1792
D_FF = 2816
REL_ROWS, REL_COLS = 15, 31
RPB = HEADS * REL_ROWS * REL_COLS
RPB_PAD = 64
MASKED = -1e30
FT = D_FF // P
ALPHA = 2.0 ** 0.25
EPS = 1e-6
HI, LO = 0, 1
PASSES = ((HI, HI), (HI, LO), (LO, HI))
LAT, CTX = 0, 1
SHIFT1, SCALE1, GATE1, SHIFT2, SCALE2, GATE2 = range(6)


def phase_tools(nc, ctx):
    def sb(name, shape, dt=F32):
        return ctx.enter_context(nc.sbuf_tensor(name, shape, dt))

    def ps(name, shape, dt=F32):
        return ctx.enter_context(nc.psum_tensor(name, shape, dt))

    def sem(name):
        return nc.alloc_semaphore(name)

    return sb, ps, sem


def modulation_phase(nc, conds, w_ada, b_ada, cache_k, cache_v, rpb, ident_in, mod, k_t, v_parts, rpb_pad, rel_bias):
    with ExitStack() as ctx:
        sb, ps, sem = phase_tools(nc, ctx)
        COLS, SLOTS = 512, 4
        N = 6 * D // COLS
        w = sb("ada_w", [P, SLOTS, KT, COLS])
        cond = sb("ada_cond", [P, 2, KT])
        act = sb("ada_silu", [P, KT, 2])
        bias = sb("ada_bias", [2, 6 * D])
        row = sb("ada_row", [2, 6 * D])
        acc = ps("ada_acc", [P, SLOTS, 512])
        small_loaded = sem("ada_small_loaded")
        w_loaded = [sem(f"ada_w_loaded{s}") for s in range(SLOTS)]
        silu_done = sem("ada_silu_done")
        acc_done = sem("ada_acc_done")
        acc_read = sem("ada_acc_read")
        stored = sem("ada_stored")
        CT = T_PAST // P
        ident = sb("ada_ident", [P, P])
        kc = sb("ada_kc", [P, CT, D_C])
        kct = [sb(f"ada_kct{h}", [P, D_C // P, T_PAST]) for h in (HI, LO)]
        vc = sb("ada_vc", [P, CT, HEADS, HD])
        vparts = sb("ada_vparts", [P, CT, HEADS, 3, HD], BF16)
        bias_row = sb("ada_bias_row", [1, RPB_PAD + RPB + RPB_PAD])
        kps = ps("ada_kps", [P, D_C // P, T_PAST])
        kc_loaded, kc_turned, kc_hi, kc_lo, kc_stored = (
            sem("ada_kc_loaded"), sem("ada_kc_turned"), sem("ada_kc_hi"), sem("ada_kc_lo"), sem("ada_kc_stored"))
        vc_loaded, vc_step, vc_stored = sem("ada_vc_loaded"), sem("ada_vc_step"), sem("ada_vc_stored")
        bias_zeroed, bias_loaded, bias_stored = sem("ada_bias_zeroed"), sem("ada_bias_loaded"), sem("ada_bias_stored")
        w_cols = w_ada.rearrange("l (k p) (n c) -> (l n) p k c", p=P, c=COLS)

        with nc.Block() as block:
            @block.sync
            def _(sp):
                with nc.allow_non_contiguous_dma(reason="two conditioning vectors, channel on partition"):
                    for v in (LAT, CTX):
                        sp.dma_start(cond[:, v, :], conds[v].rearrange("(k p) -> p k", p=P)).then_inc(small_loaded, 16)
                for v in range(2):
                    sp.dma_start(bias[v:v + 1, :], b_ada).then_inc(small_loaded, 16)
                sp.dma_start(ident[:, :], ident_in).then_inc(kc_loaded, 16)
                sp.dma_start(kc[:, :, :], cache_k.rearrange("b l (n p) h d -> p (b l n) (h d)", p=P)).then_inc(kc_loaded, 16)
                sp.dma_start(vc[:, :, :, :], cache_v.rearrange("b l (n p) h d -> p (b l n) h d", p=P)).then_inc(vc_loaded, 16)
                sp.wait_ge(bias_zeroed, 1)
                sp.dma_start(bias_row[:, RPB_PAD:RPB_PAD + RPB], rpb.rearrange("l h r c -> l (h r c)")).then_inc(bias_loaded, 16)
                with sp.Fori(0, N // SLOTS) as i:
                    for s in range(SLOTS):
                        sp.wait_ge(acc_done, i * SLOTS + s + 1)
                        sp.dma_start(w[:, s], w_cols[i * SLOTS + s]).then_inc(w_loaded[s], 16)
                sp.wait_ge(bias_loaded, 16)
                sp.dma_start(rpb_pad, bias_row[:, :]).then_inc(bias_stored, 16)
                sp.wait_ge(kc_lo, D_C // P)
                for part in (HI, LO):
                    sp.dma_start(k_t[part, :, T_ALL:T_ALL + T_PAST].rearrange("(m p) t -> p m t", p=P), kct[part][:, :, :]).then_inc(kc_stored, 16)
                sp.wait_ge(vc_step, 5)
                sp.dma_start(v_parts[T_ALL:T_ALL + T_PAST, :].rearrange("(n p) c -> p n c", p=P),
                             vparts[:, :, :, :, :].rearrange("p n h k d -> p n (h k d)")).then_inc(vc_stored, 16)
                sp.wait_ge(bias_stored, 16)
                shifted = bass.AP(rpb_pad.tensor, RPB_PAD + REL_COLS // 2, [[REL_COLS, HEADS * REL_ROWS], [-1, GRID], [1, GRID]])
                sp.dma_start(rel_bias.rearrange("q r k -> r q k"), shifted).then_inc(bias_stored, 16)
                sp.wait_ge(kc_stored, 32)
                sp.wait_ge(vc_stored, 16)
                sp.wait_ge(bias_stored, 32)
                sp.wait_ge(acc_read, N + SLOTS)
                sp.dma_start(mod, row[:, :]).then_inc(stored, 16)
                sp.wait_ge(stored, 16)

            @block.scalar
            def _(act_):
                act_.wait_ge(small_loaded, 64)
                act_.activation(act[:, :, :].rearrange("p k v -> p v k"), cond[:, :, :], ACT.Silu).then_inc(silu_done, 1)
                for m in range(D_C // P):
                    act_.wait_ge(kc_turned, m + 1)
                    act_.copy(kct[HI][:, m, :].bitcast(F32R), kps[:, m, :]).then_inc(kc_hi, 1)

            @block.gpsimd
            def _(pool):
                pool.memset(bias_row[:, :], 0.0).then_inc(bias_zeroed, 1)
                pool.wait_ge(vc_loaded, 16)
                for n in range(3):
                    if n:
                        pool.wait_ge(vc_step, 2 * n)
                    pool.tensor_copy(vparts[:, :, :, n, :], vc[:, :, :, :]).then_inc(vc_step, 1)
                    if n < 2:
                        pool.wait_ge(vc_step, 2 * n + 1)
                        pool.tensor_tensor(vc[:, :, :, :], vc[:, :, :, :], vparts[:, :, :, n, :], ALU.subtract).then_inc(vc_step, 1)

            @block.tensor
            def _(pe):
                pe.wait_ge(kc_loaded, 32)
                for m in range(D_C // P):
                    for t in range(CT):
                        mm = pe.transpose(kps[:, m, t * P:(t + 1) * P], kc[:, t, m * P:(m + 1) * P], ident[:, :])
                    mm.then_inc(kc_turned, 1)
                pe.sem_inc(acc_done, SLOTS)
                pe.wait_ge(silu_done, 1)
                with pe.Fori(0, N // SLOTS) as i:
                    for s in range(SLOTS):
                        pe.wait_ge(w_loaded[s], i * 16 + 16)
                        pe.wait_ge(acc_read, i * SLOTS + s + 1)
                        for k in range(KT):
                            mm = pe.matmul(acc[0:2, s], act[:, k, :], w[:, s, k], start=k == 0, stop=k == KT - 1)
                        mm.then_inc(acc_done, 1)

            @block.vector
            def _(dve):
                dve.sem_inc(acc_read, SLOTS)
                for m in range(D_C // P):
                    dve.wait_ge(kc_hi, m + 1)
                    dve.tensor_tensor(kct[LO][:, m, :].bitcast(F32R), kps[:, m, :], kct[HI][:, m, :], ALU.subtract).then_inc(kc_lo, 1)
                dve.wait_ge(small_loaded, 64)
                with dve.Fori(0, N // SLOTS) as i:
                    for s in range(SLOTS):
                        dve.wait_ge(acc_done, i * SLOTS + s + 1 + SLOTS)
                        at = bass.ts(i * SLOTS + s, COLS)
                        dve.tensor_tensor(row[:, at], acc[0:2, s], bias[:, at], ALU.add).then_inc(acc_read, 1)


def projection_phase(nc, x_all, w_in, a_ws, a_bs, f_w, ident_in, dft_c64, dft_s64,
                     mod, y, q_t, k_t, v_parts, chan_dft, new_k, new_v):
    G_TOK = 256
    NT = G_TOK // P
    GROUPS = T_ALL // G_TOK
    UNITS, PSLOTS, STAGES = 9, 3, 6
    SUB = KT // 2
    WCH, WSLOTS = 6, 3
    WC = P_IN // WCH
    with ExitStack() as ctx:
        sb, ps, sem = phase_tools(nc, ctx)
        w = [sb(f"pj_w{h}", [P, KT, P_IN], F32R) for h in (HI, LO)]
        ht = [sb(f"pj_ht{h}", [P, 2, KT, G_TOK], F32R) for h in (HI, LO)]
        x = sb("pj_x", [P, NT, D])
        hm = sb("pj_hm", [P, 2, G_TOK])
        st = sb("pj_out_stage", [P, 2, 512])
        st_lo = sb("pj_lo_stage", [P, 512])
        st_v = sb("pj_v_stage", [P, HEADS, 3, HD], BF16)
        zbt = sb("pj_zbt", [P, 2, G_TOK])
        zg = sb("pj_gelu", [P, 512])
        vn = sb("pj_vn", [P, D_A])
        ya = sb("pj_ya", [P, D_A])
        wst = sb("pj_wst", [P, A_HEADS, P])
        bd = sb("pj_bd", [P, 2, 2, P])
        ident = sb("pj_ident", [P, P])
        shift = sb("pj_shift", [P, 2, KT])
        scale = sb("pj_scale", [P, 2, KT])
        scale1p = sb("pj_scale1p", [P, 2, KT])
        bs = sb("pj_bs", [P, A_HEADS])
        stats = sb("pj_stats", [P, NT, 2, 6])
        mv = sb("pj_mv", [P, NT, 2])
        veps = sb("pj_veps", [P, NT])
        rstd = sb("pj_rstd", [P, NT])
        vstats = sb("pj_vstats", [P, 6])
        vmv = sb("pj_vmv", [P, 2])
        vveps = sb("pj_vveps", [P, 1])
        vrstd = sb("pj_vrstd", [P, 1])
        minus_half = sb("pj_minus_half", [P, 2])
        eps = sb("pj_eps", [P, 2])
        waited = sb("pj_waited", [P, 1])
        tps = ps("pj_tps", [P, 2, 2, G_TOK])
        gps = ps("pj_gps", [P, PSLOTS, 512])
        mixps = ps("pj_mixps", [P, 512])
        abps = ps("pj_abps", [P, 2, 512])

        consts_loaded, fw_zeroed, fw_loaded = sem("pj_consts_loaded"), sem("pj_fw_zeroed"), sem("pj_fw_loaded")
        setup_mm, setup_done, scale_done, half_done = (sem("pj_setup_mm"), sem("pj_setup_done"),
                                                       sem("pj_scale_done"), sem("pj_half_done"))
        w_staged = [sem(f"pj_w_staged{s}") for s in range(WSLOTS)]
        w_hi, w_lo = sem("pj_w_hi"), sem("pj_w_lo")
        x_loaded = sem("pj_x_loaded")
        stats_done, mv_done, veps_done, rstd_done, xn_done = (
            sem("pj_stats_done"), sem("pj_mv_done"), sem("pj_veps_done"), sem("pj_rstd_done"), sem("pj_xn_done"))
        tps_done, hm_done, h_hi, h_lo = sem("pj_tps_done"), sem("pj_hm_done"), sem("pj_h_hi"), sem("pj_h_lo")
        unit_done = sem("pj_unit_done")
        slot_read = [sem(f"pj_slot_read{s}") for s in range(PSLOTS)]
        qk_hi, v_hi, v_mid, v_done, raw_done = sem("pj_qk_hi"), sem("pj_v_hi"), sem("pj_v_mid"), sem("pj_v_done"), sem("pj_raw_done")
        lo_stored, v_stored, raw_stored = sem("pj_lo_stored"), sem("pj_v_stored"), sem("pj_raw_stored")
        vstats_done, vmv_done, vveps_done, vrstd_done, vn_done = (
            sem("pj_vstats_done"), sem("pj_vmv_done"), sem("pj_vveps_done"),
            sem("pj_vrstd_done"), sem("pj_vn_done"))
        mix_done, ya_done, ya_stored = sem("pj_mix_done"), sem("pj_ya_done"), sem("pj_ya_stored")
        zbt_done, ab_done = sem("pj_zbt_done"), sem("pj_ab_done")
        ab_read = sem("pj_ab_read")
        st_stored = [sem(f"pj_st_stored{s}") for s in range(2)]
        N_CONSTS = 8

        w_tiles = w_in.rearrange("l (k p) n -> (l k) p n", p=P)
        stage_w = x[:, :, :].rearrange("p t d -> p (t d)")[:, 0:WSLOTS * WC].rearrange("p (s c) -> p s c", s=WSLOTS)
        x_groups = x_all.rearrange("(g t p) d -> g p t d", p=P, t=NT)
        tok = lambda g, t: bass.ds(g * G_TOK + t * P, P)
        grp = lambda g: bass.ds(g * G_TOK, G_TOK)
        qt_tiles = q_t.rearrange("x (m p) t -> x p m t", p=P)
        kt_tiles = k_t.rearrange("x (m p) t -> x p m t", p=P)
        fw2 = zg
        ws = hm
        v_rest = zg

        def every_group(eng, body):
            with eng.Fori(0, (GROUPS - 3) // 2) as i:
                for s in range(2):
                    body(i * 2 + s, s, True, LAT, False)
            body(GROUPS - 3, 0, True, LAT, False)
            body(GROUPS - 2, 1, False, CTX, False)
            body(GROUPS - 1, 0, False, None, True)

        with nc.Block() as block:
            @block.sync
            def _(sp):
                for s in range(2):
                    sp.sem_inc(st_stored[s], 16)
                sp.sem_inc(ya_stored, 16)
                sp.sem_inc(lo_stored, 16)
                sp.sem_inc(v_stored, 16)
                with nc.allow_non_contiguous_dma(reason="modulation and biases, channel on partition"):
                    for v in range(2):
                        for dst, what in ((shift, SHIFT1), (scale, SCALE1)):
                            sp.dma_start(dst[:, v, :], mod[v, what * D:(what + 1) * D].rearrange("(k p) -> p k", p=P)).then_inc(consts_loaded, 16)
                    sp.dma_start(bs[:, :], a_bs.rearrange("l h p -> p (l h)")).then_inc(consts_loaded, 16)
                sp.dma_start(ident[:, :], ident_in).then_inc(consts_loaded, 16)
                sp.dma_start(zbt[:, 0, 0:P], dft_c64).then_inc(consts_loaded, 16)
                sp.dma_start(zbt[:, 1, 0:P], dft_s64).then_inc(consts_loaded, 16)
                sp.dma_start(ws[:, :, :].rearrange("p a (b q) -> p (a b) q", q=P), a_ws.rearrange("l h p q -> p (l h) q")).then_inc(fw_loaded, 16)
                sp.wait_ge(fw_zeroed, 1)
                for g in range(4):
                    pair, half = g // 2, g % 2
                    sp.dma_start(fw2[half * 64:half * 64 + 64, pair * P + half * 64:pair * P + half * 64 + 64],
                                 f_w[0, g]).then_inc(fw_loaded, 16)
                with sp.Fori(0, KT) as k:
                    for n in range(WCH):
                        sp.wait_ge(w_lo, k * WCH + n + 1)
                        sp.dma_start(stage_w[:, n % WSLOTS, :], w_tiles[k][:, n * WC:(n + 1) * WC]).then_inc(w_staged[n % WSLOTS], 16)
                sp.wait_ge(w_lo, KT * WCH + WSLOTS)
                sp.dma_start(x[:, :, :], x_groups[0]).then_inc(x_loaded, 16)
                sp.wait_ge(tps_done, SUB)
                sp.dma_start(x[:, :, :], x_groups[1]).then_inc(x_loaded, 16)

                def group(g, s, next2, next1, is_ctx):
                    if next2:
                        sp.wait_ge(tps_done, (g + 2) * SUB)
                        sp.dma_start(x[:, :, :], x_groups[g + 2]).then_inc(x_loaded, 16)
                    staged = [0]

                    def stage():
                        staged[0] += 1
                        return (staged[0] - 1) % 2

                    def store_qk(dst, m, unit, n):
                        slot = stage()
                        sp.wait_ge(slot_read[unit % PSLOTS], g * (UNITS // PSLOTS) + unit // PSLOTS + 2)
                        view = lambda ap: ap.rearrange("p (m t) -> p m t", m=2)
                        sp.dma_start(dst[HI][:, m:m + 2, grp(g)], view(st[:, slot, :])).then_inc(st_stored[slot], 16)
                        sp.dma_start(dst[LO][:, m:m + 2, grp(g)], view(st_lo[:, :])).then_inc(lo_stored, 16)

                    def store_ab(t):
                        slot = stage()
                        sp.wait_ge(ab_read, g * NT + t + 1 + NT)
                        sp.dma_start(chan_dft[tok(g, t), :], st[:, slot, :]).then_inc(st_stored[slot], 16)

                    def store_ya(t):
                        sp.wait_ge(ya_done, g * NT + t + 2)
                        sp.dma_start(y[tok(g, t), 0:D_A], ya[:, :]).then_inc(ya_stored, 16)

                    store_qk(qt_tiles, 0, 1, 0)
                    store_ya(0)
                    store_qk(qt_tiles, 2, 4, 1)
                    store_ya(1)
                    store_qk(kt_tiles, 0, 5, 2)
                    store_ab(0)
                    store_qk(kt_tiles, 2, 6, 3)
                    store_ab(1)
                    for t in range(NT):
                        sp.wait_ge(v_done, g * NT + t + 1)
                        sp.dma_start(v_parts[tok(g, t), :], st_v[:, :, :, :].rearrange("p h n d -> p (h n d)")).then_inc(v_stored, 16)
                    if is_ctx:
                        for n, (out, t) in enumerate(((new_v, 0), (new_v, 1), (new_k, 0), (new_k, 1))):
                            sp.wait_ge(raw_done, n + 1)
                            sp.dma_start(out[t * P:(t + 1) * P, :], x[:, t, (n // 2) * 512:(n // 2 + 1) * 512]).then_inc(raw_stored, 16)

                every_group(sp, group)
                for s in range(2):
                    sp.wait_ge(st_stored[s], 16 * (GROUPS * STAGES // 2 + 1))
                sp.wait_ge(lo_stored, 16 * (GROUPS * 4 + 1))
                sp.wait_ge(v_stored, 16 * (GROUPS * NT + 1))
                sp.wait_ge(raw_stored, 16 * 4)
                sp.wait_ge(ya_stored, 16 * (GROUPS * NT + 1))

            @block.gpsimd
            def _(pool):
                pool.memset(fw2[:, :], 0.0).then_inc(fw_zeroed, 1)
                pool.memset(minus_half[:, :], -0.5).then_inc(half_done, 1)
                pool.memset(eps[:, :], EPS).then_inc(half_done, 1)
                pool.wait_ge(half_done, 2)

                def row_rstd(n):
                    pool.wait_ge(mv_done, n * NT + NT)
                    pool.tensor_tensor(veps[:, :], mv[:, :, 1], eps[:, :], ALU.add).then_inc(veps_done, 1)
                    pool.wait_ge(veps_done, n + 1)
                    pool.tensor_tensor(rstd[:, :], veps[:, :], minus_half[:, :], ALU.pow).then_inc(rstd_done, 1)

                def gate_rstd(n):
                    pool.wait_ge(vmv_done, n + 1)
                    pool.tensor_tensor(vveps[:, :], vmv[:, 1:2], eps[:, 0:1], ALU.add).then_inc(vveps_done, 1)
                    pool.wait_ge(vveps_done, n + 1)
                    pool.tensor_tensor(vrstd[:, :], vveps[:, :], minus_half[:, 0:1], ALU.pow).then_inc(vrstd_done, 1)

                row_rstd(0)
                row_rstd(1)

                def group(g, s, next2, next1, is_ctx):
                    gate_rstd(g * NT)
                    if next2:
                        row_rstd(g + 2)
                    gate_rstd(g * NT + 1)

                every_group(pool, group)

            @block.scalar
            def _(act):
                for s in range(PSLOTS):
                    act.sem_inc(slot_read[s], 1)
                act.sem_inc(ab_read, NT)
                with act.Fori(0, KT) as k:
                    for n in range(WCH):
                        act.wait_ge(w_staged[n % WSLOTS], (k * (WCH // WSLOTS) + n // WSLOTS) * 16 + 16)
                        act.copy(w[HI][:, k, n * WC:(n + 1) * WC], stage_w[:, n % WSLOTS, :]).then_inc(w_hi, 1)

                def round_h(n, s, j, used=None):
                    if used is not None:
                        act.wait_ge(unit_done, used * UNITS)
                    act.wait_ge(hm_done, n * SUB * 2 + 2 * j + 2)
                    act.copy(ht[HI][:, s, 2 * j:2 * j + 2, :], hm[:, :, :]).then_inc(h_hi, 1)

                for j in range(SUB):
                    round_h(0, 0, j)

                def group(g, s, next2, next1, is_ctx):
                    if next1 is not None:
                        for j in range(SUB):
                            round_h(g + 1, 1 - s, j, used=g)
                    unit, staged = [0], [0]

                    def product():
                        unit[0] += 1
                        act.wait_ge(unit_done, g * UNITS + unit[0])
                        return (unit[0] - 1) % PSLOTS

                    def stage():
                        slot, use = staged[0] % 2, staged[0] // 2
                        staged[0] += 1
                        act.wait_ge(st_stored[slot], (g * (STAGES // 2) + use + 1) * 16)
                        return st[:, slot, :]

                    def gelu(t):
                        n = product()
                        act.wait_ge(ya_done, g * NT + t + 1)
                        if t == 0:
                            act.wait_ge(v_done, g * NT)
                        act.activation(zg[:, :], gps[:, n, :], ACT.Gelu_apprx_tanh).then_inc(slot_read[n], 1)

                    def round_qk(times=1.0):
                        n = product()
                        act.activation(stage().bitcast(F32R), gps[:, n, :], ACT.Copy, scale=times).then_inc(qk_hi, 1)

                    def ab_to_stage(t):
                        act.wait_ge(ab_done, g * NT + t + 1 + NT)
                        act.copy(stage(), abps[:, t, :]).then_inc(ab_read, 1)

                    gelu(0)
                    round_qk(HD ** -0.5)
                    n = product()
                    act.wait_ge(ab_done, g * NT + NT)
                    act.copy(zbt[:, :, :].rearrange("p m t -> p (m t)"), gps[:, n, :]).then_inc(slot_read[n], 1)
                    gelu(1)
                    round_qk(HD ** -0.5)
                    round_qk()
                    ab_to_stage(0)
                    round_qk()
                    ab_to_stage(1)
                    for t in range(NT):
                        n = product()
                        act.wait_ge(v_stored, (g * NT + t + 1) * 16)
                        if is_ctx:
                            act.copy(x[:, t, 0:512], gps[:, n, :]).then_inc(raw_done, 1)
                        act.copy(st_v[:, :, 0, :], gps[:, n, :].rearrange("p (h d) -> p h d", h=HEADS)).then_inc(v_hi, 1)
                    if is_ctx:
                        for t in range(NT):
                            n = product()
                            act.copy(x[:, t, 512:1024], gps[:, n, :]).then_inc(raw_done, 1)

                act.wait_ge(setup_mm, 2)
                every_group(act, group)

            @block.tensor
            def _(pe):
                pe.sem_inc(ab_done, NT)
                pe.wait_ge(consts_loaded, 16 * N_CONSTS)
                pe.wait_ge(fw_loaded, 16 * 5)
                for h in range(A_HEADS):
                    mm = pe.transpose(gps[:, 0, h * P:(h + 1) * P], ws[:, h // 2, (h % 2) * P:(h % 2 + 1) * P], ident[:, :])
                mm.then_inc(setup_mm, 1)
                for m in range(2):
                    for ri in range(2):
                        mm = pe.matmul(gps[:, 1, (2 * m + ri) * P:(2 * m + ri + 1) * P], zbt[:, ri, 0:P],
                                       fw2[:, m * P:(m + 1) * P], start=True, stop=True)
                mm.then_inc(setup_mm, 1)
                pe.wait_ge(setup_done, 2)

                def transposes(n, j):
                    if not (isinstance(n, int) and n == 0 and j < 2):
                        pe.wait_ge(hm_done, (n * SUB + j - 2) * 2 + 2)
                    for kk in range(2):
                        for t in range(NT):
                            k = 2 * j + kk
                            mm = pe.transpose(tps[:, j % 2, kk, t * P:(t + 1) * P], x[:, t, k * P:(k + 1) * P], ident[:, :])
                    mm.then_inc(tps_done, 1)

                def transpose_group(n):
                    pe.wait_ge(xn_done, n * NT + NT)
                    for j in range(SUB):
                        transposes(n, j)

                transpose_group(0)
                pe.wait_ge(w_lo, KT * WCH + WSLOTS)

                def group(g, s, next2, next1, is_ctx):
                    if next1 is not None:
                        transpose_group(g + 1)
                    unit = [0]

                    def product():
                        pe.wait_ge(slot_read[unit[0] % PSLOTS], g * (UNITS // PSLOTS) + unit[0] // PSLOTS + 1)
                        unit[0] += 1
                        return gps[:, (unit[0] - 1) % PSLOTS, :]

                    def rows(t, col):
                        out = product()
                        for k in range(KT):
                            for a, b in PASSES:
                                mm = pe.matmul(out, ht[a][:, s, k, t * P:(t + 1) * P], w[b][:, k, col:col + 512],
                                               start=(k, a, b) == (0, HI, HI), stop=(k, a, b) == (KT - 1, LO, HI))
                        mm.then_inc(unit_done, 1)

                    def channels(col):
                        out = product()
                        for m in range(2):
                            for k in range(KT):
                                for a, b in PASSES:
                                    mm = pe.matmul(out[:, m * G_TOK:(m + 1) * G_TOK],
                                                   w[a][:, k, col + m * P:col + (m + 1) * P], ht[b][:, s, k, :],
                                                   start=(k, a, b) == (0, HI, HI), stop=(k, a, b) == (KT - 1, LO, HI))
                        mm.then_inc(unit_done, 1)

                    def mix(t):
                        pe.wait_ge(vn_done, g * NT + t + 1)
                        pe.wait_ge(ya_done, g * NT + t + 1)
                        for h in range(A_HEADS):
                            mm = pe.matmul(mixps[:, h * HD:(h + 1) * HD], wst[:, h, :], vn[:, h * HD:(h + 1) * HD],
                                           start=True, stop=True)
                        mm.then_inc(mix_done, 1)

                    def channel_dft(t):
                        if t == 0:
                            pe.wait_ge(slot_read[2], g * (UNITS // PSLOTS) + 2)
                        pe.wait_ge(ab_read, g * NT + t + 1)
                        for m in range(2):
                            mm = pe.matmul(abps[:, t, m * 256:(m + 1) * 256], zbt[:, m, t * P:(t + 1) * P],
                                           bd[:, m, :, :].rearrange("p r c -> p (r c)"), start=True, stop=True)
                        mm.then_inc(ab_done, 1)

                    rows(0, COL_ZA)
                    channels(COL_Q)
                    mix(0)
                    channels(COL_ZB)
                    rows(1, COL_ZA)
                    channels(COL_Q + 256)
                    mix(1)
                    channels(COL_K)
                    channel_dft(0)
                    channels(COL_K + 256)
                    channel_dft(1)
                    for t in range(NT):
                        rows(t, COL_V)
                    if is_ctx:
                        for t in range(NT):
                            rows(t, COL_K)

                every_group(pe, group)

            @block.vector
            def _(dve):
                dve.sem_inc(w_lo, WSLOTS)
                dve.sem_inc(ya_done, 1)
                dve.wait_ge(consts_loaded, 16 * N_CONSTS)
                dve.tensor_scalar(scale1p[:, :, :], scale[:, :, :], 1.0, None, ALU.add).then_inc(scale_done, 1)
                dve.wait_ge(setup_mm, 2)
                dve.tensor_copy(wst[:, :, :].rearrange("p h q -> p (h q)"), gps[:, 0, :]).then_inc(setup_done, 1)
                dve.tensor_copy(bd[:, :, :, :].rearrange("p m r c -> p (m r c)"), gps[:, 1, :]).then_inc(setup_done, 1)
                with dve.Fori(0, KT) as k:
                    for n in range(WCH):
                        dve.wait_ge(w_hi, k * WCH + n + 1)
                        at = slice(n * WC, (n + 1) * WC)
                        dve.tensor_tensor(w[LO][:, k, at], stage_w[:, n % WSLOTS, :], w[HI][:, k, at].bitcast(F32),
                                          ALU.subtract).then_inc(w_lo, 1)

                def norm_x(n):
                    dve.wait_ge(x_loaded, n * 16 + 16)
                    for t in range(NT):
                        for half in range(2):
                            last = dve.bn_stats(stats[:, t, half, :], x[:, t, half * 512:(half + 1) * 512])
                    last.then_inc(stats_done, 1)
                    dve.wait_ge(stats_done, n + 1)
                    dve.tensor_copy(waited[:, :], stats[:, 0, 0, 0:1])
                    for t in range(NT):
                        dve.bn_aggr(mv[:, t, :], stats[:, t, :, :].rearrange("p a b -> p (a b)")).then_inc(mv_done, 1)
                    dve.wait_ge(rstd_done, n + 1)
                    for t in range(NT):
                        dve.tensor_scalar(x[:, t, :], x[:, t, :], mv[:, t, 0:1], rstd[:, t:t + 1],
                                          ALU.subtract, ALU.mult).then_inc(xn_done, 1)

                def modulate(n, s, vec, used=None):
                    if used is not None:
                        dve.wait_ge(unit_done, used * UNITS)
                    for j in range(SUB):
                        dve.wait_ge(tps_done, n * SUB + j + 1)
                        dve.wait_ge(h_lo, n * SUB + j)
                        for kk in range(2):
                            k = 2 * j + kk
                            dve.tensor_scalar(hm[:, kk, :], tps[:, j % 2, kk, :], scale1p[:, vec, k:k + 1],
                                              shift[:, vec, k:k + 1], ALU.mult, ALU.add).then_inc(hm_done, 1)
                        dve.wait_ge(h_hi, n * SUB + j + 1)
                        dve.tensor_tensor(ht[LO][:, s, 2 * j:2 * j + 2, :], hm[:, :, :],
                                          ht[HI][:, s, 2 * j:2 * j + 2, :].bitcast(F32), ALU.subtract).then_inc(h_lo, 1)

                norm_x(0)
                dve.wait_ge(scale_done, 1)
                modulate(0, 0, LAT)
                norm_x(1)

                def group(g, s, next2, next1, is_ctx):
                    if next1 is not None:
                        modulate(g + 1, 1 - s, next1, used=g)

                    def gate_norm(t):
                        n = g * NT + t
                        dve.wait_ge(slot_read[0], g * (UNITS // PSLOTS) + t + 2)
                        dve.bn_stats(vstats[:, :], zg[:, D_A:2 * D_A]).then_inc(vstats_done, 1)
                        dve.wait_ge(vstats_done, n + 1)
                        dve.tensor_copy(waited[:, :], vstats[:, 0:1])
                        dve.bn_aggr(vmv[:, :], vstats[:, :]).then_inc(vmv_done, 1)
                        dve.wait_ge(vrstd_done, n + 1)
                        dve.tensor_scalar(vn[:, :], zg[:, D_A:2 * D_A], vmv[:, 0:1], vrstd[:, :],
                                          ALU.subtract, ALU.mult).then_inc(vn_done, 1)

                    def gate(t):
                        n = g * NT + t
                        dve.wait_ge(mix_done, n + 1)
                        dve.wait_ge(ya_stored, n * 16 + 16)
                        for h in range(A_HEADS):
                            at = slice(h * HD, (h + 1) * HD)
                            last = dve.scalar_tensor_tensor(ya[:, at], mixps[:, at], bs[:, h:h + 1], zg[:, at], ALU.add, ALU.mult)
                        last.then_inc(ya_done, 1)

                    def low_qk(n, unit, times=1.0):
                        slot = unit % PSLOTS
                        dve.wait_ge(qk_hi, g * 4 + n + 1)
                        dve.wait_ge(lo_stored, (g * 4 + n + 1) * 16)
                        hi = st[:, (0, 1, 0, 0)[n], :]
                        dve.scalar_tensor_tensor(st_lo[:, :].bitcast(F32R), gps[:, slot, :], times, hi,
                                                 ALU.mult, ALU.subtract).then_inc(slot_read[slot], 1)

                    def v_tail(t, unit):
                        n = g * NT + t
                        slot = unit % PSLOTS
                        heads = lambda ap: ap.rearrange("p (h d) -> p h d", h=HEADS)
                        dve.wait_ge(v_hi, n + 1)
                        dve.tensor_tensor(heads(v_rest[:, :]), heads(gps[:, slot, :]), st_v[:, :, 0, :], ALU.subtract).then_inc(slot_read[slot], 1)
                        dve.wait_ge(slot_read[slot], g * (UNITS // PSLOTS) + unit // PSLOTS + 2)
                        dve.tensor_copy(st_v[:, :, 1, :], heads(v_rest[:, :])).then_inc(v_mid, 1)
                        dve.wait_ge(v_mid, n + 1)
                        dve.tensor_tensor(st_v[:, :, 2, :], heads(v_rest[:, :]), st_v[:, :, 1, :], ALU.subtract).then_inc(v_done, 1)

                    gate_norm(0)
                    low_qk(0, 1, HD ** -0.5)
                    gate(0)
                    if next2:
                        norm_x(g + 2)
                    gate_norm(1)
                    low_qk(1, 4, HD ** -0.5)
                    gate(1)
                    low_qk(2, 5)
                    low_qk(3, 6)
                    v_tail(0, 7)
                    v_tail(1, 8)

                every_group(dve, group)


def fourier_phase(nc, chan_dft, twiddle_in, dft512_in, dft256_in, y):
    R = 4
    with ExitStack() as ctx:
        sb, ps, sem = phase_tools(nc, ctx)
        tw = sb("fo_tw", [P, R, R, 2])
        table = [sb(f"fo_table{h}", [P, 2, R, 512], F32R) for h in (HI, LO)]
        table_in = sb("fo_table_in", [P, 2, R, 512])
        ctab = sb("fo_ctab", [P, 2, 2, 256])
        x = sb("fo_x", [P, 4 * R, 512])
        xc = sb("fo_xc", [P, 2, 512])
        sums = sb("fo_sums", [P, 2, 2, 512])
        yj = sb("fo_y", [P, R, 2, R, 256])
        prod = sb("fo_prod", [P, 2, 256])
        ys = [sb(f"fo_ys{h}", [P, R, 2, R, 256], F32R) for h in (HI, LO)]
        out = sb("fo_out", [P, 2, 2, 256])
        acc = ps("fo_acc", [P, 4, 512])
        tables_loaded, x_loaded = sem("fo_tables_loaded"), [sem(f"fo_x_loaded{i}") for i in range(R)]
        xc_loaded = sem("fo_xc_loaded")
        table_hi, table_lo = sem("fo_table_hi"), sem("fo_table_lo")
        sums_done, bfly_done, prod_done, tw_done = sem("fo_sums_done"), sem("fo_bfly_done"), sem("fo_prod_done"), sem("fo_tw_done")
        y_hi, y_lo = sem("fo_y_hi"), sem("fo_y_lo")
        acc_done, acc_read = sem("fo_acc_done"), sem("fo_acc_read")
        stored = [sem(f"fo_stored{s}") for s in range(2)]
        ctx_stored = sem("fo_ctx_stored")
        UNITS = 8

        y_lat = y[0:T_LAT, D_A:D_A + D_B].rearrange("(m p j) c -> m p j c", p=P, j=R)
        flat = lambda ap: ap.rearrange("p a b c d -> p (a b c d)")
        SPLITS = R

        with nc.Block() as block:
            @block.sync
            def _(sp):
                xs = chan_dft[0:T_LAT, :].rearrange("(q i p) c -> i p q c", p=P, i=R)
                sp.dma_start(tw[:, :, :, :], twiddle_in.rearrange("(i p) j r -> p i j r", p=P)).then_inc(tables_loaded, 16)
                for i in range(R):
                    sp.dma_start(x[:, i * R:(i + 1) * R, :], xs[i]).then_inc(x_loaded[i], 16)
                    if i == 0:
                        sp.dma_start(table_in[:, :, :, :], dft512_in.rearrange("r (i p) m -> p r i m", p=P)).then_inc(tables_loaded, 16)
                sp.dma_start(ctab[:, :, :, :], dft256_in.rearrange("r (i p) m -> p r i m", p=P)).then_inc(xc_loaded, 16)
                sp.dma_start(xc[:, :, :], chan_dft[T_LAT:T_ALL, :].rearrange("(i p) c -> p i c", p=P)).then_inc(xc_loaded, 16)
                for u in range(UNITS):
                    jp, m = u // R, u % R
                    sp.wait_ge(acc_read, 4 + u + 1)
                    sp.dma_start(y_lat[m, :, 2 * jp:2 * jp + 2, :], out[:, u % 2, :, :]).then_inc(stored[u % 2], 16)
                for t in range(2):
                    sp.wait_ge(acc_read, 4 + UNITS + t + 1)
                    sp.dma_start(y[T_LAT + t * P:T_LAT + (t + 1) * P, D_A:D_A + D_B], out[:, t, 0, :]).then_inc(ctx_stored, 16)
                for s in range(2):
                    sp.wait_ge(stored[s], UNITS // 2 * 16)
                sp.wait_ge(ctx_stored, 32)

            @block.scalar
            def _(act):
                act.sem_inc(acc_read, 4)
                act.wait_ge(tables_loaded, 32)
                act.copy(table[HI][:, :, :, :].rearrange("p r i m -> p (r i m)"), table_in[:, :, :, :].rearrange("p r i m -> p (r i m)")).then_inc(table_hi, 1)
                for i in range(R):
                    act.wait_ge(bfly_done, 8 * (i + 1))
                    act.wait_ge(tw_done, 3 * 4 * (i + 1))
                    act.copy(ys[HI][:, i].rearrange("p r j c -> p (r j c)"), yj[:, i].rearrange("p r j c -> p (r j c)")).then_inc(y_hi, 1)
                for u in range(UNITS + 2):
                    act.wait_ge(acc_done, u + 1)
                    if 2 <= u < UNITS + 2:
                        act.wait_ge(stored[u % 2], min(u // 2, UNITS // 2) * 16)
                    if u < UNITS:
                        act.copy(out[:, u % 2, :, :].rearrange("p j c -> p (j c)"), acc[:, u % 4, :]).then_inc(acc_read, 1)
                    else:
                        act.copy(out[:, u % 2, 0, :], acc[:, u % 4, 0:256]).then_inc(acc_read, 1)

            @block.vector
            def _(dve):
                for i in range(R):
                    xi = x[:, i * R:(i + 1) * R, :]
                    dve.wait_ge(x_loaded[i], 16)
                    for odd in range(2):
                        for diff in range(2):
                            dve.tensor_tensor(sums[:, odd, diff, :], xi[:, odd, :], xi[:, odd + 2, :],
                                              ALU.subtract if diff else ALU.add).then_inc(sums_done, 1)
                    dve.wait_ge(sums_done, 4 * (i + 1))
                    part = lambda odd, diff, ri: sums[:, odd, diff, :].rearrange("p (h r c) -> p r h c", h=2, r=2)[:, ri]
                    y_of = lambda ri, j: yj[:, i, ri, j, :].rearrange("p (h c) -> p h c", h=2)
                    for ri in range(2):
                        for j in (0, 2):
                            dve.tensor_tensor(y_of(ri, j), part(0, 0, ri), part(1, 0, ri),
                                              ALU.subtract if j else ALU.add).then_inc(bfly_done, 1)
                    for ri in range(2):
                        for j in (1, 3):
                            op = ALU.add if (ri == 0) == (j == 1) else ALU.subtract
                            dve.tensor_tensor(y_of(ri, j), part(0, 1, ri), part(1, 1, 1 - ri), op).then_inc(bfly_done, 1)
                    if i == 0:
                        dve.wait_ge(tables_loaded, 32)
                    dve.wait_ge(bfly_done, 8 * (i + 1))
                    for j in range(1, R):
                        n = (i * 3 + j - 1)
                        cos, sin = tw[:, i, j, 0:1], tw[:, i, j, 1:2]
                        if n:
                            dve.wait_ge(tw_done, 4 * n)
                        dve.tensor_scalar(prod[:, 0, :], yj[:, i, 1, j, :], sin, None, ALU.mult).then_inc(prod_done, 1)
                        dve.tensor_scalar(prod[:, 1, :], yj[:, i, 0, j, :], sin, None, ALU.mult).then_inc(prod_done, 1)
                        dve.wait_ge(prod_done, 2 * n + 2)
                        dve.scalar_tensor_tensor(yj[:, i, 0, j, :], yj[:, i, 0, j, :], cos, prod[:, 0, :],
                                                 ALU.mult, ALU.add).then_inc(tw_done, 2)
                        dve.scalar_tensor_tensor(yj[:, i, 1, j, :], yj[:, i, 1, j, :], cos, prod[:, 1, :],
                                                 ALU.mult, ALU.subtract).then_inc(tw_done, 2)
                    if i == 0:
                        dve.wait_ge(table_hi, 1)
                        dve.tensor_tensor(table[LO][:, :, :, :].rearrange("p r i m -> p (r i m)"), table_in[:, :, :, :].rearrange("p r i m -> p (r i m)"),
                                          table[HI][:, :, :, :].rearrange("p r i m -> p (r i m)").bitcast(F32), ALU.subtract).then_inc(table_lo, 1)
                    dve.wait_ge(y_hi, i + 1)
                    dve.tensor_tensor(ys[LO][:, i].rearrange("p r j c -> p (r j c)"), yj[:, i].rearrange("p r j c -> p (r j c)"),
                                      ys[HI][:, i].rearrange("p r j c -> p (r j c)").bitcast(F32), ALU.subtract).then_inc(y_lo, 1)

            @block.tensor
            def _(pe):
                pe.wait_ge(table_lo, 1)
                for jp in range(2):
                    for i in range(R):
                        if jp == 0:
                            pe.wait_ge(y_lo, i + 1)
                        for m in range(R):
                            if i == 0:
                                pe.wait_ge(acc_read, jp * R + m + 1)
                            for ri in range(2):
                                for a, b in PASSES:
                                    first, last = (i, ri, a, b) == (0, 0, HI, HI), (i, ri, a, b) == (R - 1, 1, LO, HI)
                                    mm = pe.matmul(acc[:, m, :], table[a][:, ri, i, m * P:(m + 1) * P],
                                                   ys[b][:, i, ri, 2 * jp:2 * jp + 2, :].rearrange("p j c -> p (j c)"),
                                                   start=first, stop=last)
                            if i == R - 1:
                                mm.then_inc(acc_done, 1)
                pe.wait_ge(xc_loaded, 32)
                for t in range(2):
                    pe.wait_ge(acc_read, UNITS + t + 1)
                    for h in range(2):
                        for n, (i, ri) in enumerate(((0, 0), (0, 1), (1, 0), (1, 1))):
                            mm = pe.matmul(acc[:, t, h * P:(h + 1) * P], ctab[:, ri, i, t * P:(t + 1) * P],
                                           xc[:, i, (2 * h + ri) * P:(2 * h + ri + 1) * P], start=n == 0, stop=n == 3)
                    mm.then_inc(acc_done, 1)


def attention_phase(nc, q_t, k_t, v_parts, rel_bias, col_mask_in, row_mask_in, ident_in, y):
    TILES, EDGES, INNER = 18, 4, 12
    EDGE_T = (0, 1, 14, 15)
    WIN, WIN_IN = 8 * GRID, 9 * GRID
    KCOLS = T_ALL + T_PAST
    VT = KCOLS // P
    VT_CTX, VT_PAST = T_LAT // P, T_ALL // P
    E_ROWS = 14
    with ExitStack() as ctx:
        sb, ps, sem = phase_tools(nc, ctx)
        ident = sb("at_ident", [P, P])
        col_mask = sb("at_col_mask", [P, GRID])
        row_mask = sb("at_row_mask", [P, WIN_IN])
        qs = sb("at_q", [P, 2, T_ALL], F32R)
        bin_ = sb("at_bias_in", [P, E_ROWS, GRID])
        k = [sb(f"at_k{h}", [P, 2, KCOLS], F32R) for h in (HI, LO)]
        vp = sb("at_v_parts", [P, 2, VT, 3, HD], BF16)
        ebias = sb("at_edge_bias", [P, 2, E_ROWS, GRID])
        ibias = sb("at_inner_bias", [P, 2, WIN_IN])
        sl = sb("at_local_scores", [P, 2, WIN_IN])
        prob = sb("at_prob", [P, 2, WIN_IN + T_PAST])
        ph = sb("at_prob_hi", [P, 2, 9, P], FP16)
        pl = sb("at_prob_lo", [P, 2, 9, P], FP16)
        ncmax = sb("at_neg_context_max", [P, 2])
        lmax = sb("at_local_max", [P, 2])
        nmx = sb("at_neg_max", [P, 2])
        sums = sb("at_sums", [P, 2, 2])
        den = sb("at_den", [P, 2])
        rden = sb("at_rden", [P, 2])
        osum = sb("at_osum", [P, HD])
        out = sb("at_out", [P, 2, TILES, HD])
        loc_ps = ps("at_loc_ps", [P, 2, 512])
        ctx_ps = ps("at_ctx_ps", [P, 2, 512])
        ta_ps = ps("at_ta_ps", [P, 4, P])
        tb_ps = ps("at_tb_ps", [P, 4, P])
        th_ps = ps("at_th_ps", [P, 512])
        o_ps = ps("at_o_ps", [P, 2, 256])

        consts_loaded = sem("at_consts_loaded")
        qk_loaded = [sem(f"at_qk_loaded{s}") for s in range(2)]
        v_loaded = [sem(f"at_v_loaded{s}") for s in range(2)]
        bias_loaded, ebias_done, bias_ready = sem("at_bias_loaded"), sem("at_ebias_done"), sem("at_bias_ready")
        qk_done = sem("at_qk_done")
        cmax_done, smax_done, nmax_done, exp_done = sem("at_cmax_done"), sem("at_smax_done"), sem("at_nmax_done"), sem("at_exp_done")
        exp_local_done, lo_a = sem("at_exp_local_done"), sem("at_lo_a")
        ta_done, tb_done, hi_a, hi_b, lo_done = sem("at_ta_done"), sem("at_tb_done"), sem("at_hi_a"), sem("at_hi_b"), sem("at_lo_done")
        pv_done, den_done, rden_done, o_read, out_done = (
            sem("at_pv_done"), sem("at_den_done"), sem("at_rden_done"), sem("at_o_read"), sem("at_out_done"))
        stored = [sem(f"at_stored{s}") for s in range(2)]

        v_tiles = v_parts.rearrange("(n p) c -> p n c", p=P)
        y_tiles = y.rearrange("(n p) c -> p n c", p=P)
        DMAS_QK = 6

        def kind(pos):
            if EDGES <= pos < EDGES + INNER:
                return (pos - EDGES) * P, WIN_IN, (pos - EDGES + 2) * P
            if pos < EDGES:
                return (0 if pos < 2 else T_LAT - WIN), WIN, EDGE_T[pos] * P
            return None, 0, T_LAT + (pos - EDGES - INNER) * P

        def every_tile(eng, body):
            def one_head(h, parity, first, last):
                for p in range(TILES):
                    before = (h, parity, p - 1) if p else (None if first else (h - 1, 1 - parity, TILES - 1))
                    after = (h, parity, p + 1) if p < TILES - 1 else (None if last else (h + 1, 1 - parity, 0))
                    body(before, (h, parity, p), after)

            one_head(0, 0, True, False)
            with eng.Fori(0, (HEADS - 2) // 2) as i:
                for s in range(2):
                    one_head(i * 2 + (1 + s), 1 - s, False, False)
            one_head(HEADS - 1, 1, False, True)

        with nc.Block() as block:
            @block.sync
            def _(sp):
                sp.sem_inc(stored[0], 16)
                sp.sem_inc(stored[1], 16)
                sp.dma_start(ident[:, :], ident_in).then_inc(consts_loaded, 16)
                sp.dma_start(col_mask[:, :], col_mask_in).then_inc(consts_loaded, 16)
                sp.dma_start(row_mask[:, :], row_mask_in).then_inc(consts_loaded, 16)

                def load_head(h, parity, bias_read=None):
                    rows = bass.ds(h * HD, HD)
                    for half in range(2):
                        for part in (HI, LO):
                            sp.dma_start(k[part][half * HD:(half + 1) * HD, parity, :].bitcast(F32), k_t[part, rows, :]).then_inc(qk_loaded[parity], 16)
                        sp.dma_start(qs[half * HD:(half + 1) * HD, parity, :].bitcast(F32), q_t[half, rows, :]).then_inc(qk_loaded[parity], 16)
                    sp.dma_start(vp[:, parity].rearrange("p t n d -> p t (n d)"),
                                 v_tiles[:, :, bass.ds(h * (3 * HD), 3 * HD)]).then_inc(v_loaded[parity], 16)
                    if bias_read is not None:
                        sp.wait_ge(bias_ready, bias_read)
                    for half in range(2):
                        src = rel_bias[:, bass.ds(h * REL_ROWS + (1 - half), E_ROWS), :]
                        sp.dma_start(bin_[half * HD:(half + 1) * HD, :, :], src).then_inc(bias_loaded, 16)

                load_head(0, 0)

                def one_head(h, parity, last):
                    if not last:
                        sp.wait_ge(pv_done, h * TILES + 2)
                        load_head(h + 1, 1 - parity, bias_read=h + 1)
                    sp.wait_ge(out_done, (h + 1) * TILES)
                    sp.dma_start(y_tiles[:, :, bass.ds(h * HD + (D_A + D_B), HD)], out[:, parity]).then_inc(stored[parity], 16)

                with sp.Fori(0, HEADS // 2 - 1) as i:
                    for s in range(2):
                        one_head(i * 2 + s, s, False)
                one_head(HEADS - 2, 0, False)
                one_head(HEADS - 1, 1, True)
                for s in range(2):
                    sp.wait_ge(stored[s], 16 * (HEADS // 2 + 1))

            @block.gpsimd
            def _(pool):
                pool.wait_ge(consts_loaded, 48)
                smax_per_head = EDGES + INNER

                def bias_of(h, parity, heads_before):
                    if heads_before is not None:
                        pool.wait_ge(smax_done, heads_before * smax_per_head)
                    pool.wait_ge(bias_loaded, (h + 1) * 32)
                    pool.tensor_tensor(ebias[:, parity], bin_[:, :, :],
                                       col_mask[:, :].unsqueeze(1).to_broadcast([P, E_ROWS, GRID]), ALU.add).then_inc(ebias_done, 1)
                    pool.wait_ge(ebias_done, h + 1)
                    pool.tensor_tensor(ibias[:, parity, :], ebias[:, parity, 2:11, :].rearrange("p e c -> p (e c)"),
                                       row_mask[:, :], ALU.add).then_inc(bias_ready, 1)

                bias_of(0, 0, None)
                bias_of(1, 1, None)
                with pool.Fori(1, HEADS // 2) as i:
                    for s in range(2):
                        bias_of(i * 2 + s, s, i * 2 + (s - 1))

            @block.tensor
            def _(pe):
                pe.sem_inc(qk_done, 2)
                pe.sem_inc(pv_done, 2)
                pe.wait_ge(consts_loaded, 48)

                def head_uses(h, parity):
                    return (h - parity) // 2 + 1 if isinstance(h, int) else ((h - parity) >> 1) + 1

                def qk(tile):
                    h, parity, pos = tile
                    s, inner = pos % 2, EDGES <= pos < EDGES + INNER
                    u = h * TILES + pos
                    if pos == 0:
                        pe.wait_ge(qk_loaded[parity], head_uses(h, parity) * (16 * DMAS_QK))
                    pe.wait_ge(nmax_done, u)
                    pe.wait_ge(exp_done, u + 1)
                    key0, n, token = kind(pos)
                    q = qs[:, parity, token:token + P]
                    for c in range(2 if n else 0):
                        w = n // 2
                        for b in (HI, LO):
                            pe.matmul(loc_ps[:, c, 0:w], q, k[b][:, parity, key0 + c * w:key0 + (c + 1) * w],
                                      start=b == HI, stop=b == LO)
                    col, w = (T_ALL, T_PAST) if n else (T_LAT, T_CTX)
                    for b in (HI, LO):
                        mm = pe.matmul(ctx_ps[:, s, 0:w], q, k[b][:, parity, col:col + w], start=b == HI, stop=b == LO)
                    mm.then_inc(qk_done, 1)

                def turn(tile):
                    h, parity, pos = tile
                    s, inner = pos % 2, EDGES <= pos < EDGES + INNER
                    u = h * TILES + pos
                    n = kind(pos)[1]
                    if n:
                        n_loc = h * (EDGES + INNER) + pos
                        pe.wait_ge(exp_local_done, n_loc + 1)
                        if not (isinstance(h, int) and h == 0 and pos == 0):
                            pe.wait_ge(lo_a, n_loc)
                        for b in range(4):
                            mm = pe.transpose(ta_ps[:, b, :], prob[:, s, b * P:(b + 1) * P], ident[:, :])
                        mm.then_inc(ta_done, 1)
                    pe.wait_ge(exp_done, u + 3)
                    pe.wait_ge(lo_done, u)
                    for b in range(4 if n else 2):
                        if inner and b == 1:
                            pe.transpose(th_ps[0:GRID, 0:P], prob[:, s, 4 * P:4 * P + GRID], ident[:, :])
                        mm = pe.transpose(tb_ps[:, b, :], prob[:, s, n + b * P:n + (b + 1) * P], ident[:, :])
                    mm.then_inc(tb_done, 1)

                def pv(tile):
                    h, parity, pos = tile
                    s, inner = pos % 2, EDGES <= pos < EDGES + INNER
                    u = h * TILES + pos
                    if pos == 0:
                        pe.wait_ge(v_loaded[parity], head_uses(h, parity) * 16)
                    pe.wait_ge(lo_done, u + 1)
                    pe.wait_ge(o_read, u + 2)
                    key0, n, _ = kind(pos)
                    vt = key0 // P if n else None
                    blocks = [(b, vt + b, P) for b in range(4)] if n else []
                    if inner:
                        blocks.append((8, vt + 4, GRID))
                    blocks += [(4 + b, (VT_PAST if n else VT_CTX) + b, P) for b in range(4 if n else 2)]
                    for i, (b, v, rows) in enumerate(blocks):
                        for part, width in ((ph, 3), (pl, 2)):
                            mm = pe.matmul(o_ps[:, s, 0:width * HD], part[0:rows, s, b, :],
                                           vp[0:rows, parity, v, 0:width, :].rearrange("p n d -> p (n d)"),
                                           start=i == 0 and width == 3, stop=i == len(blocks) - 1 and width == 2)
                    mm.then_inc(pv_done, 1)

                def step(before, tile, after):
                    if after is not None:
                        qk(after)
                    turn(tile)
                    if before is not None:
                        pv(before)

                qk((0, 0, 0))
                every_tile(pe, step)
                pv((HEADS - 1, 1, TILES - 1))

            @block.vector
            def _(dve):
                dve.sem_inc(o_read, 2)
                dve.wait_ge(consts_loaded, 48)

                def row_max(tile, between):
                    h, parity, pos = tile
                    s, inner = pos % 2, EDGES <= pos < EDGES + INNER
                    u = h * TILES + pos
                    key0, n, _ = kind(pos)
                    if pos == 0:
                        dve.wait_ge(bias_ready, h + 1)
                    dve.wait_ge(qk_done, u + 3)
                    w = T_PAST if n else T_CTX
                    if n:
                        if inner:
                            bias = ibias[:, parity, :]
                        else:
                            e0 = (0 if pos < 2 else GRID // 2 - 8) - 2 * EDGE_T[pos] + 7 - 1
                            bias = ebias[:, parity, e0:e0 + 8, :].rearrange("p e c -> p (e c)")
                    dve.tensor_reduce(ncmax[:, s:s + 1], ctx_ps[:, s, 0:w], AX_X, ALU.max, negate=True).then_inc(cmax_done if n else nmax_done, 1)
                    between()
                    if n:
                        dve.tensor_tensor_reduce(sl[:, s, 0:n].rearrange("p (a c) -> p a c", a=2), loc_ps[:, :, 0:n // 2],
                                                 bias.rearrange("p (a c) -> p a c", a=2), 1.0, 2 * MASKED,
                                                 ALU.add, ALU.max, lmax[:, s:s + 1]).then_inc(smax_done, 1)
                        dve.wait_ge(smax_done, h * (EDGES + INNER) + pos + 1)
                        dve.scalar_tensor_tensor(nmx[:, s:s + 1], lmax[:, s:s + 1], -1.0, ncmax[:, s:s + 1],
                                                 ALU.mult, ALU.min).then_inc(nmax_done, 1)

                def low_part(tile):
                    h, parity, pos = tile
                    s, inner = pos % 2, EDGES <= pos < EDGES + INNER
                    u = h * TILES + pos
                    n = kind(pos)[1]
                    if n:
                        dve.wait_ge(hi_a, h * (EDGES + INNER) + pos + 1)
                        dve.tensor_tensor(pl[:, s, 0:4, :], ta_ps[:, :, :], ph[:, s, 0:4, :], ALU.subtract).then_inc(lo_a, 1)
                    dve.wait_ge(hi_b, u + 1)
                    if inner:
                        dve.tensor_tensor(pl[0:GRID, s, 8, :], th_ps[0:GRID, 0:P], ph[0:GRID, s, 8, :], ALU.subtract)
                    b = 4 if n else 2
                    dve.tensor_tensor(pl[:, s, 4:4 + b, :], tb_ps[:, 0:b, :], ph[:, s, 4:4 + b, :], ALU.subtract).then_inc(lo_done, 1)

                def total(tile):
                    h, parity, pos = tile
                    s, inner = pos % 2, EDGES <= pos < EDGES + INNER
                    u = h * TILES + pos
                    dve.wait_ge(exp_done, u + 3)
                    if kind(pos)[1]:
                        dve.tensor_tensor(den[:, s:s + 1], sums[:, s, 0:1], sums[:, s, 1:2], ALU.add).then_inc(den_done, 1)
                    else:
                        dve.tensor_copy(den[:, s:s + 1], sums[:, s, 1:2]).then_inc(den_done, 1)

                def invert(tile):
                    h, parity, pos = tile
                    s, inner = pos % 2, EDGES <= pos < EDGES + INNER
                    dve.wait_ge(den_done, h * TILES + pos + 1)
                    dve.reciprocal(rden[:, s:s + 1], den[:, s:s + 1]).then_inc(rden_done, 1)

                def finish(tile):
                    h, parity, pos = tile
                    s, inner = pos % 2, EDGES <= pos < EDGES + INNER
                    u = h * TILES + pos
                    dve.wait_ge(pv_done, u + 3)
                    dve.tensor_reduce(osum[:, :], o_ps[:, s, 0:3 * HD].rearrange("p (n d) -> p d n", n=3), AX_X, ALU.add).then_inc(o_read, 1)
                    dve.wait_ge(rden_done, u + 1)
                    if pos == 0:
                        dve.wait_ge(stored[parity], (h - parity) * 8 + 16)
                    dve.wait_ge(o_read, u + 3)
                    dve.tensor_scalar(out[:, parity, kind(pos)[2] // P, :], osum[:, :], rden[:, s:s + 1], None, ALU.mult).then_inc(out_done, 1)

                def step(before, tile, after):
                    if before is not None:
                        total(before)
                    if after is not None:
                        row_max(after, (lambda: invert(before)) if before is not None else (lambda: None))
                    elif before is not None:
                        invert(before)
                    low_part(tile)
                    if before is not None:
                        finish(before)

                row_max((0, 0, 0), lambda: None)
                every_tile(dve, step)
                last = (HEADS - 1, 1, TILES - 1)
                total(last)
                invert(last)
                finish(last)

            @block.scalar
            def _(act):
                act.sem_inc(exp_done, 2)
                act.wait_ge(consts_loaded, 48)

                def exps(tile):
                    h, parity, pos = tile
                    s, inner = pos % 2, EDGES <= pos < EDGES + INNER
                    u = h * TILES + pos
                    n = kind(pos)[1]
                    act.wait_ge(nmax_done, u + 1)
                    nmax = (nmx if n else ncmax)[:, s:s + 1]
                    if n:
                        act.activation(prob[:, s, 0:n], sl[:, s, 0:n], ACT.Exp, bias=nmax,
                                       accum_out=sums[:, s, 0:1]).then_inc(exp_local_done, 1)
                    w = T_PAST if n else T_CTX
                    act.activation(prob[:, s, n:n + w], ctx_ps[:, s, 0:w], ACT.Exp, bias=nmax,
                                   accum_out=sums[:, s, 1:2]).then_inc(exp_done, 1)

                def high_part(tile):
                    h, parity, pos = tile
                    s, inner = pos % 2, EDGES <= pos < EDGES + INNER
                    u = h * TILES + pos
                    n = kind(pos)[1]
                    act.wait_ge(pv_done, u + 1)
                    if n:
                        act.wait_ge(ta_done, h * (EDGES + INNER) + pos + 1)
                        act.copy(ph[:, s, 0:4, :], ta_ps[:, :, :]).then_inc(hi_a, 1)
                    act.wait_ge(tb_done, u + 1)
                    if inner:
                        act.copy(ph[0:GRID, s, 8, :], th_ps[0:GRID, 0:P])
                    b = 4 if n else 2
                    act.copy(ph[:, s, 4:4 + b, :], tb_ps[:, 0:b, :]).then_inc(hi_b, 1)

                def step(before, tile, after):
                    exps(tile)
                    high_part(tile)

                every_tile(act, step)


def mix_phase(nc, y, x_all, w_out, ln1_g, ln1_b, mod, ident_in, x1, h2_t):
    N = T_ALL // P
    N_LAT = T_LAT // P
    HALVES = D // 512
    with ExitStack() as ctx:
        sb, ps, sem = phase_tools(nc, ctx)
        w = [sb(f"mx_w{h}", [P, KT, D], F32R) for h in (HI, LO)]
        stage = sb("mx_w_stage", [P, 2, D])
        yb = sb("mx_y", [P, 2, D])
        xb = sb("mx_x", [P, 2, D])
        yt = [sb(f"mx_yt{h}", [P, 2, KT, P], F32R) for h in (HI, LO)]
        res = sb("mx_res", [P, 2, D])
        x1b = sb("mx_x1", [P, 2, D])
        xn = sb("mx_xn", [P, 2, D])
        hst = sb("mx_h_stage", [P, 2, KT, P])
        gate = sb("mx_gate", [P, 2, D])
        ln_g = sb("mx_ln_g", [P, D])
        ln_b = sb("mx_ln_b", [P, D])
        shift = sb("mx_shift", [P, 2, KT])
        scale = sb("mx_scale", [P, 2, KT])
        scale1p = sb("mx_scale1p", [P, 2, KT])
        ident = sb("mx_ident", [P, P])
        stats = sb("mx_stats", [P, 2, 12])
        mv = sb("mx_mv", [P, 2, 2])
        veps = sb("mx_veps", [P, 2])
        rstd = sb("mx_rstd", [P, 2])
        waited = sb("mx_waited", [P, 2])
        minus_half = sb("mx_minus_half", [P, 1])
        eps = sb("mx_eps", [P, 1])
        acc = ps("mx_acc", [P, 2, D])
        yps = ps("mx_yps", [P, KT, P])
        hps = ps("mx_hps", [P, KT, P])

        consts_loaded, half_done, scale_done = sem("mx_consts_loaded"), sem("mx_half_done"), sem("mx_scale_done")
        w_staged = [sem(f"mx_w_staged{s}") for s in range(2)]
        w_hi, w_lo = sem("mx_w_hi"), sem("mx_w_lo")
        y_loaded = [sem(f"mx_y_loaded{s}") for s in range(2)]
        x_loaded = [sem(f"mx_x_loaded{s}") for s in range(2)]
        y_turned, y_hi, y_lo = sem("mx_y_turned"), sem("mx_y_hi"), sem("mx_y_lo")
        acc_done, gated, res_done = sem("mx_acc_done"), sem("mx_gated"), sem("mx_res_done")
        stats_done = [sem(f"mx_stats_done{n}") for n in range(2)]
        mv_done = [sem(f"mx_mv_done{n}") for n in range(2)]
        veps_done = [sem(f"mx_veps_done{n}") for n in range(2)]
        rstd_done = [sem(f"mx_rstd_done{n}") for n in range(2)]
        normed = [sem(f"mx_normed{n}") for n in range(2)]
        scaled, x1_done, h_turned, h_done = sem("mx_scaled"), sem("mx_x1_done"), sem("mx_h_turned"), sem("mx_h_done")
        x1_stored = [sem(f"mx_x1_stored{s}") for s in range(2)]
        h_stored = [sem(f"mx_h_stored{s}") for s in range(2)]
        N_CONSTS = 9

        w_tiles = w_out.rearrange("l (k p) n -> (l k) p n", p=P)
        tiles = lambda ap: ap.rearrange("(t p) d -> t p d", p=P)
        y_tiles, x_tiles, x1_tiles = tiles(y), tiles(x_all), tiles(x1)
        h_tiles = h2_t.rearrange("(k p) t -> p k t", p=P)
        use = lambda t, s: (t - s) * 8

        def every_tile(body):
            def loop(eng):
                body(0, 0, LAT)
                body(1, 1, LAT)
                with eng.Fori(0, (N_LAT - 2) // 2) as i:
                    for s in range(2):
                        body(i * 2 + (2 + s), s, LAT)
                for t in range(N_LAT, N):
                    body(t, t % 2, CTX)
            return loop

        last_tile = lambda t: isinstance(t, int) and t == N - 1
        first = lambda t, n: isinstance(t, int) and t < n

        with nc.Block() as block:
            @block.sync
            def _(sp):
                for s in range(2):
                    sp.sem_inc(x1_stored[s], 16)
                sp.dma_start(ident[:, :], ident_in).then_inc(consts_loaded, 16)
                for k in range(KT):
                    sp.wait_ge(w_lo, k + 1)
                    sp.dma_start(stage[:, k % 2, :], w_tiles[k]).then_inc(w_staged[k % 2], 16)
                    if k < 2:
                        sp.dma_start(yb[:, k, :], y_tiles[k]).then_inc(y_loaded[k], 16)
                with nc.allow_non_contiguous_dma(reason="modulation, channel on partition"):
                    for v in range(2):
                        for dst, what in ((shift, SHIFT2), (scale, SCALE2)):
                            sp.dma_start(dst[:, v, :], mod[v, what * D:(what + 1) * D].rearrange("(k p) -> p k", p=P)).then_inc(consts_loaded, 16)
                        sp.dma_start(gate[:, v, :], mod[v, GATE1 * D:(GATE1 + 1) * D].partition_broadcast(P)).then_inc(consts_loaded, 16)
                sp.dma_start(ln_g[:, :], ln1_g[0].partition_broadcast(P)).then_inc(consts_loaded, 16)
                sp.dma_start(ln_b[:, :], ln1_b[0].partition_broadcast(P)).then_inc(consts_loaded, 16)
                for t in range(2):
                    sp.dma_start(xb[:, t, :], x_tiles[t]).then_inc(x_loaded[t], 16)

                def store_x1(t, s):
                    sp.wait_ge(x1_done, t + 1)
                    sp.dma_start(x1_tiles[t], x1b[:, s, :]).then_inc(x1_stored[s], 16)

                def tile(t, s, vec):
                    if not isinstance(t, int) or t + 2 < N:
                        sp.wait_ge(y_turned, t + 1)
                        sp.dma_start(yb[:, s, :], y_tiles[t + 2]).then_inc(y_loaded[s], 16)
                    if not first(t, 1):
                        store_x1(t - 1, 1 - s)
                    if not isinstance(t, int) or t + 2 < N:
                        sp.wait_ge(res_done, t + 1)
                        sp.dma_start(xb[:, s, :], x_tiles[t + 2]).then_inc(x_loaded[s], 16)

                every_tile(tile)(sp)
                store_x1(N - 1, 1)
                for s in range(2):
                    sp.wait_ge(x1_stored[s], 16 * (N // 2 + 1))
                    sp.wait_ge(h_stored[s], 16 * (N // 2 + 1))

            @block.gpsimd
            def _(pool):
                pool.memset(minus_half[:, :], -0.5).then_inc(half_done, 1)
                pool.memset(eps[:, :], EPS).then_inc(half_done, 1)
                pool.wait_ge(half_done, 2)
                pool.wait_ge(consts_loaded, 16 * N_CONSTS)

                def make_rstd(t, n):
                    pool.wait_ge(mv_done[n], t + 1)
                    pool.tensor_tensor(veps[:, n:n + 1], mv[:, n, 1:2], eps[:, :], ALU.add).then_inc(veps_done[n], 1)
                    pool.wait_ge(veps_done[n], t + 1)
                    pool.tensor_tensor(rstd[:, n:n + 1], veps[:, n:n + 1], minus_half[:, :], ALU.pow).then_inc(rstd_done[n], 1)

                def affine(t, s):
                    pool.wait_ge(normed[0], t + 1)
                    pool.tensor_tensor(res[:, s, :], res[:, s, :], ln_g[:, :], ALU.mult).then_inc(scaled, 1)
                    pool.wait_ge(scaled, t + 1)
                    pool.wait_ge(x1_stored[s], use(t, s) + 16)
                    if not first(t, 2):
                        pool.wait_ge(normed[1], t - 1)
                    pool.tensor_tensor(x1b[:, s, :], res[:, s, :], ln_b[:, :], ALU.add).then_inc(x1_done, 1)

                def tile(t, s, vec):
                    make_rstd(t, 0)
                    if not first(t, 1):
                        make_rstd(t - 1, 1)
                    affine(t, s)

                every_tile(tile)(pool)
                make_rstd(N - 1, 1)

            @block.tensor
            def _(pe):
                pe.sem_inc(gated, 2)
                pe.wait_ge(consts_loaded, 16)

                def turn_y(t, s):
                    pe.wait_ge(y_loaded[s], use(t, s) + 16)
                    if not first(t, 1):
                        pe.wait_ge(y_lo, t)
                    for k in range(KT):
                        mm = pe.transpose(yps[:, k, :], yb[:, s, k * P:(k + 1) * P], ident[:, :])
                    mm.then_inc(y_turned, 1)

                def product(t, s):
                    pe.wait_ge(y_lo, t + 1)
                    pe.wait_ge(gated, t + 1)
                    for half in range(HALVES):
                        for k in range(KT):
                            if first(t, 1) and half == 0:
                                pe.wait_ge(w_lo, k + 3)
                            for a, b in PASSES:
                                mm = pe.matmul(acc[:, s, half * 512:(half + 1) * 512], yt[a][:, s, k, :],
                                               w[b][:, k, half * 512:(half + 1) * 512],
                                               start=(k, a, b) == (0, HI, HI), stop=(k, a, b) == (KT - 1, LO, HI))
                    mm.then_inc(acc_done, 1)

                def turn_h(t, s):
                    pe.wait_ge(normed[1], t + 1)
                    if not first(t, 1):
                        pe.wait_ge(h_done, t)
                    for k in range(KT):
                        mm = pe.transpose(hps[:, k, :], xn[:, s, k * P:(k + 1) * P], ident[:, :])
                    mm.then_inc(h_turned, 1)

                def tile(t, s, vec):
                    if not last_tile(t):
                        turn_y(t + 1, 1 - s)
                    product(t, s)
                    if not first(t, 2):
                        turn_h(t - 2, s)

                turn_y(0, 0)
                every_tile(tile)(pe)
                turn_h(N - 2, 0)
                turn_h(N - 1, 1)

            @block.scalar
            def _(act):
                for s in range(2):
                    act.sem_inc(h_stored[s], 16)
                for k in range(KT):
                    act.wait_ge(w_staged[k % 2], k // 2 * 16 + 16)
                    act.copy(w[HI][:, k, :], stage[:, k % 2, :]).then_inc(w_hi, 1)
                    if k == 1:
                        act.wait_ge(y_turned, 1)
                        act.copy(yt[HI][:, 0, :, :], yps[:, :, :]).then_inc(y_hi, 1)

                def round_y(t, s):
                    act.wait_ge(y_turned, t + 1)
                    if not first(t, 2):
                        act.wait_ge(acc_done, t - 1)
                    act.copy(yt[HI][:, s, :, :], yps[:, :, :]).then_inc(y_hi, 1)

                def modulate(t, s, vec):
                    act.wait_ge(h_turned, t + 1)
                    act.wait_ge(h_stored[s], use(t, s) + 16)
                    for k in range(KT):
                        last = act.activation(hst[:, s, k, :], hps[:, k, :], ACT.Identity,
                                              bias=shift[:, vec, k:k + 1], scale=scale1p[:, vec, k:k + 1])
                    last.then_inc(h_done, 1)
                    act.wait_ge(h_done, t + 1)
                    act.dma_start(h_tiles[:, :, bass.ds(t * P, P)], hst[:, s, :, :]).then_inc(h_stored[s], 16)

                def tile(t, s, vec):
                    if not last_tile(t):
                        round_y(t + 1, 1 - s)
                    if not first(t, 2):
                        modulate(t - 2, s, LAT)

                act.wait_ge(scale_done, 1)
                every_tile(tile)(act)
                modulate(N - 2, 0, CTX)
                modulate(N - 1, 1, CTX)

            @block.vector
            def _(dve):
                dve.sem_inc(w_lo, 2)

                def low_y(t, s):
                    dve.wait_ge(y_hi, t + 1)
                    dve.tensor_tensor(yt[LO][:, s, :, :], yps[:, :, :], yt[HI][:, s, :, :].bitcast(F32), ALU.subtract).then_inc(y_lo, 1)

                for k in range(KT):
                    dve.wait_ge(w_hi, k + 1)
                    dve.tensor_tensor(w[LO][:, k, :], stage[:, k % 2, :], w[HI][:, k, :].bitcast(F32), ALU.subtract).then_inc(w_lo, 1)
                    if k == 1:
                        low_y(0, 0)
                dve.wait_ge(consts_loaded, 16 * N_CONSTS)
                dve.tensor_scalar(scale1p[:, :, :], scale[:, :, :], 1.0, None, ALU.add).then_inc(scale_done, 1)

                def statistics(t, n, src):
                    for half in range(HALVES):
                        last = dve.bn_stats(stats[:, n, half * 6:half * 6 + 6], src[:, half * 512:(half + 1) * 512])
                    last.then_inc(stats_done[n], 1)
                    dve.wait_ge(stats_done[n], t + 1)
                    dve.tensor_copy(waited[:, n:n + 1], stats[:, n, 0:1])
                    dve.bn_aggr(mv[:, n, :], stats[:, n, :]).then_inc(mv_done[n], 1)

                def norm(t, n, dst, src):
                    dve.wait_ge(rstd_done[n], t + 1)
                    dve.tensor_scalar(dst, src, mv[:, n, 0:1], rstd[:, n:n + 1], ALU.subtract, ALU.mult).then_inc(normed[n], 1)

                def second_statistics(t, s):
                    dve.wait_ge(x1_done, t + 1)
                    statistics(t, 1, x1b[:, s, :])

                def second_norm(t, s):
                    if not first(t, 2):
                        dve.wait_ge(h_turned, t - 1)
                    norm(t, 1, xn[:, s, :], x1b[:, s, :])

                def tile(t, s, vec):
                    if not last_tile(t):
                        low_y(t + 1, 1 - s)
                    dve.wait_ge(acc_done, t + 1)
                    if not first(t, 2):
                        dve.wait_ge(x1_done, t - 1)
                    dve.tensor_tensor(res[:, s, :], acc[:, s, :], gate[:, vec, :], ALU.mult).then_inc(gated, 1)
                    dve.wait_ge(gated, t + 3)
                    dve.wait_ge(x_loaded[s], use(t, s) + 16)
                    dve.scalar_tensor_tensor(res[:, s, :], xb[:, s, :], ALPHA, res[:, s, :], ALU.mult, ALU.add).then_inc(res_done, 1)
                    dve.wait_ge(res_done, t + 1)
                    statistics(t, 0, res[:, s, :])
                    if not first(t, 1):
                        second_statistics(t - 1, 1 - s)
                    norm(t, 0, res[:, s, :], res[:, s, :])
                    if not first(t, 1):
                        second_norm(t - 1, 1 - s)

                every_tile(tile)(dve)
                second_statistics(N - 1, 1)
                second_norm(N - 1, 1)


def ffn_up_phase(nc, h2_t, w_gu, conv_w, conv_b, f_t):
    CHUNKS = [(c * 512, 512) for c in range(T_LAT // 512)] + [(T_LAT, T_CTX)]
    NC = len(CHUNKS)
    PIECE = 256
    H_PIECES = T_ALL // PIECE
    G_LEN = T_ALL + 4
    G_AT = [1 + at for at, _ in CHUNKS[:-1]] + [T_LAT + 3]
    ZEROS = (0, T_LAT + 1, T_LAT + 2, G_LEN - 1)
    BANK = (0, 1, 2, 3, 0)
    SLOT = (0, 1, 2, 0, 1)
    with ExitStack() as ctx:
        sb, ps, sem = phase_tools(nc, ctx)
        ht = [sb(f"fu_ht{h}", [P, KT, T_ALL], F32R) for h in (HI, LO)]
        w = [sb(f"fu_w{h}", [P, 2, KT, PIECE], F32R) for h in (HI, LO)]
        stage = sb("fu_stage", [P, 2, KT, PIECE])
        grow = sb("fu_g", [P, G_LEN])
        res = sb("fu_result", [P, 3, 512])
        cw = sb("fu_conv_w", [P, 3, FT])
        cb = sb("fu_conv_b", [P, FT])
        gps = ps("fu_gps", [P, 4, 512])
        ups = ps("fu_ups", [P, 4, 512])

        consts_loaded, zeroed = sem("fu_consts_loaded"), sem("fu_zeroed")
        staged = [sem(f"fu_staged{s}") for s in range(2)]
        part_hi, part_lo = sem("fu_part_hi"), sem("fu_part_lo")
        g_done, u_done, g_read, u_read = sem("fu_g_done"), sem("fu_u_done"), sem("fu_g_read"), sem("fu_u_read")
        tap = [sem(f"fu_tap{n}") for n in range(3)]
        silu_done = sem("fu_silu_done")
        stored = [sem(f"fu_stored{s}") for s in range(3)]
        USES = [SLOT.count(s) for s in range(3)]

        def uses(f, c):
            return f * USES[SLOT[c]] + SLOT[:c].count(SLOT[c])

        w_cols = w_gu.rearrange("l (k p) (h f c) -> (l h f) p k c", p=P, h=2, c=P)
        h_tiles = h2_t.rearrange("(k p) t -> p k t", p=P)
        piece_of = lambda f: H_PIECES + f
        h_pieces = lambda c: 1 + (CHUNKS[c][0] + CHUNKS[c][1]) // PIECE

        def every_tile(eng, body):
            body(0, 0)
            with eng.Fori(0, (FT - 2) // 2) as i:
                for s in range(2):
                    body(i * 2 + (1 + s), 1 - s)
            body(FT - 1, 1)

        def chunk_order(do_g, do_u):
            do_g(0)
            for c in range(NC):
                if c + 1 < NC:
                    do_g(c + 1)
                do_u(c)

        is_first = lambda f: isinstance(f, int) and f == 0
        is_last = lambda f: isinstance(f, int) and f == FT - 1

        with nc.Block() as block:
            @block.sync
            def _(sp):
                for s in range(3):
                    sp.sem_inc(stored[s], 16)

                def load_w(f, slot):
                    for h in range(2):
                        sp.dma_start(stage[:, slot, :, h * P:(h + 1) * P], w_cols[h * FT + f]).then_inc(staged[slot], 16)

                load_w(0, 0)
                for n in range(H_PIECES):
                    slot = (n + 1) % 2
                    if n:
                        sp.wait_ge(part_lo, n)
                    for h in range(2):
                        ks = slice(h * KT // 2, (h + 1) * KT // 2)
                        sp.dma_start(stage[:, slot, ks, :], h_tiles[:, ks, n * PIECE:(n + 1) * PIECE]).then_inc(staged[slot], 16)
                    if n == 1:
                        with nc.allow_non_contiguous_dma(reason="convolution weights, channel on partition"):
                            for tp in range(3):
                                sp.dma_start(cw[:, tp, :], conv_w[0, tp].rearrange("(f p) -> p f", p=P)).then_inc(consts_loaded, 16)
                            sp.dma_start(cb[:, :], conv_b[0].rearrange("(f p) -> p f", p=P)).then_inc(consts_loaded, 16)
                sp.wait_ge(part_lo, H_PIECES)
                load_w(1, (H_PIECES + 1) % 2)

                def tile(f, s):
                    for c, (at, n) in enumerate(CHUNKS):
                        sp.wait_ge(u_read, f * NC + c + 1)
                        sp.dma_start(f_t[bass.ds(f * P, P), at:at + n], res[:, SLOT[c], 0:n]).then_inc(stored[SLOT[c]], 16)
                        if c == 1 and not (isinstance(f, int) and f >= FT - 2):
                            sp.wait_ge(part_lo, f + (H_PIECES + 1))
                            load_w(f + 2, (H_PIECES + s) % 2)

                tile(0, 0)
                with sp.Fori(0, (FT - 4) // 2) as i:
                    for s in range(2):
                        tile(i * 2 + (1 + s), 1 - s)
                tile(FT - 3, 1)
                tile(FT - 2, 0)
                tile(FT - 1, 1)
                for s in range(3):
                    sp.wait_ge(stored[s], 16 * (FT * USES[s] + 1))

            @block.gpsimd
            def _(pool):
                for at in ZEROS:
                    pool.memset(grow[:, at:at + 1], 0.0).then_inc(zeroed, 1)

            @block.tensor
            def _(pe):
                def tile(f, s):
                    pe.wait_ge(part_lo, 1 if is_first(f) else f + (H_PIECES + 1))

                    def product(out, half, c):
                        at, n = CHUNKS[c]
                        for k in range(KT):
                            for a, b in PASSES:
                                mm = pe.matmul(out[:, BANK[c], 0:n], w[a][:, s, k, half * P:(half + 1) * P],
                                               ht[b][:, k, at:at + n],
                                               start=(k, a, b) == (0, HI, HI), stop=(k, a, b) == (KT - 1, LO, HI))
                        return mm

                    def g(c):
                        if is_first(f):
                            pe.wait_ge(part_lo, h_pieces(c))
                        if not (is_first(f) and c < 4):
                            pe.wait_ge(g_read, (f * NC + 1) if c == 4 else ((f - 1) * NC + (5 if c == 0 else c + 1)))
                        product(gps, 0, c).then_inc(g_done, 1)

                    def u(c):
                        if not (is_first(f) and c < 4):
                            pe.wait_ge(u_read, (f * NC + 1) if c == 4 else ((f - 1) * NC + (5 if c == 0 else c + 1)))
                        product(ups, 1, c).then_inc(u_done, 1)

                    chunk_order(g, u)

                every_tile(pe, tile)

            @block.scalar
            def _(act):
                def high(n, slot, dst):
                    act.wait_ge(staged[slot], (n - slot) * 16 + 32)
                    act.copy(dst, stage[:, slot, :, :]).then_inc(part_hi, 1)

                high(0, 0, w[HI][:, 0, :, :])
                for n in range(H_PIECES):
                    high(n + 1, (n + 1) % 2, ht[HI][:, :, n * PIECE:(n + 1) * PIECE])
                act.wait_ge(zeroed, len(ZEROS))

                def tile(f, s):
                    def g(c):
                        act.wait_ge(g_done, f * NC + c + 1)
                        if not is_first(f):
                            act.wait_ge(tap[2], (f - 1) * NC + min(c + 2, NC))
                        act.copy(grow[:, G_AT[c]:G_AT[c] + CHUNKS[c][1]], gps[:, BANK[c], 0:CHUNKS[c][1]]).then_inc(g_read, 1)

                    def u(c):
                        act.wait_ge(tap[2], f * NC + c + 1)
                        part = res[:, SLOT[c], 0:CHUNKS[c][1]]
                        act.activation(part, part, ACT.Silu).then_inc(silu_done, 1)
                        if c == 0 and not is_last(f):
                            if not is_first(f):
                                act.wait_ge(u_done, f * NC)
                            high(piece_of(1) + f, (H_PIECES + 1 + s) % 2, w[HI][:, 1 - s, :, :])

                    chunk_order(g, u)

                every_tile(act, tile)

            @block.vector
            def _(dve):
                def low(n, slot, dst, hi):
                    dve.wait_ge(part_hi, n + 1)
                    dve.tensor_tensor(dst, stage[:, slot, :, :], hi.bitcast(F32), ALU.subtract).then_inc(part_lo, 1)

                low(0, 0, w[LO][:, 0, :, :], w[HI][:, 0, :, :])
                for n in range(H_PIECES):
                    at = slice(n * PIECE, (n + 1) * PIECE)
                    low(n + 1, (n + 1) % 2, ht[LO][:, :, at], ht[HI][:, :, at])
                dve.wait_ge(consts_loaded, 64)
                dve.wait_ge(zeroed, len(ZEROS))

                def tile(f, s):
                    par = lambda ap: ap[:, bass.ds(f, 1)]

                    def conv(c):
                        u0 = f * NC + c + 1
                        n = CHUNKS[c][1]
                        dve.wait_ge(g_read, f * NC + (c + 2 if c < NC - 2 else c + 1))
                        dve.wait_ge(stored[SLOT[c]], (uses(f, c) + 1) * 16)
                        out = res[:, SLOT[c], 0:n]
                        src = lambda tp: grow[:, G_AT[c] + tp - 1:G_AT[c] + tp - 1 + n]
                        dve.tensor_scalar(out, src(0), par(cw[:, 0]), par(cb[:, :]), ALU.mult, ALU.add).then_inc(tap[0], 1)
                        for tp in (1, 2):
                            dve.wait_ge(tap[tp - 1], u0)
                            dve.scalar_tensor_tensor(out, src(tp), par(cw[:, tp]), out, ALU.mult, ALU.add).then_inc(tap[tp], 1)

                    def gate(c):
                        n = CHUNKS[c][1]
                        dve.wait_ge(u_done, f * NC + c + 1)
                        dve.wait_ge(silu_done, f * NC + c + 1)
                        out = res[:, SLOT[c], 0:n]
                        dve.tensor_tensor(out, out, ups[:, BANK[c], 0:n], ALU.mult).then_inc(u_read, 1)
                        if c == 0 and not is_last(f):
                            low(piece_of(1) + f, (H_PIECES + 1 + s) % 2, w[LO][:, 1 - s, :, :], w[HI][:, 1 - s, :, :])

                    conv(0)
                    for c in range(NC):
                        if c + 1 < NC:
                            conv(c + 1)
                        gate(c)

                every_tile(dve, tile)


def ffn_down_phase(nc, f_t, w_down, x1, ln2_g, ln2_b, mod, out_all):
    GT = 4
    GROUPS_LAT = T_LAT // (GT * P)
    CT = T_CTX // P
    TAILS = GT
    with ExitStack() as ctx:
        sb, ps, sem = phase_tools(nc, ctx)
        fst = sb("fd_f_stage", [P, 2, GT * P])
        wst = sb("fd_w_stage", [P, 2, D])
        f = [sb(f"fd_f{h}", [P, 2, GT * P], F32R) for h in (HI, LO)]
        w = [sb(f"fd_w{h}", [P, 2, D], F32R) for h in (HI, LO)]
        x = sb("fd_x1", [P, GT, D])
        res = sb("fd_res", [P, GT, D])
        out = sb("fd_out", [P, 2, D])
        gate = sb("fd_gate", [P, 2, D])
        ln_g = sb("fd_ln_g", [P, D])
        ln_b = sb("fd_ln_b", [P, D])
        stats = sb("fd_stats", [P, 12])
        mv = sb("fd_mv", [P, 2])
        veps = sb("fd_veps", [P, 1])
        rstd = sb("fd_rstd", [P, 1])
        waited = sb("fd_waited", [P, 1])
        minus_half = sb("fd_minus_half", [P, 1])
        eps = sb("fd_eps", [P, 1])
        acc = ps("fd_acc", [P, GT, D])

        consts_loaded, half_done = sem("fd_consts_loaded"), sem("fd_half_done")
        staged = [sem(f"fd_staged{s}") for s in range(2)]
        hi_done, lo_done = sem("fd_hi_done"), sem("fd_lo_done")
        step_done, acc_done, gated = sem("fd_step_done"), sem("fd_acc_done"), sem("fd_gated")
        x_loaded, res_done, stats_done, mv_done = sem("fd_x_loaded"), sem("fd_res_done"), sem("fd_stats_done"), sem("fd_mv_done")
        veps_done, rstd_done, normed, scaled, out_done = (
            sem("fd_veps_done"), sem("fd_rstd_done"), sem("fd_normed"), sem("fd_scaled"), sem("fd_out_done"))
        stored = [sem(f"fd_stored{s}") for s in range(2)]
        f_tiles = f_t.rearrange("(f p) t -> f p t", p=P)
        w_tiles = w_down.rearrange("l (f p) n -> (l f) p n", p=P)
        x_groups = x1[0:T_LAT, :].rearrange("(g t p) d -> g p t d", p=P, t=GT)
        x_ctx = x1[T_LAT:T_ALL, :].rearrange("(t p) d -> p t d", p=P)
        out_tiles = out_all.rearrange("(t p) d -> t p d", p=P)

        def every_step(eng, body, tail, store=lambda *a: None):
            def group(g, tiles, after_first):
                for t in range(TAILS + 1):
                    for s in range(2):
                        body(g, 2 * t + s, s, tiles)
                        if after_first and t < TAILS:
                            tail(g - 1, t, LAT, s)
                    if after_first and t:
                        store(g - 1, t - 1)
                with eng.Fori(TAILS + 1, FT // 2 - 1) as i:
                    for s in range(2):
                        body(g, i * 2 + s, s, tiles)
                for s in range(2):
                    body(g, FT - 2 + s, s, tiles)

            group(0, GT, False)
            with eng.Fori(1, GROUPS_LAT) as g:
                group(g, GT, True)
            group(GROUPS_LAT, CT, True)
            for t in range(CT):
                for half in range(2):
                    tail(GROUPS_LAT, t, CTX, half)
                store(GROUPS_LAT, t)

        number = lambda g, t: g * GT + t
        is_step = lambda st, n: isinstance(st, int) and st == n
        is_first = lambda g: isinstance(g, int) and g == 0
        is_ctx = lambda g: isinstance(g, int) and g == GROUPS_LAT

        with nc.Block() as block:
            @block.sync
            def _(sp):
                for s in range(2):
                    sp.sem_inc(stored[s], 16)

                def load(g, st, slot, tiles):
                    n = tiles * P
                    if not (is_first(g) and isinstance(st, int) and st < 2):
                        sp.wait_ge(lo_done, g * FT + st - 1)
                    sp.dma_start(fst[:, slot, 0:n], f_tiles[st][:, bass.ds(g * (GT * P), n)]).then_inc(staged[slot], 16)
                    sp.dma_start(wst[:, slot, :], w_tiles[st]).then_inc(staged[slot], 16)
                    if is_first(g) and is_step(st, 1):
                        for v in range(2):
                            sp.dma_start(gate[:, v, :], mod[v, GATE2 * D:(GATE2 + 1) * D].partition_broadcast(P)).then_inc(consts_loaded, 16)
                        sp.dma_start(ln_g[:, :], ln2_g[0].partition_broadcast(P)).then_inc(consts_loaded, 16)
                        sp.dma_start(ln_b[:, :], ln2_b[0].partition_broadcast(P)).then_inc(consts_loaded, 16)
                    if is_step(st, FT - 2):
                        if not is_first(g):
                            sp.wait_ge(res_done, g * GT)
                        sp.dma_start(x[:, 0:tiles, :], x_ctx if is_ctx(g) else x_groups[g]).then_inc(x_loaded, 16)

                def store(g, t):
                    sp.wait_ge(out_done, number(g, t) + 1)
                    sp.dma_start(out_tiles[number(g, t)], out[:, t % 2, :]).then_inc(stored[t % 2], 16)

                every_step(sp, load, lambda *a: None, store)
                for s in range(2):
                    sp.wait_ge(stored[s], 16 * ((GROUPS_LAT * GT + CT) // 2 + 1))

            @block.scalar
            def _(act):
                def high(g, st, slot, tiles):
                    n = tiles * P
                    act.wait_ge(staged[slot], (g * FT + st - slot) * 16 + 32)
                    if not (is_first(g) and isinstance(st, int) and st < 2):
                        act.wait_ge(step_done, g * FT + st - 1)
                    act.copy(f[HI][:, slot, 0:n], fst[:, slot, 0:n])
                    act.copy(w[HI][:, slot, :], wst[:, slot, :]).then_inc(hi_done, 1)

                every_step(act, high, lambda *a: None)

            @block.tensor
            def _(pe):
                def step(g, st, slot, tiles):
                    pe.wait_ge(lo_done, g * FT + st + 1)
                    last = is_step(st, FT - 1)
                    for t in range(tiles):
                        if is_step(st, 0) and not is_first(g):
                            pe.wait_ge(gated, number(g - 1, t) + 1)
                        for half in range(2):
                            at = slice(half * 512, (half + 1) * 512)
                            for a, b in PASSES:
                                mm = pe.matmul(acc[:, t, at], f[a][:, slot, t * P:(t + 1) * P], w[b][:, slot, at],
                                               start=is_step(st, 0) and (a, b) == (HI, HI), stop=last and (a, b) == (LO, HI))
                        if last and t < tiles - 1:
                            mm.then_inc(acc_done, 1)
                    mm.then_inc(step_done, 1)

                every_step(pe, step, lambda *a: None)

            @block.vector
            def _(dve):
                def gate_sums(g, tiles, vec):
                    for t in range(tiles):
                        if t < tiles - 1:
                            dve.wait_ge(acc_done, g * (GT - 1) + t + 1)
                        else:
                            dve.wait_ge(step_done, (g + 1) * FT)
                        dve.wait_ge(scaled, number(g, t) + 1)
                        dve.tensor_tensor(res[:, t, :], acc[:, t, :], gate[:, vec, :], ALU.mult).then_inc(gated, 1)

                def low(g, st, slot, tiles):
                    n = tiles * P
                    dve.wait_ge(hi_done, g * FT + st + 1)
                    dve.tensor_tensor(f[LO][:, slot, 0:n], fst[:, slot, 0:n], f[HI][:, slot, 0:n].bitcast(F32), ALU.subtract)
                    dve.tensor_tensor(w[LO][:, slot, :], wst[:, slot, :], w[HI][:, slot, :].bitcast(F32), ALU.subtract).then_inc(lo_done, 1)
                    if is_step(st, 0) and not is_first(g):
                        gate_sums(g - 1, GT, LAT)
                    if is_ctx(g) and is_step(st, FT - 1):
                        gate_sums(g, CT, CTX)

                def tail(g, t, vec, half):
                    n = number(g, t)
                    if half == 0:
                        if t == 0:
                            dve.wait_ge(x_loaded, g * 16 + 16)
                        dve.wait_ge(gated, n + 1)
                        dve.scalar_tensor_tensor(res[:, t, :], x[:, t, :], ALPHA, res[:, t, :], ALU.mult, ALU.add).then_inc(res_done, 1)
                        dve.wait_ge(res_done, n + 1)
                        for h in range(2):
                            last = dve.bn_stats(stats[:, h * 6:h * 6 + 6], res[:, t, h * 512:(h + 1) * 512])
                        last.then_inc(stats_done, 1)
                        dve.wait_ge(stats_done, n + 1)
                        dve.tensor_copy(waited[:, :], stats[:, 0:1])
                        dve.bn_aggr(mv[:, :], stats[:, :]).then_inc(mv_done, 1)
                    else:
                        dve.wait_ge(rstd_done, n + 1)
                        dve.tensor_scalar(res[:, t, :], res[:, t, :], mv[:, 0:1], rstd[:, :], ALU.subtract, ALU.mult).then_inc(normed, 1)

                dve.wait_ge(consts_loaded, 64)
                every_step(dve, low, tail)

            @block.gpsimd
            def _(pool):
                pool.memset(minus_half[:, :], -0.5).then_inc(half_done, 1)
                pool.memset(eps[:, :], EPS).then_inc(half_done, 1)
                pool.wait_ge(half_done, 2)
                pool.sem_inc(scaled, GT)
                pool.wait_ge(consts_loaded, 64)

                def affine(g, t):
                    n, slot = number(g, t), t % 2
                    pool.wait_ge(mv_done, n + 1)
                    pool.tensor_tensor(veps[:, :], mv[:, 1:2], eps[:, :], ALU.add).then_inc(veps_done, 1)
                    pool.wait_ge(veps_done, n + 1)
                    pool.tensor_tensor(rstd[:, :], veps[:, :], minus_half[:, :], ALU.pow).then_inc(rstd_done, 1)
                    pool.wait_ge(normed, n + 1)
                    pool.tensor_tensor(res[:, t, :], res[:, t, :], ln_g[:, :], ALU.mult).then_inc(scaled, 1)
                    pool.wait_ge(scaled, n + GT + 1)
                    pool.wait_ge(stored[slot], (n - slot) * 8 + 16)
                    pool.tensor_tensor(out[:, slot, :], res[:, t, :], ln_b[:, :], ALU.add).then_inc(out_done, 1)

                with pool.Fori(0, GROUPS_LAT) as g:
                    for t in range(GT):
                        affine(g, t)
                for t in range(CT):
                    affine(GROUPS_LAT, t)


def shape_constants():
    import numpy as np

    def angles(rows, cols, n):
        return 2 * np.pi * (np.outer(rows, cols) % n) / n

    c64, s64 = np.zeros((P, P)), np.zeros((P, P))
    a = angles(np.arange(64), np.arange(64), 64)
    for h in (0, 64):
        c64[h:h + 64, h:h + 64] = np.cos(a) / 8
        s64[h:h + 64, h:h + 64] = -np.sin(a) / 8
    r = np.arange(512)
    a = angles(r, np.arange(4), T_LAT)
    twiddle = np.stack([np.cos(a), np.sin(a)], -1)
    a = angles(r, np.arange(512), 512)
    dft512 = np.stack([np.cos(a), np.sin(a)]) / np.sqrt(T_LAT)
    a = angles(np.arange(T_CTX), np.arange(T_CTX), T_CTX)
    dft256 = np.stack([np.cos(a), np.sin(a)]) / np.sqrt(T_CTX)
    col = np.arange(GRID)
    start = np.clip(col - 8, 0, GRID - 16)[:, None]
    col_mask = np.where((col >= start) & (col < start + 16), 0.0, MASKED)
    row_mask = np.zeros((2, GRID, 9, GRID))
    row_mask[0, :, 8] = MASKED
    row_mask[1, :, 0] = MASKED
    f = lambda v: np.ascontiguousarray(v, np.float32)
    return {"col_mask": f(np.tile(col_mask, (2, 1))), "row_mask": f(row_mask.reshape(P, 9 * GRID)), "ident": f(np.eye(P)), "dft_c64": f(c64), "dft_s64": f(s64), "twiddle": f(twiddle),
            "dft512": f(dft512), "dft256": f(dft256)}


def build_program(nc, x_all, conds, cache_k, cache_v, w_ada, b_ada, w_in, a_ws, a_bs, f_w, rpb, w_out, ln1_g, ln1_b,
                  w_gu, conv_w, conv_b, w_down, ln2_g, ln2_b,
                  ident, dft_c64, dft_s64, twiddle, dft512, dft256, col_mask, row_mask,
                  y_all, new_k, new_v):
    def scratch(name, shape, dt=F32):
        return nc.dram_tensor(name, shape, dt, kind="Internal").ap()

    mod = scratch("mod", [2, 6 * D])
    q_t = scratch("q_t", [2, D_C, T_ALL])
    k_t = scratch("k_t", [2, D_C, T_ALL + T_PAST])
    v_parts = scratch("v_parts", [T_ALL + T_PAST, 3 * D_C], BF16)
    chan_dft = scratch("chan_dft", [T_ALL, 2 * D_B])
    y = scratch("y_mixed", [T_ALL, D])
    rpb_pad = scratch("rpb_pad", [1, RPB_PAD + RPB + RPB_PAD])
    rel_bias = scratch("rel_bias", [GRID, HEADS * REL_ROWS, GRID])
    x1 = scratch("x1", [T_ALL, D])
    h2_t = scratch("h2_t", [D, T_ALL])
    f_t = scratch("f_t", [D_FF, T_ALL])

    with nc.cleanup_on_exit():
        modulation_phase(nc, conds, w_ada, b_ada, cache_k, cache_v, rpb, ident, mod, k_t, v_parts, rpb_pad, rel_bias)
        projection_phase(nc, x_all, w_in, a_ws, a_bs, f_w, ident, dft_c64, dft_s64,
                         mod, y, q_t, k_t, v_parts, chan_dft, new_k, new_v)
        fourier_phase(nc, chan_dft, twiddle, dft512, dft256, y)
        attention_phase(nc, q_t, k_t, v_parts, rel_bias, col_mask, row_mask, ident, y)
    mix_phase(nc, y, x_all, w_out, ln1_g, ln1_b, mod, ident, x1, h2_t)
    ffn_up_phase(nc, h2_t, w_gu, conv_w, conv_b, f_t)
    ffn_down_phase(nc, f_t, w_down, x1, ln2_g, ln2_b, mod, y_all)


WEIGHTS = ("cache_k", "cache_v", "w_ada", "b_ada", "w_in", "a_ws", "a_bs", "f_w", "rpb", "w_out", "ln1_g", "ln1_b",
           "w_gu", "conv_w", "conv_b", "w_down", "ln2_g", "ln2_b")
TABLES = ("ident", "dft_c64", "dft_s64", "twiddle", "dft512", "dft256", "col_mask", "row_mask")


def kernel(**inputs):
    import numpy as np
    import concourse.bacc as bacc
    from concourse.bass_utils import run_bass_kernel_spmd

    arrays = {"x_all": np.concatenate([inputs["x_sample"][0], inputs["x_prompt"][0]]),
              "conds": np.stack([inputs["c"][0], inputs["c_ctx"]])}
    arrays.update((name, np.ascontiguousarray(inputs[name])) for name in WEIGHTS)
    tables = shape_constants()
    arrays.update((name, tables[name]) for name in TABLES)
    outputs = {"y_all": (T_ALL, D), "new_k": (T_CTX, D_C), "new_v": (T_CTX, D_C)}

    nc = bacc.Bacc("TRN2", target_bir_lowering=False, num_devices=1)
    args = [nc.dram_tensor(f"in_{name}_dram", a.shape, mybir.dt.from_np(a.dtype), kind="ExternalInput").ap()
            for name, a in arrays.items()]
    args += [nc.dram_tensor(f"out_{name}_dram", shape, F32, kind="ExternalOutput").ap() for name, shape in outputs.items()]
    build_program(nc, *args)
    r = run_bass_kernel_spmd(nc, [{f"in_{name}_dram": a for name, a in arrays.items()}], core_ids=[0])
    y_all, new_k, new_v = (r.results[0][f"out_{name}_dram"] for name in outputs)
    cache_shape = (1, 1, T_CTX, HEADS, HD)
    return (y_all[T_LAT:].reshape(1, T_CTX, D), y_all[:T_LAT].reshape(1, T_LAT, D),
            new_k.reshape(cache_shape), new_v.reshape(cache_shape))
```

```python
from contextlib import ExitStack

import concourse.bass as bass
from concourse import mybir

F32 = mybir.dt.float32
F32R = mybir.dt.float32r
FP16 = mybir.dt.float16
BF16 = mybir.dt.bfloat16
ALU = mybir.AluOpType
ACT = mybir.ActivationFunctionType
AX_X = mybir.AxisListType.X

P = 128
D = 1024
KT = D // P
T_LAT, T_CTX, T_PAST = 2048, 256, 512
T_ALL = T_LAT + T_CTX
D_A, D_B, D_C = 256, 256, 512
HEADS, HD = 8, 64
A_HEADS = 4
GRID = 64
P_IN = 2 * D_A + D_B + 3 * D_C
COL_ZA, COL_ZB, COL_Q, COL_K, COL_V = 0, 512, 768, 1280, 1792
D_FF = 2816
REL_ROWS, REL_COLS = 15, 31
RPB = HEADS * REL_ROWS * REL_COLS
RPB_PAD = 64
MASKED = -1e30
FT = D_FF // P
ALPHA = 2.0 ** 0.25
EPS = 1e-6
HI, LO = 0, 1
ADA_COLS = 512
PASSES = ((HI, HI), (HI, LO), (LO, HI))
LAT, CTX = 0, 1
SHIFT1, SCALE1, GATE1, SHIFT2, SCALE2, GATE2 = range(6)


def phase_tools(nc, ctx):
    def sb(name, shape, dt=F32):
        return ctx.enter_context(nc.sbuf_tensor(name, shape, dt))

    def ps(name, shape, dt=F32):
        return ctx.enter_context(nc.psum_tensor(name, shape, dt))

    def sem(name):
        return nc.alloc_semaphore(name)

    return sb, ps, sem


def ada_columns(w_ada):
    return w_ada.rearrange("l (k p) (n c) -> (l n) p k c", p=P, c=ADA_COLS)


def modulation_phase(nc, conds, w_ada, b_ada, cache_k, cache_v, rpb, ident_in, mod, k_t, v_parts, rpb_pad, rel_bias):
    with ExitStack() as ctx:
        sb, ps, sem = phase_tools(nc, ctx)
        N = 2 * D // ADA_COLS
        w = sb("ada_w", [P, N, KT, ADA_COLS])
        cond = sb("ada_cond", [P, 2, KT])
        act = sb("ada_silu", [P, KT, 2])
        bias = sb("ada_bias", [2, 2 * D])
        row = sb("ada_row", [2, 2 * D])
        acc = ps("ada_acc", [P, N, ADA_COLS])
        small_loaded = sem("ada_small_loaded")
        w_loaded = [sem(f"ada_w_loaded{n}") for n in range(N)]
        silu_done = sem("ada_silu_done")
        acc_done = sem("ada_acc_done")
        acc_read = sem("ada_acc_read")
        stored = sem("ada_stored")
        CT = T_PAST // P
        ident = sb("ada_ident", [P, P])
        kc = sb("ada_kc", [P, CT, D_C])
        kct = [sb(f"ada_kct{h}", [P, D_C // P, T_PAST]) for h in (HI, LO)]
        vc = sb("ada_vc", [P, CT, HEADS, HD])
        vparts = sb("ada_vparts", [P, CT, HEADS, 3, HD], BF16)
        bias_row = sb("ada_bias_row", [1, RPB_PAD + RPB + RPB_PAD])
        kps = ps("ada_kps", [P, D_C // P, T_PAST])
        kc_loaded, kc_turned, kc_hi, kc_lo, kc_stored = (
            sem("ada_kc_loaded"), sem("ada_kc_turned"), sem("ada_kc_hi"), sem("ada_kc_lo"), sem("ada_kc_stored"))
        vc_loaded, vc_step, vc_stored = sem("ada_vc_loaded"), sem("ada_vc_step"), sem("ada_vc_stored")
        bias_zeroed, bias_loaded, bias_stored = sem("ada_bias_zeroed"), sem("ada_bias_loaded"), sem("ada_bias_stored")
        rel_stored = sem("ada_rel_stored")
        w_cols = ada_columns(w_ada)

        with nc.Block() as block:
            @block.sync
            def _(sp):
                with nc.allow_non_contiguous_dma(reason="two conditioning vectors, channel on partition"):
                    for v in (LAT, CTX):
                        sp.dma_start(cond[:, v, :], conds[v].rearrange("(k p) -> p k", p=P)).then_inc(small_loaded, 16)
                for v in range(2):
                    sp.dma_start(bias[v:v + 1, :], b_ada[:, 0:2 * D]).then_inc(small_loaded, 16)
                sp.dma_start(ident[:, :], ident_in).then_inc(kc_loaded, 16)
                sp.dma_start(kc[:, :, :], cache_k.rearrange("b l (n p) h d -> p (b l n) (h d)", p=P)).then_inc(kc_loaded, 16)
                sp.dma_start(vc[:, :, :, :], cache_v.rearrange("b l (n p) h d -> p (b l n) h d", p=P)).then_inc(vc_loaded, 16)
                sp.wait_ge(bias_zeroed, 1)
                sp.dma_start(bias_row[:, RPB_PAD:RPB_PAD + RPB], rpb.rearrange("l h r c -> l (h r c)")).then_inc(bias_loaded, 16)
                for n in range(N):
                    sp.dma_start(w[:, n], w_cols[n]).then_inc(w_loaded[n], 16)
                sp.wait_ge(bias_loaded, 16)
                sp.dma_start(rpb_pad, bias_row[:, :]).then_inc(bias_stored, 16)
                sp.wait_ge(kc_lo, D_C // P)
                for part in (HI, LO):
                    sp.dma_start(k_t[part, :, T_ALL:T_ALL + T_PAST].rearrange("(m p) t -> p m t", p=P), kct[part][:, :, :]).then_inc(kc_stored, 16)
                sp.wait_ge(vc_step, 5)
                sp.dma_start(v_parts[T_ALL:T_ALL + T_PAST, :].rearrange("(n p) c -> p n c", p=P),
                             vparts[:, :, :, :, :].rearrange("p n h k d -> p n (h k d)")).then_inc(vc_stored, 16)
                sp.wait_ge(bias_stored, 16)
                shifted = bass.AP(rpb_pad.tensor, RPB_PAD + REL_COLS // 2, [[REL_COLS, HEADS * REL_ROWS], [-1, GRID], [1, GRID]])
                sp.wait_ge(acc_read, N)
                sp.dma_start(mod[:, 0:2 * D], row[:, :]).then_inc(stored, 16)
                sp.dma_start(rel_bias.rearrange("q r k -> r q k"), shifted).then_inc(rel_stored, 16)
                sp.wait_ge(kc_stored, 32)
                sp.wait_ge(vc_stored, 16)
                sp.wait_ge(stored, 16)

            @block.scalar
            def _(act_):
                act_.wait_ge(small_loaded, 64)
                act_.activation(act[:, :, :].rearrange("p k v -> p v k"), cond[:, :, :], ACT.Silu).then_inc(silu_done, 1)
                for m in range(D_C // P):
                    act_.wait_ge(kc_turned, m + 1)
                    act_.copy(kct[HI][:, m, :].bitcast(F32R), kps[:, m, :]).then_inc(kc_hi, 1)

            @block.gpsimd
            def _(pool):
                pool.memset(bias_row[:, :], 0.0).then_inc(bias_zeroed, 1)
                pool.wait_ge(vc_loaded, 16)
                for n in range(3):
                    if n:
                        pool.wait_ge(vc_step, 2 * n)
                    pool.tensor_copy(vparts[:, :, :, n, :], vc[:, :, :, :]).then_inc(vc_step, 1)
                    if n < 2:
                        pool.wait_ge(vc_step, 2 * n + 1)
                        pool.tensor_tensor(vc[:, :, :, :], vc[:, :, :, :], vparts[:, :, :, n, :], ALU.subtract).then_inc(vc_step, 1)

            @block.tensor
            def _(pe):
                pe.wait_ge(kc_loaded, 32)
                for m in range(D_C // P):
                    for t in range(CT):
                        mm = pe.transpose(kps[:, m, t * P:(t + 1) * P], kc[:, t, m * P:(m + 1) * P], ident[:, :])
                    mm.then_inc(kc_turned, 1)
                pe.wait_ge(silu_done, 1)
                for n in range(N):
                    pe.wait_ge(w_loaded[n], 16)
                    for k in range(KT):
                        mm = pe.matmul(acc[0:2, n], act[:, k, :], w[:, n, k], start=k == 0, stop=k == KT - 1)
                    mm.then_inc(acc_done, 1)

            @block.vector
            def _(dve):
                for m in range(D_C // P):
                    dve.wait_ge(kc_hi, m + 1)
                    dve.tensor_tensor(kct[LO][:, m, :].bitcast(F32R), kps[:, m, :], kct[HI][:, m, :], ALU.subtract).then_inc(kc_lo, 1)
                dve.wait_ge(small_loaded, 64)
                for n in range(N):
                    dve.wait_ge(acc_done, n + 1)
                    at = slice(n * ADA_COLS, (n + 1) * ADA_COLS)
                    dve.tensor_tensor(row[:, at], acc[0:2, n], bias[:, at], ALU.add).then_inc(acc_read, 1)
    return rel_stored


def projection_phase(nc, x_all, w_in, a_ws, a_bs, f_w, ident_in, dft_c64, dft_s64,
                     mod, y, q_t, k_t, v_parts, chan_dft, new_k, new_v):
    G_TOK = 256
    NT = G_TOK // P
    GROUPS = T_ALL // G_TOK
    UNITS, PSLOTS, STAGES = 9, 3, 6
    SUB = KT // 2
    WCH = 6
    WC = P_IN // WCH
    with ExitStack() as ctx:
        sb, ps, sem = phase_tools(nc, ctx)
        w = [sb(f"pj_w{h}", [P, KT, P_IN], F32R) for h in (HI, LO)]
        ht = [sb(f"pj_ht{h}", [P, 2, KT, G_TOK], F32R) for h in (HI, LO)]
        x = sb("pj_x", [P, NT, D])
        hm = sb("pj_hm", [P, 2, G_TOK])
        st = sb("pj_out_stage", [P, 2, 512])
        st_lo = sb("pj_lo_stage", [P, 512])
        st_v = sb("pj_v_stage", [P, HEADS, 3, HD], BF16)
        zbt = sb("pj_zbt", [P, 2, G_TOK])
        zg = sb("pj_gelu", [P, 512])
        vn = sb("pj_vn", [P, D_A])
        ya = sb("pj_ya", [P, D_A])
        wst = sb("pj_wst", [P, A_HEADS, P])
        bd = sb("pj_bd", [P, 2, 2, P])
        ident = sb("pj_ident", [P, P])
        shift = sb("pj_shift", [P, 2, KT])
        scale = sb("pj_scale", [P, 2, KT])
        scale1p = sb("pj_scale1p", [P, 2, KT])
        bs = sb("pj_bs", [P, A_HEADS])
        stats = sb("pj_stats", [P, NT, 2, 6])
        mv = sb("pj_mv", [P, NT, 2])
        veps = sb("pj_veps", [P, NT])
        rstd = sb("pj_rstd", [P, NT])
        vstats = sb("pj_vstats", [P, 6])
        vmv = sb("pj_vmv", [P, 2])
        vveps = sb("pj_vveps", [P, 1])
        vrstd = sb("pj_vrstd", [P, 1])
        minus_half = sb("pj_minus_half", [P, 2])
        eps = sb("pj_eps", [P, 2])
        waited = sb("pj_waited", [P, 1])
        tps = ps("pj_tps", [P, 2, 2, G_TOK])
        gps = ps("pj_gps", [P, PSLOTS, 512])
        mixps = ps("pj_mixps", [P, 512])
        abps = ps("pj_abps", [P, 2, 512])

        consts_loaded, fw_zeroed, fw_loaded = sem("pj_consts_loaded"), sem("pj_fw_zeroed"), sem("pj_fw_loaded")
        setup_mm, setup_done, scale_done, half_done = (sem("pj_setup_mm"), sem("pj_setup_done"),
                                                       sem("pj_scale_done"), sem("pj_half_done"))
        w_staged = [sem(f"pj_w_staged{s}") for s in range(WCH)]
        w_hi, w_lo = sem("pj_w_hi"), sem("pj_w_lo")
        x_loaded = sem("pj_x_loaded")
        stats_done, mv_done, veps_done, rstd_done, xn_done = (
            sem("pj_stats_done"), sem("pj_mv_done"), sem("pj_veps_done"), sem("pj_rstd_done"), sem("pj_xn_done"))
        tps_done, hm_done, h_hi, h_lo = sem("pj_tps_done"), sem("pj_hm_done"), sem("pj_h_hi"), sem("pj_h_lo")
        unit_done = sem("pj_unit_done")
        slot_read = [sem(f"pj_slot_read{s}") for s in range(PSLOTS)]
        qk_hi, v_hi, v_mid, v_done, raw_done = sem("pj_qk_hi"), sem("pj_v_hi"), sem("pj_v_mid"), sem("pj_v_done"), sem("pj_raw_done")
        lo_stored, v_stored, raw_stored = sem("pj_lo_stored"), sem("pj_v_stored"), sem("pj_raw_stored")
        vstats_done, vmv_done, vveps_done, vrstd_done, vn_done = (
            sem("pj_vstats_done"), sem("pj_vmv_done"), sem("pj_vveps_done"),
            sem("pj_vrstd_done"), sem("pj_vn_done"))
        mix_done, ya_done, ya_stored = sem("pj_mix_done"), sem("pj_ya_done"), sem("pj_ya_stored")
        zbt_done, ab_done = sem("pj_zbt_done"), sem("pj_ab_done")
        ab_read = sem("pj_ab_read")
        st_stored = [sem(f"pj_st_stored{s}") for s in range(2)]
        N_CONSTS = 8

        w_tiles = w_in.rearrange("l (k p) n -> (l k) p n", p=P)
        x_flat = x[:, :, :].rearrange("p t d -> p (t d)")
        stage_w = [x_flat[:, n * WC:(n + 1) * WC] for n in range(WCH - 1)] + [st[:, 0, 0:WC]]
        x_groups = x_all.rearrange("(g t p) d -> g p t d", p=P, t=NT)
        tok = lambda g, t: bass.ds(g * G_TOK + t * P, P)
        grp = lambda g: bass.ds(g * G_TOK, G_TOK)
        qt_tiles = q_t.rearrange("x (m p) t -> x p m t", p=P)
        kt_tiles = k_t.rearrange("x (m p) t -> x p m t", p=P)
        fw2 = zg
        ws = hm
        v_rest = zg

        def every_group(eng, body):
            with eng.Fori(0, (GROUPS - 3) // 2) as i:
                for s in range(2):
                    body(i * 2 + s, s, True, LAT, False)
            body(GROUPS - 3, 0, True, LAT, False)
            body(GROUPS - 2, 1, False, CTX, False)
            body(GROUPS - 1, 0, False, None, True)

        with nc.Block() as block:
            @block.sync
            def _(sp):
                for s in range(2):
                    sp.sem_inc(st_stored[s], 16)
                sp.sem_inc(ya_stored, 16)
                sp.sem_inc(lo_stored, 16)
                sp.sem_inc(v_stored, 16)
                with nc.allow_non_contiguous_dma(reason="modulation and biases, channel on partition"):
                    for v in range(2):
                        for dst, what in ((shift, SHIFT1), (scale, SCALE1)):
                            sp.dma_start(dst[:, v, :], mod[v, what * D:(what + 1) * D].rearrange("(k p) -> p k", p=P)).then_inc(consts_loaded, 16)
                    sp.dma_start(bs[:, :], a_bs.rearrange("l h p -> p (l h)")).then_inc(consts_loaded, 16)
                sp.dma_start(ident[:, :], ident_in).then_inc(consts_loaded, 16)
                sp.dma_start(zbt[:, 0, 0:P], dft_c64).then_inc(consts_loaded, 16)
                sp.dma_start(zbt[:, 1, 0:P], dft_s64).then_inc(consts_loaded, 16)
                sp.dma_start(ws[:, :, :].rearrange("p a (b q) -> p (a b) q", q=P), a_ws.rearrange("l h p q -> p (l h) q")).then_inc(fw_loaded, 16)
                sp.wait_ge(fw_zeroed, 1)
                for g in range(4):
                    pair, half = g // 2, g % 2
                    sp.dma_start(fw2[half * 64:half * 64 + 64, pair * P + half * 64:pair * P + half * 64 + 64],
                                 f_w[0, g]).then_inc(fw_loaded, 16)
                with sp.Fori(0, KT) as k:
                    for n in range(WCH):
                        sp.wait_ge(w_lo, k * WCH + n + 1)
                        sp.dma_start(stage_w[n], w_tiles[k][:, n * WC:(n + 1) * WC]).then_inc(w_staged[n], 16)
                sp.wait_ge(w_lo, KT * WCH + WCH)
                sp.dma_start(x[:, :, :], x_groups[0]).then_inc(x_loaded, 16)
                sp.wait_ge(tps_done, SUB)
                sp.dma_start(x[:, :, :], x_groups[1]).then_inc(x_loaded, 16)

                def group(g, s, next2, next1, is_ctx):
                    if next2:
                        sp.wait_ge(tps_done, (g + 2) * SUB)
                        sp.dma_start(x[:, :, :], x_groups[g + 2]).then_inc(x_loaded, 16)
                    staged = [0]

                    def stage():
                        staged[0] += 1
                        return (staged[0] - 1) % 2

                    def store_qk(dst, m, unit, n):
                        slot = stage()
                        sp.wait_ge(slot_read[unit % PSLOTS], g * (UNITS // PSLOTS) + unit // PSLOTS + 2)
                        view = lambda ap: ap.rearrange("p (m t) -> p m t", m=2)
                        sp.dma_start(dst[HI][:, m:m + 2, grp(g)], view(st[:, slot, :])).then_inc(st_stored[slot], 16)
                        sp.dma_start(dst[LO][:, m:m + 2, grp(g)], view(st_lo[:, :])).then_inc(lo_stored, 16)

                    def store_ab(t):
                        slot = stage()
                        sp.wait_ge(ab_read, g * NT + t + 1 + NT)
                        sp.dma_start(chan_dft[tok(g, t), :], st[:, slot, :]).then_inc(st_stored[slot], 16)

                    def store_ya(t):
                        sp.wait_ge(ya_done, g * NT + t + 2)
                        sp.dma_start(y[tok(g, t), 0:D_A], ya[:, :]).then_inc(ya_stored, 16)

                    store_qk(qt_tiles, 0, 1, 0)
                    store_ya(0)
                    store_qk(qt_tiles, 2, 4, 1)
                    store_ya(1)
                    store_qk(kt_tiles, 0, 5, 2)
                    store_ab(0)
                    store_qk(kt_tiles, 2, 6, 3)
                    store_ab(1)
                    for t in range(NT):
                        sp.wait_ge(v_done, g * NT + t + 1)
                        sp.dma_start(v_parts[tok(g, t), :], st_v[:, :, :, :].rearrange("p h n d -> p (h n d)")).then_inc(v_stored, 16)
                    if is_ctx:
                        for n, (out, t) in enumerate(((new_v, 0), (new_v, 1), (new_k, 0), (new_k, 1))):
                            sp.wait_ge(raw_done, n + 1)
                            sp.dma_start(out[t * P:(t + 1) * P, :], x[:, t, (n // 2) * 512:(n // 2 + 1) * 512]).then_inc(raw_stored, 16)

                every_group(sp, group)
                for s in range(2):
                    sp.wait_ge(st_stored[s], 16 * (GROUPS * STAGES // 2 + 1))
                sp.wait_ge(lo_stored, 16 * (GROUPS * 4 + 1))
                sp.wait_ge(v_stored, 16 * (GROUPS * NT + 1))
                sp.wait_ge(raw_stored, 16 * 4)
                sp.wait_ge(ya_stored, 16 * (GROUPS * NT + 1))

            @block.gpsimd
            def _(pool):
                pool.memset(fw2[:, :], 0.0).then_inc(fw_zeroed, 1)
                pool.memset(minus_half[:, :], -0.5).then_inc(half_done, 1)
                pool.memset(eps[:, :], EPS).then_inc(half_done, 1)
                pool.wait_ge(half_done, 2)

                def row_rstd(n):
                    pool.wait_ge(mv_done, n * NT + NT)
                    pool.tensor_tensor(veps[:, :], mv[:, :, 1], eps[:, :], ALU.add).then_inc(veps_done, 1)
                    pool.wait_ge(veps_done, n + 1)
                    pool.tensor_tensor(rstd[:, :], veps[:, :], minus_half[:, :], ALU.pow).then_inc(rstd_done, 1)

                def gate_rstd(n):
                    pool.wait_ge(vmv_done, n + 1)
                    pool.tensor_tensor(vveps[:, :], vmv[:, 1:2], eps[:, 0:1], ALU.add).then_inc(vveps_done, 1)
                    pool.wait_ge(vveps_done, n + 1)
                    pool.tensor_tensor(vrstd[:, :], vveps[:, :], minus_half[:, 0:1], ALU.pow).then_inc(vrstd_done, 1)

                row_rstd(0)
                row_rstd(1)

                def group(g, s, next2, next1, is_ctx):
                    gate_rstd(g * NT)
                    if next2:
                        row_rstd(g + 2)
                    gate_rstd(g * NT + 1)

                every_group(pool, group)

            @block.scalar
            def _(act):
                for s in range(PSLOTS):
                    act.sem_inc(slot_read[s], 1)
                act.sem_inc(ab_read, NT)
                with act.Fori(0, KT) as k:
                    for n in range(WCH):
                        act.wait_ge(w_staged[n], k * 16 + 16)
                        act.copy(w[HI][:, k, n * WC:(n + 1) * WC], stage_w[n]).then_inc(w_hi, 1)

                def round_h(n, s, j, used=None):
                    if used is not None:
                        act.wait_ge(unit_done, used * UNITS)
                    act.wait_ge(hm_done, n * SUB * 2 + 2 * j + 2)
                    act.copy(ht[HI][:, s, 2 * j:2 * j + 2, :], hm[:, :, :]).then_inc(h_hi, 1)

                for j in range(SUB):
                    round_h(0, 0, j)

                def group(g, s, next2, next1, is_ctx):
                    if next1 is not None:
                        for j in range(SUB):
                            round_h(g + 1, 1 - s, j, used=g)
                    unit, staged = [0], [0]

                    def product():
                        unit[0] += 1
                        act.wait_ge(unit_done, g * UNITS + unit[0])
                        return (unit[0] - 1) % PSLOTS

                    def stage():
                        slot, use = staged[0] % 2, staged[0] // 2
                        staged[0] += 1
                        act.wait_ge(st_stored[slot], (g * (STAGES // 2) + use + 1) * 16)
                        return st[:, slot, :]

                    def gelu(t):
                        n = product()
                        act.wait_ge(ya_done, g * NT + t + 1)
                        if t == 0:
                            act.wait_ge(v_done, g * NT)
                        act.activation(zg[:, :], gps[:, n, :], ACT.Gelu_apprx_tanh).then_inc(slot_read[n], 1)

                    def round_qk(times=1.0):
                        n = product()
                        act.activation(stage().bitcast(F32R), gps[:, n, :], ACT.Copy, scale=times).then_inc(qk_hi, 1)

                    def ab_to_stage(t):
                        act.wait_ge(ab_done, g * NT + t + 1 + NT)
                        act.copy(stage(), abps[:, t, :]).then_inc(ab_read, 1)

                    gelu(0)
                    round_qk(HD ** -0.5)
                    n = product()
                    act.wait_ge(ab_done, g * NT + NT)
                    act.copy(zbt[:, :, :].rearrange("p m t -> p (m t)"), gps[:, n, :]).then_inc(slot_read[n], 1)
                    gelu(1)
                    round_qk(HD ** -0.5)
                    round_qk()
                    ab_to_stage(0)
                    round_qk()
                    ab_to_stage(1)
                    for t in range(NT):
                        n = product()
                        act.wait_ge(v_stored, (g * NT + t + 1) * 16)
                        if is_ctx:
                            act.copy(x[:, t, 0:512], gps[:, n, :]).then_inc(raw_done, 1)
                        act.copy(st_v[:, :, 0, :], gps[:, n, :].rearrange("p (h d) -> p h d", h=HEADS)).then_inc(v_hi, 1)
                    if is_ctx:
                        for t in range(NT):
                            n = product()
                            act.copy(x[:, t, 512:1024], gps[:, n, :]).then_inc(raw_done, 1)

                act.wait_ge(setup_mm, 2)
                every_group(act, group)

            @block.tensor
            def _(pe):
                pe.sem_inc(ab_done, NT)
                pe.wait_ge(consts_loaded, 16 * N_CONSTS)
                pe.wait_ge(fw_loaded, 16 * 5)
                for h in range(A_HEADS):
                    mm = pe.transpose(gps[:, 0, h * P:(h + 1) * P], ws[:, h // 2, (h % 2) * P:(h % 2 + 1) * P], ident[:, :])
                mm.then_inc(setup_mm, 1)
                for m in range(2):
                    for ri in range(2):
                        mm = pe.matmul(gps[:, 1, (2 * m + ri) * P:(2 * m + ri + 1) * P], zbt[:, ri, 0:P],
                                       fw2[:, m * P:(m + 1) * P], start=True, stop=True)
                mm.then_inc(setup_mm, 1)
                pe.wait_ge(setup_done, 2)

                def transposes(n, j):
                    if not (isinstance(n, int) and n == 0 and j < 2):
                        pe.wait_ge(hm_done, (n * SUB + j - 2) * 2 + 2)
                    for kk in range(2):
                        for t in range(NT):
                            k = 2 * j + kk
                            mm = pe.transpose(tps[:, j % 2, kk, t * P:(t + 1) * P], x[:, t, k * P:(k + 1) * P], ident[:, :])
                    mm.then_inc(tps_done, 1)

                pe.wait_ge(xn_done, NT)
                for j in range(SUB):
                    transposes(0, j)
                pe.wait_ge(w_lo, KT * WCH + WCH)

                def group(g, s, next2, next1, is_ctx):
                    def turn_next(js):
                        if next1 is not None:
                            if 0 in js:
                                pe.wait_ge(xn_done, (g + 1) * NT + NT)
                            for j in js:
                                transposes(g + 1, j)

                    unit = [0]

                    def product():
                        pe.wait_ge(slot_read[unit[0] % PSLOTS], g * (UNITS // PSLOTS) + unit[0] // PSLOTS + 1)
                        unit[0] += 1
                        return gps[:, (unit[0] - 1) % PSLOTS, :]

                    def rows(t, col):
                        out = product()
                        for k in range(KT):
                            for a, b in PASSES:
                                mm = pe.matmul(out, ht[a][:, s, k, t * P:(t + 1) * P], w[b][:, k, col:col + 512],
                                               start=(k, a, b) == (0, HI, HI), stop=(k, a, b) == (KT - 1, LO, HI))
                        mm.then_inc(unit_done, 1)

                    def channels(col):
                        out = product()
                        for m in range(2):
                            for k in range(KT):
                                for a, b in PASSES:
                                    mm = pe.matmul(out[:, m * G_TOK:(m + 1) * G_TOK],
                                                   w[a][:, k, col + m * P:col + (m + 1) * P], ht[b][:, s, k, :],
                                                   start=(k, a, b) == (0, HI, HI), stop=(k, a, b) == (KT - 1, LO, HI))
                        mm.then_inc(unit_done, 1)

                    def mix(t):
                        pe.wait_ge(vn_done, g * NT + t + 1)
                        pe.wait_ge(ya_done, g * NT + t + 1)
                        for h in range(A_HEADS):
                            mm = pe.matmul(mixps[:, h * HD:(h + 1) * HD], wst[:, h, :], vn[:, h * HD:(h + 1) * HD],
                                           start=True, stop=True)
                        mm.then_inc(mix_done, 1)

                    def channel_dft(t):
                        if t == 0:
                            pe.wait_ge(slot_read[2], g * (UNITS // PSLOTS) + 2)
                        pe.wait_ge(ab_read, g * NT + t + 1)
                        for m in range(2):
                            mm = pe.matmul(abps[:, t, m * 256:(m + 1) * 256], zbt[:, m, t * P:(t + 1) * P],
                                           bd[:, m, :, :].rearrange("p r c -> p (r c)"), start=True, stop=True)
                        mm.then_inc(ab_done, 1)

                    turn_next((0, 1))
                    rows(0, COL_ZA)
                    turn_next((2, 3))
                    channels(COL_Q)
                    channels(COL_ZB)
                    mix(0)
                    rows(1, COL_ZA)
                    channels(COL_Q + 256)
                    mix(1)
                    channels(COL_K)
                    channel_dft(0)
                    channels(COL_K + 256)
                    channel_dft(1)
                    for t in range(NT):
                        rows(t, COL_V)
                    if is_ctx:
                        for t in range(NT):
                            rows(t, COL_K)

                every_group(pe, group)

            @block.vector
            def _(dve):
                dve.sem_inc(w_lo, WCH)
                dve.sem_inc(ya_done, 1)
                dve.wait_ge(consts_loaded, 16 * N_CONSTS)
                dve.tensor_scalar(scale1p[:, :, :], scale[:, :, :], 1.0, None, ALU.add).then_inc(scale_done, 1)
                dve.wait_ge(setup_mm, 2)
                dve.tensor_copy(wst[:, :, :].rearrange("p h q -> p (h q)"), gps[:, 0, :]).then_inc(setup_done, 1)
                dve.tensor_copy(bd[:, :, :, :].rearrange("p m r c -> p (m r c)"), gps[:, 1, :]).then_inc(setup_done, 1)
                with dve.Fori(0, KT) as k:
                    for n in range(WCH):
                        dve.wait_ge(w_hi, k * WCH + n + 1)
                        at = slice(n * WC, (n + 1) * WC)
                        dve.tensor_tensor(w[LO][:, k, at], stage_w[n], w[HI][:, k, at].bitcast(F32),
                                          ALU.subtract).then_inc(w_lo, 1)

                def norm_x(n):
                    dve.wait_ge(x_loaded, n * 16 + 16)
                    for t in range(NT):
                        for half in range(2):
                            last = dve.bn_stats(stats[:, t, half, :], x[:, t, half * 512:(half + 1) * 512])
                    last.then_inc(stats_done, 1)
                    dve.wait_ge(stats_done, n + 1)
                    dve.tensor_copy(waited[:, :], stats[:, 0, 0, 0:1])
                    for t in range(NT):
                        dve.bn_aggr(mv[:, t, :], stats[:, t, :, :].rearrange("p a b -> p (a b)")).then_inc(mv_done, 1)
                    dve.wait_ge(rstd_done, n + 1)
                    for t in range(NT):
                        dve.tensor_scalar(x[:, t, :], x[:, t, :], mv[:, t, 0:1], rstd[:, t:t + 1],
                                          ALU.subtract, ALU.mult).then_inc(xn_done, 1)

                def modulate(n, s, vec, used=None):
                    if used is not None:
                        dve.wait_ge(unit_done, used * UNITS)
                    for j in range(SUB):
                        dve.wait_ge(tps_done, n * SUB + j + 1)
                        dve.wait_ge(h_lo, n * SUB + j)
                        for kk in range(2):
                            k = 2 * j + kk
                            dve.tensor_scalar(hm[:, kk, :], tps[:, j % 2, kk, :], scale1p[:, vec, k:k + 1],
                                              shift[:, vec, k:k + 1], ALU.mult, ALU.add).then_inc(hm_done, 1)
                        dve.wait_ge(h_hi, n * SUB + j + 1)
                        dve.tensor_tensor(ht[LO][:, s, 2 * j:2 * j + 2, :], hm[:, :, :],
                                          ht[HI][:, s, 2 * j:2 * j + 2, :].bitcast(F32), ALU.subtract).then_inc(h_lo, 1)

                norm_x(0)
                dve.wait_ge(scale_done, 1)
                modulate(0, 0, LAT)
                norm_x(1)

                def group(g, s, next2, next1, is_ctx):
                    if next1 is not None:
                        modulate(g + 1, 1 - s, next1, used=g)

                    def gate_norm(t):
                        n = g * NT + t
                        dve.wait_ge(slot_read[0], g * (UNITS // PSLOTS) + t + 2)
                        dve.bn_stats(vstats[:, :], zg[:, D_A:2 * D_A]).then_inc(vstats_done, 1)
                        dve.wait_ge(vstats_done, n + 1)
                        dve.tensor_copy(waited[:, :], vstats[:, 0:1])
                        dve.bn_aggr(vmv[:, :], vstats[:, :]).then_inc(vmv_done, 1)
                        dve.wait_ge(vrstd_done, n + 1)
                        dve.tensor_scalar(vn[:, :], zg[:, D_A:2 * D_A], vmv[:, 0:1], vrstd[:, :],
                                          ALU.subtract, ALU.mult).then_inc(vn_done, 1)

                    def gate(t):
                        n = g * NT + t
                        dve.wait_ge(mix_done, n + 1)
                        dve.wait_ge(ya_stored, n * 16 + 16)
                        for h in range(A_HEADS):
                            at = slice(h * HD, (h + 1) * HD)
                            last = dve.scalar_tensor_tensor(ya[:, at], mixps[:, at], bs[:, h:h + 1], zg[:, at], ALU.add, ALU.mult)
                        last.then_inc(ya_done, 1)

                    def low_qk(n, unit, times=1.0):
                        slot = unit % PSLOTS
                        dve.wait_ge(qk_hi, g * 4 + n + 1)
                        dve.wait_ge(lo_stored, (g * 4 + n + 1) * 16)
                        hi = st[:, (0, 1, 0, 0)[n], :]
                        dve.scalar_tensor_tensor(st_lo[:, :].bitcast(F32R), gps[:, slot, :], times, hi,
                                                 ALU.mult, ALU.subtract).then_inc(slot_read[slot], 1)

                    def v_tail(t, unit):
                        n = g * NT + t
                        slot = unit % PSLOTS
                        heads = lambda ap: ap.rearrange("p (h d) -> p h d", h=HEADS)
                        dve.wait_ge(v_hi, n + 1)
                        dve.tensor_tensor(heads(v_rest[:, :]), heads(gps[:, slot, :]), st_v[:, :, 0, :], ALU.subtract).then_inc(slot_read[slot], 1)
                        dve.wait_ge(slot_read[slot], g * (UNITS // PSLOTS) + unit // PSLOTS + 2)
                        dve.tensor_copy(st_v[:, :, 1, :], heads(v_rest[:, :])).then_inc(v_mid, 1)
                        dve.wait_ge(v_mid, n + 1)
                        dve.tensor_tensor(st_v[:, :, 2, :], heads(v_rest[:, :]), st_v[:, :, 1, :], ALU.subtract).then_inc(v_done, 1)

                    gate_norm(0)
                    low_qk(0, 1, HD ** -0.5)
                    gate(0)
                    if next2:
                        norm_x(g + 2)
                    gate_norm(1)
                    low_qk(1, 4, HD ** -0.5)
                    gate(1)
                    low_qk(2, 5)
                    low_qk(3, 6)
                    v_tail(0, 7)
                    v_tail(1, 8)

                every_group(dve, group)


def fourier_phase(nc, chan_dft, twiddle_in, dft512_in, dft256_in, conds, w_ada, b_ada, mod, y):
    R = 4
    with ExitStack() as ctx:
        sb, ps, sem = phase_tools(nc, ctx)
        tw = sb("fo_tw", [P, R, R, 2])
        table = [sb(f"fo_table{h}", [P, 2, R, 512], F32R) for h in (HI, LO)]
        w = sb("fo_w", [P, 2, KT, ADA_COLS])
        table_in = w[:, 1].rearrange("p (r i) m -> p r i m", r=2)
        cond = sb("fo_cond", [P, 2, KT])
        silu = sb("fo_silu", [P, KT, 2])
        bias = sb("fo_bias", [2, 2, ADA_COLS])
        row = sb("fo_row", [2, 2, ADA_COLS])
        ctab = sb("fo_ctab", [P, 2, 2, 256])
        x = sb("fo_x", [P, 4 * R, 512])
        xc = sb("fo_xc", [P, 2, 512])
        sums = sb("fo_sums", [P, 2, 2, 512])
        yj = sb("fo_y", [P, 2, R, 256])
        prod = sb("fo_prod", [P, 2, 256])
        ys = [sb(f"fo_ys{h}", [P, R, 2, R, 256], F32R) for h in (HI, LO)]
        out = sb("fo_out", [P, 4, 2, 256])
        acc = ps("fo_acc", [P, 4, 512])
        ada_acc = ps("fo_ada_acc", [P, 2, ADA_COLS])
        tables_loaded, x_loaded = sem("fo_tables_loaded"), [sem(f"fo_x_loaded{i}") for i in range(R)]
        xc_loaded = sem("fo_xc_loaded")
        table_hi, table_lo = sem("fo_table_hi"), sem("fo_table_lo")
        sums_done, bfly_done, prod_done, tw_done = sem("fo_sums_done"), sem("fo_bfly_done"), sem("fo_prod_done"), sem("fo_tw_done")
        y_hi, y_lo = sem("fo_y_hi"), sem("fo_y_lo")
        acc_done, acc_read = sem("fo_acc_done"), sem("fo_acc_read")
        stored = [sem(f"fo_stored{s}") for s in range(4)]
        ctx_stored = sem("fo_ctx_stored")
        cond_loaded, silu_done = sem("fo_cond_loaded"), sem("fo_silu_done")
        w_loaded = [sem(f"fo_w_loaded{s}") for s in range(2)]
        bias_loaded = [sem(f"fo_bias_loaded{s}") for s in range(2)]
        ada_done, ada_read = sem("fo_ada_done"), sem("fo_ada_read")
        row_stored = [sem(f"fo_row_stored{s}") for s in range(2)]
        FIRST, CHUNKS = 2 * D // ADA_COLS, 4 * D // ADA_COLS
        w_cols = ada_columns(w_ada)
        UNITS = 8

        y_lat = y[0:T_LAT, D_A:D_A + D_B].rearrange("(m p j) c -> m p j c", p=P, j=R)
        flat = lambda ap: ap.rearrange("p a b c d -> p (a b c d)")
        SPLITS = R

        with nc.Block() as block:
            @block.sync
            def _(sp):
                xs = chan_dft[0:T_LAT, :].rearrange("(q i p) c -> i p q c", p=P, i=R)

                def store_unit(u):
                    jp, m = u // R, u % R
                    sp.wait_ge(acc_read, 4 + u + 1)
                    sp.dma_start(y_lat[m, :, 2 * jp:2 * jp + 2, :], out[:, u % 4, :, :]).then_inc(stored[u % 4], 16)

                with nc.allow_non_contiguous_dma(reason="two conditioning vectors, channel on partition"):
                    for v in (LAT, CTX):
                        sp.dma_start(cond[:, v, :], conds[v].rearrange("(k p) -> p k", p=P)).then_inc(cond_loaded, 16)

                def load_chunk(c):
                    slot, col = c % 2, (FIRST + c) * ADA_COLS
                    if c >= 2:
                        sp.wait_ge(ada_done, c - 1)
                    sp.dma_start(w[:, slot], w_cols[FIRST + c]).then_inc(w_loaded[slot], 16)
                    if c >= 2:
                        sp.wait_ge(ada_read, c - 1)
                    for v in range(2):
                        sp.dma_start(bias[v:v + 1, slot, :], b_ada[:, col:col + ADA_COLS]).then_inc(bias_loaded[slot], 16)

                def store_chunk(c):
                    col = (FIRST + c) * ADA_COLS
                    sp.wait_ge(ada_read, c + 1)
                    sp.dma_start(mod[:, col:col + ADA_COLS], row[:, c % 2, :]).then_inc(row_stored[c % 2], 16)

                sp.dma_start(tw[:, :, :, :], twiddle_in.rearrange("(i p) j r -> p i j r", p=P)).then_inc(tables_loaded, 16)
                for i in range(R):
                    sp.dma_start(x[:, i * R:(i + 1) * R, :], xs[i]).then_inc(x_loaded[i], 16)
                    if i == 0:
                        sp.dma_start(table_in, dft512_in.rearrange("r (i p) m -> p r i m", p=P)).then_inc(tables_loaded, 16)
                        load_chunk(0)
                sp.dma_start(ctab[:, :, :, :], dft256_in.rearrange("r (i p) m -> p r i m", p=P)).then_inc(xc_loaded, 16)
                sp.dma_start(xc[:, :, :], chan_dft[T_LAT:T_ALL, :].rearrange("(i p) c -> p i c", p=P)).then_inc(xc_loaded, 16)
                sp.wait_ge(table_lo, 1)
                load_chunk(1)
                for c in range(2, CHUNKS):
                    load_chunk(c)
                    store_chunk(c - 2)
                    if c in (4, 5):
                        store_unit(2 * c - 8)
                        store_unit(2 * c - 7)
                for u in range(4, UNITS):
                    store_unit(u)
                for c in (CHUNKS - 2, CHUNKS - 1):
                    store_chunk(c)
                for t in range(2):
                    sp.wait_ge(acc_read, 4 + UNITS + t + 1)
                    sp.dma_start(y[T_LAT + t * P:T_LAT + (t + 1) * P, D_A:D_A + D_B], out[:, t, 0, :]).then_inc(ctx_stored, 16)
                for s in range(4):
                    sp.wait_ge(stored[s], UNITS // 4 * 16)
                for s in range(2):
                    sp.wait_ge(row_stored[s], CHUNKS // 2 * 16)
                sp.wait_ge(ctx_stored, 32)

            @block.scalar
            def _(act):
                act.sem_inc(acc_read, 4)
                act.wait_ge(tables_loaded, 32)
                act.copy(table[HI][:, :, :, :].rearrange("p r i m -> p (r i m)"), table_in.rearrange("p r i m -> p (r i m)")).then_inc(table_hi, 1)
                act.wait_ge(cond_loaded, 32)
                act.activation(silu[:, :, :].rearrange("p k v -> p v k"), cond[:, :, :], ACT.Silu).then_inc(silu_done, 1)
                for i in range(R):
                    act.wait_ge(bfly_done, 8 * (i + 1))
                    act.wait_ge(tw_done, 3 * 4 * (i + 1))
                    act.copy(ys[HI][:, i].rearrange("p r j c -> p (r j c)"), yj[:, :, :, :].rearrange("p r j c -> p (r j c)")).then_inc(y_hi, 1)
                for u in range(UNITS + 2):
                    act.wait_ge(acc_done, u + 1)
                    if u >= 4:
                        act.wait_ge(stored[u % 4], u // 4 * 16)
                    if u < UNITS:
                        act.copy(out[:, u % 4, :, :].rearrange("p j c -> p (j c)"), acc[:, u % 4, :]).then_inc(acc_read, 1)
                    else:
                        act.copy(out[:, u % 4, 0, :], acc[:, u % 4, 0:256]).then_inc(acc_read, 1)

            @block.vector
            def _(dve):
                def add_bias(c):
                    dve.wait_ge(ada_done, c + 1)
                    dve.wait_ge(bias_loaded[c % 2], (c // 2 + 1) * 32)
                    if c >= 2:
                        dve.wait_ge(row_stored[c % 2], c // 2 * 16)
                    dve.tensor_tensor(row[:, c % 2, :], ada_acc[0:2, c % 2, :], bias[:, c % 2, :], ALU.add).then_inc(ada_read, 1)

                for i in range(R):
                    xi = x[:, i * R:(i + 1) * R, :]
                    dve.wait_ge(x_loaded[i], 16)
                    for odd in range(2):
                        for diff in range(2):
                            dve.tensor_tensor(sums[:, odd, diff, :], xi[:, odd, :], xi[:, odd + 2, :],
                                              ALU.subtract if diff else ALU.add).then_inc(sums_done, 1)
                    dve.wait_ge(sums_done, 4 * (i + 1))
                    part = lambda odd, diff, ri: sums[:, odd, diff, :].rearrange("p (h r c) -> p r h c", h=2, r=2)[:, ri]
                    y_of = lambda ri, j: yj[:, ri, j, :].rearrange("p (h c) -> p h c", h=2)
                    for ri in range(2):
                        for j in (0, 2):
                            dve.tensor_tensor(y_of(ri, j), part(0, 0, ri), part(1, 0, ri),
                                              ALU.subtract if j else ALU.add).then_inc(bfly_done, 1)
                    for ri in range(2):
                        for j in (1, 3):
                            op = ALU.add if (ri == 0) == (j == 1) else ALU.subtract
                            dve.tensor_tensor(y_of(ri, j), part(0, 1, ri), part(1, 1, 1 - ri), op).then_inc(bfly_done, 1)
                    if i == 0:
                        dve.wait_ge(tables_loaded, 32)
                    dve.wait_ge(bfly_done, 8 * (i + 1))
                    for j in range(1, R):
                        n = (i * 3 + j - 1)
                        cos, sin = tw[:, i, j, 0:1], tw[:, i, j, 1:2]
                        if n:
                            dve.wait_ge(tw_done, 4 * n)
                        dve.tensor_scalar(prod[:, 0, :], yj[:, 1, j, :], sin, None, ALU.mult).then_inc(prod_done, 1)
                        dve.tensor_scalar(prod[:, 1, :], yj[:, 0, j, :], sin, None, ALU.mult).then_inc(prod_done, 1)
                        dve.wait_ge(prod_done, 2 * n + 2)
                        dve.scalar_tensor_tensor(yj[:, 0, j, :], yj[:, 0, j, :], cos, prod[:, 0, :],
                                                 ALU.mult, ALU.add).then_inc(tw_done, 2)
                        dve.scalar_tensor_tensor(yj[:, 1, j, :], yj[:, 1, j, :], cos, prod[:, 1, :],
                                                 ALU.mult, ALU.subtract).then_inc(tw_done, 2)
                    if i == 0:
                        dve.wait_ge(table_hi, 1)
                        dve.tensor_tensor(table[LO][:, :, :, :].rearrange("p r i m -> p (r i m)"), table_in.rearrange("p r i m -> p (r i m)"),
                                          table[HI][:, :, :, :].rearrange("p r i m -> p (r i m)").bitcast(F32), ALU.subtract).then_inc(table_lo, 1)
                    dve.wait_ge(y_hi, i + 1)
                    dve.tensor_tensor(ys[LO][:, i].rearrange("p r j c -> p (r j c)"), yj[:, :, :, :].rearrange("p r j c -> p (r j c)"),
                                      ys[HI][:, i].rearrange("p r j c -> p (r j c)").bitcast(F32), ALU.subtract).then_inc(y_lo, 1)
                    if i >= 1:
                        add_bias(i - 1)
                for c in range(R - 1, CHUNKS):
                    add_bias(c)

            @block.tensor
            def _(pe):
                def ada_product(c):
                    if c == 0:
                        pe.wait_ge(silu_done, 1)
                    pe.wait_ge(w_loaded[c % 2], (c // 2 + 1) * 16)
                    if c >= 2:
                        pe.wait_ge(ada_read, c - 1)
                    for k in range(KT):
                        mm = pe.matmul(ada_acc[0:2, c % 2], silu[:, k, :], w[:, c % 2, k], start=k == 0, stop=k == KT - 1)
                    mm.then_inc(ada_done, 1)

                ada_product(0)
                pe.wait_ge(table_lo, 1)
                for jp in range(2):
                    for i in range(R):
                        if jp == 0:
                            pe.wait_ge(y_lo, i + 1)
                        for m in range(R):
                            if i == 0:
                                pe.wait_ge(acc_read, jp * R + m + 1)
                            for ri in range(2):
                                for a, b in PASSES:
                                    first, last = (i, ri, a, b) == (0, 0, HI, HI), (i, ri, a, b) == (R - 1, 1, LO, HI)
                                    mm = pe.matmul(acc[:, m, :], table[a][:, ri, i, m * P:(m + 1) * P],
                                                   ys[b][:, i, ri, 2 * jp:2 * jp + 2, :].rearrange("p j c -> p (j c)"),
                                                   start=first, stop=last)
                            if i == R - 1:
                                mm.then_inc(acc_done, 1)
                        if jp * R + i < CHUNKS - 1:
                            ada_product(jp * R + i + 1)
                pe.wait_ge(xc_loaded, 32)
                for t in range(2):
                    pe.wait_ge(acc_read, UNITS + t + 1)
                    for h in range(2):
                        for n, (i, ri) in enumerate(((0, 0), (0, 1), (1, 0), (1, 1))):
                            mm = pe.matmul(acc[:, t, h * P:(h + 1) * P], ctab[:, ri, i, t * P:(t + 1) * P],
                                           xc[:, i, (2 * h + ri) * P:(2 * h + ri + 1) * P], start=n == 0, stop=n == 3)
                    mm.then_inc(acc_done, 1)


def attention_phase(nc, q_t, k_t, v_parts, rel_bias, rel_stored, col_mask_in, row_mask_in, ident_in, y):
    TILES, EDGES, INNER = 18, 4, 12
    EDGE_T = (0, 1, 14, 15)
    WIN, WIN_IN = 8 * GRID, 9 * GRID
    KCOLS = T_ALL + T_PAST
    VT = KCOLS // P
    VT_CTX, VT_PAST = T_LAT // P, T_ALL // P
    E_ROWS = 14
    with ExitStack() as ctx:
        sb, ps, sem = phase_tools(nc, ctx)
        ident = sb("at_ident", [P, P])
        col_mask = sb("at_col_mask", [P, GRID])
        row_mask = sb("at_row_mask", [P, WIN_IN])
        qs = sb("at_q", [P, 2, T_ALL], F32R)
        bin_ = sb("at_bias_in", [P, E_ROWS, GRID])
        k = [sb(f"at_k{h}", [P, 2, KCOLS], F32R) for h in (HI, LO)]
        vp = sb("at_v_parts", [P, 2, VT, 3, HD], BF16)
        ebias = sb("at_edge_bias", [P, 2, E_ROWS, GRID])
        ibias = sb("at_inner_bias", [P, 2, WIN_IN])
        sl = sb("at_local_scores", [P, 2, WIN_IN])
        prob = sb("at_prob", [P, 2, WIN_IN + T_PAST])
        ph = sb("at_prob_hi", [P, 2, 9, P], FP16)
        pl = sb("at_prob_lo", [P, 2, 9, P], FP16)
        ncmax = sb("at_neg_context_max", [P, 2])
        lmax = sb("at_local_max", [P, 2])
        nmx = sb("at_neg_max", [P, 2])
        sums = sb("at_sums", [P, 3, 2])
        den = sb("at_den", [P, 3])
        rden = sb("at_rden", [P, 3])
        minus_one = sb("at_minus_one", [P, 1])
        osum = sb("at_osum", [P, 2, HD])
        out = sb("at_out", [P, 2, TILES, HD])
        loc_ps = ps("at_loc_ps", [P, 2, 512])
        ctx_ps = ps("at_ctx_ps", [P, 2, 512])
        ta_ps = ps("at_ta_ps", [P, 4, P])
        tb_ps = ps("at_tb_ps", [P, 4, P])
        th_ps = ps("at_th_ps", [P, 512])
        o_ps = ps("at_o_ps", [P, 2, 256])

        consts_loaded, minus_one_done = sem("at_consts_loaded"), sem("at_minus_one_done")
        qk_loaded = [sem(f"at_qk_loaded{s}") for s in range(2)]
        v_loaded = [sem(f"at_v_loaded{s}") for s in range(2)]
        bias_loaded, ebias_done, bias_ready = sem("at_bias_loaded"), sem("at_ebias_done"), sem("at_bias_ready")
        qk_done = sem("at_qk_done")
        cmax_done, smax_done, nmax_done, exp_done = sem("at_cmax_done"), sem("at_smax_done"), sem("at_nmax_done"), sem("at_exp_done")
        exp_local_done, lo_a = sem("at_exp_local_done"), sem("at_lo_a")
        ta_done, tb_done, hi_a, hi_b, lo_done = sem("at_ta_done"), sem("at_tb_done"), sem("at_hi_a"), sem("at_hi_b"), sem("at_lo_done")
        pv_done, den_done, rden_done, o_read, out_done = (
            sem("at_pv_done"), sem("at_den_done"), sem("at_rden_done"), sem("at_o_read"), sem("at_out_done"))
        stored = [sem(f"at_stored{s}") for s in range(2)]

        v_tiles = v_parts.rearrange("(n p) c -> p n c", p=P)
        y_tiles = y.rearrange("(n p) c -> p n c", p=P)
        DMAS_QK = 6
        BIAS_POS = 6

        def kind(pos):
            if EDGES <= pos < EDGES + INNER:
                return (pos - EDGES) * P, WIN_IN, (pos - EDGES + 2) * P
            if pos < EDGES:
                return (0 if pos < 2 else T_LAT - WIN), WIN, EDGE_T[pos] * P
            return None, 0, T_LAT + (pos - EDGES - INNER) * P

        def every_tile(eng, body):
            def one_head(h, parity, first, last):
                for p in range(TILES):
                    before = (h, parity, p - 1) if p else (None if first else (h - 1, 1 - parity, TILES - 1))
                    after = (h, parity, p + 1) if p < TILES - 1 else (None if last else (h + 1, 1 - parity, 0))
                    body(before, (h, parity, p), after)

            one_head(0, 0, True, False)
            with eng.Fori(0, (HEADS - 2) // 2) as i:
                for s in range(2):
                    one_head(i * 2 + (1 + s), 1 - s, False, False)
            one_head(HEADS - 1, 1, False, True)

        with nc.Block() as block:
            @block.sync
            def _(sp):
                sp.sem_inc(stored[0], 16)
                sp.sem_inc(stored[1], 16)
                sp.dma_start(ident[:, :], ident_in).then_inc(consts_loaded, 16)
                sp.dma_start(col_mask[:, :], col_mask_in).then_inc(consts_loaded, 16)
                sp.dma_start(row_mask[:, :], row_mask_in).then_inc(consts_loaded, 16)

                def load_head(h, parity, bias_read=None):
                    rows = bass.ds(h * HD, HD)
                    for half in range(2):
                        for part in (HI, LO):
                            sp.dma_start(k[part][half * HD:(half + 1) * HD, parity, :].bitcast(F32), k_t[part, rows, :]).then_inc(qk_loaded[parity], 16)
                        sp.dma_start(qs[half * HD:(half + 1) * HD, parity, :].bitcast(F32), q_t[half, rows, :]).then_inc(qk_loaded[parity], 16)
                    sp.dma_start(vp[:, parity].rearrange("p t n d -> p t (n d)"),
                                 v_tiles[:, :, bass.ds(h * (3 * HD), 3 * HD)]).then_inc(v_loaded[parity], 16)
                    if bias_read is not None:
                        sp.wait_ge(bias_ready, bias_read)
                    elif rel_stored is not None:
                        sp.wait_ge(rel_stored, 16)
                    for half in range(2):
                        src = rel_bias[:, bass.ds(h * REL_ROWS + (1 - half), E_ROWS), :]
                        sp.dma_start(bin_[half * HD:(half + 1) * HD, :, :], src).then_inc(bias_loaded, 16)

                load_head(0, 0)

                def one_head(h, parity, last):
                    if not last:
                        sp.wait_ge(pv_done, h * TILES + 2)
                        load_head(h + 1, 1 - parity, bias_read=h + 1)
                    sp.wait_ge(out_done, (h + 1) * TILES)
                    sp.dma_start(y_tiles[:, :, bass.ds(h * HD + (D_A + D_B), HD)], out[:, parity]).then_inc(stored[parity], 16)

                with sp.Fori(0, HEADS // 2 - 1) as i:
                    for s in range(2):
                        one_head(i * 2 + s, s, False)
                one_head(HEADS - 2, 0, False)
                one_head(HEADS - 1, 1, True)
                for s in range(2):
                    sp.wait_ge(stored[s], 16 * (HEADS // 2 + 1))

            @block.gpsimd
            def _(pool):
                pool.memset(minus_one[:, :], -1.0).then_inc(minus_one_done, 1)
                pool.wait_ge(minus_one_done, 1)
                pool.wait_ge(consts_loaded, 48)

                def edge_bias(h, parity):
                    pool.wait_ge(bias_loaded, (h + 1) * 32)
                    pool.tensor_tensor(ebias[:, parity], bin_[:, :, :],
                                       col_mask[:, :].unsqueeze(1).to_broadcast([P, E_ROWS, GRID]), ALU.add).then_inc(ebias_done, 1)

                def inner_bias(h, parity):
                    pool.wait_ge(ebias_done, h + 1)
                    pool.tensor_tensor(ibias[:, parity, :], ebias[:, parity, 2:11, :].rearrange("p e c -> p (e c)"),
                                       row_mask[:, :], ALU.add).then_inc(bias_ready, 1)

                def step(before, tile, after):
                    h, parity, pos = tile
                    u, n = h * TILES + pos, pos % 3
                    pool.wait_ge(exp_done, u + 3)
                    if kind(pos)[1]:
                        pool.tensor_tensor(den[:, n:n + 1], sums[:, n, 0:1], sums[:, n, 1:2], ALU.add).then_inc(den_done, 1)
                        pool.wait_ge(den_done, h * (EDGES + INNER) + pos + 1)
                        pool.tensor_tensor(rden[:, n:n + 1], den[:, n:n + 1], minus_one[:, :], ALU.pow).then_inc(rden_done, 1)
                    else:
                        pool.tensor_tensor(rden[:, n:n + 1], sums[:, n, 1:2], minus_one[:, :], ALU.pow).then_inc(rden_done, 1)
                    if not (isinstance(h, int) and h == HEADS - 1):
                        if pos == BIAS_POS:
                            edge_bias(h + 1, 1 - parity)
                        if pos == BIAS_POS + 3:
                            inner_bias(h + 1, 1 - parity)

                edge_bias(0, 0)
                inner_bias(0, 0)
                every_tile(pool, step)

            @block.tensor
            def _(pe):
                pe.sem_inc(qk_done, 2)
                pe.sem_inc(pv_done, 2)
                pe.wait_ge(consts_loaded, 48)

                def head_uses(h, parity):
                    return (h - parity) // 2 + 1 if isinstance(h, int) else ((h - parity) >> 1) + 1

                def qk(tile):
                    h, parity, pos = tile
                    s, inner = pos % 2, EDGES <= pos < EDGES + INNER
                    u = h * TILES + pos
                    if pos == 0:
                        pe.wait_ge(qk_loaded[parity], head_uses(h, parity) * (16 * DMAS_QK))
                    pe.wait_ge(nmax_done, u)
                    pe.wait_ge(exp_done, u + 1)
                    key0, n, token = kind(pos)
                    q = qs[:, parity, token:token + P]
                    for c in range(2 if n else 0):
                        w = n // 2
                        for b in (HI, LO):
                            pe.matmul(loc_ps[:, c, 0:w], q, k[b][:, parity, key0 + c * w:key0 + (c + 1) * w],
                                      start=b == HI, stop=b == LO)
                    col, w = (T_ALL, T_PAST) if n else (T_LAT, T_CTX)
                    for b in (HI, LO):
                        mm = pe.matmul(ctx_ps[:, s, 0:w], q, k[b][:, parity, col:col + w], start=b == HI, stop=b == LO)
                    mm.then_inc(qk_done, 1)

                def turn(tile):
                    h, parity, pos = tile
                    s, inner = pos % 2, EDGES <= pos < EDGES + INNER
                    u = h * TILES + pos
                    n = kind(pos)[1]
                    if n:
                        n_loc = h * (EDGES + INNER) + pos
                        pe.wait_ge(exp_local_done, n_loc + 1)
                        if not (isinstance(h, int) and h == 0 and pos == 0):
                            pe.wait_ge(lo_a, n_loc)
                        for b in range(4):
                            mm = pe.transpose(ta_ps[:, b, :], prob[:, s, b * P:(b + 1) * P], ident[:, :])
                        mm.then_inc(ta_done, 1)
                    pe.wait_ge(exp_done, u + 3)
                    pe.wait_ge(lo_done, u)
                    for b in range(4 if n else 2):
                        if inner and b == 1:
                            pe.transpose(th_ps[0:GRID, 0:P], prob[:, s, 4 * P:4 * P + GRID], ident[:, :])
                        mm = pe.transpose(tb_ps[:, b, :], prob[:, s, n + b * P:n + (b + 1) * P], ident[:, :])
                    mm.then_inc(tb_done, 1)

                def pv(tile):
                    h, parity, pos = tile
                    s, inner = pos % 2, EDGES <= pos < EDGES + INNER
                    u = h * TILES + pos
                    if pos == 0:
                        pe.wait_ge(v_loaded[parity], head_uses(h, parity) * 16)
                    pe.wait_ge(lo_done, u + 1)
                    pe.wait_ge(o_read, u + 2)
                    key0, n, _ = kind(pos)
                    vt = key0 // P if n else None
                    blocks = [(b, vt + b, P) for b in range(4)] if n else []
                    if inner:
                        blocks.append((8, vt + 4, GRID))
                    blocks += [(4 + b, (VT_PAST if n else VT_CTX) + b, P) for b in range(4 if n else 2)]
                    for i, (b, v, rows) in enumerate(blocks):
                        for part, width in ((ph, 3), (pl, 2)):
                            mm = pe.matmul(o_ps[:, s, 0:width * HD], part[0:rows, s, b, :],
                                           vp[0:rows, parity, v, 0:width, :].rearrange("p n d -> p (n d)"),
                                           start=i == 0 and width == 3, stop=i == len(blocks) - 1 and width == 2)
                    mm.then_inc(pv_done, 1)

                def step(before, tile, after):
                    if after is not None:
                        qk(after)
                    turn(tile)
                    if before is not None:
                        pv(before)

                qk((0, 0, 0))
                every_tile(pe, step)
                pv((HEADS - 1, 1, TILES - 1))

            @block.vector
            def _(dve):
                dve.sem_inc(o_read, 2)
                dve.wait_ge(consts_loaded, 48)

                def row_max(tile):
                    h, parity, pos = tile
                    s, inner = pos % 2, EDGES <= pos < EDGES + INNER
                    u = h * TILES + pos
                    key0, n, _ = kind(pos)
                    if pos == 0:
                        dve.wait_ge(bias_ready, h + 1)
                    dve.wait_ge(qk_done, u + 3)
                    w = T_PAST if n else T_CTX
                    if n:
                        if inner:
                            bias = ibias[:, parity, :]
                        else:
                            e0 = (0 if pos < 2 else GRID // 2 - 8) - 2 * EDGE_T[pos] + 7 - 1
                            bias = ebias[:, parity, e0:e0 + 8, :].rearrange("p e c -> p (e c)")
                    dve.tensor_reduce(ncmax[:, s:s + 1], ctx_ps[:, s, 0:w], AX_X, ALU.max, negate=True).then_inc(cmax_done if n else nmax_done, 1)
                    if n:
                        dve.tensor_tensor_reduce(sl[:, s, 0:n].rearrange("p (a c) -> p a c", a=2), loc_ps[:, :, 0:n // 2],
                                                 bias.rearrange("p (a c) -> p a c", a=2), 1.0, 2 * MASKED,
                                                 ALU.add, ALU.max, lmax[:, s:s + 1]).then_inc(smax_done, 1)
                        dve.wait_ge(smax_done, h * (EDGES + INNER) + pos + 1)
                        dve.scalar_tensor_tensor(nmx[:, s:s + 1], lmax[:, s:s + 1], -1.0, ncmax[:, s:s + 1],
                                                 ALU.mult, ALU.min).then_inc(nmax_done, 1)

                def low_part(tile):
                    h, parity, pos = tile
                    s, inner = pos % 2, EDGES <= pos < EDGES + INNER
                    u = h * TILES + pos
                    n = kind(pos)[1]
                    if n:
                        dve.wait_ge(hi_a, h * (EDGES + INNER) + pos + 1)
                        dve.tensor_tensor(pl[:, s, 0:4, :], ta_ps[:, :, :], ph[:, s, 0:4, :], ALU.subtract).then_inc(lo_a, 1)
                    dve.wait_ge(hi_b, u + 1)
                    if inner:
                        dve.tensor_tensor(pl[0:GRID, s, 8, :], th_ps[0:GRID, 0:P], ph[0:GRID, s, 8, :], ALU.subtract)
                    b = 4 if n else 2
                    dve.tensor_tensor(pl[:, s, 4:4 + b, :], tb_ps[:, 0:b, :], ph[:, s, 4:4 + b, :], ALU.subtract).then_inc(lo_done, 1)

                def finish(tile):
                    h, parity, pos = tile
                    s, inner = pos % 2, EDGES <= pos < EDGES + INNER
                    u = h * TILES + pos
                    dve.wait_ge(pv_done, u + 3)
                    dve.tensor_reduce(osum[:, s, :], o_ps[:, s, 0:3 * HD].rearrange("p (n d) -> p d n", n=3), AX_X, ALU.add).then_inc(o_read, 1)

                def step(before, tile, after):
                    if after is not None:
                        row_max(after)
                    low_part(tile)
                    if before is not None:
                        finish(before)

                row_max((0, 0, 0))
                every_tile(dve, step)
                dve.wait_ge(out_done, HEADS * TILES - 2)
                finish((HEADS - 1, 1, TILES - 1))

            @block.scalar
            def _(act):
                act.sem_inc(exp_done, 2)
                act.wait_ge(consts_loaded, 48)

                def exps(tile):
                    h, parity, pos = tile
                    s, inner = pos % 2, EDGES <= pos < EDGES + INNER
                    u = h * TILES + pos
                    n = kind(pos)[1]
                    act.wait_ge(nmax_done, u + 1)
                    nmax = (nmx if n else ncmax)[:, s:s + 1]
                    if n:
                        act.activation(prob[:, s, 0:n], sl[:, s, 0:n], ACT.Exp, bias=nmax,
                                       accum_out=sums[:, pos % 3, 0:1]).then_inc(exp_local_done, 1)
                    w = T_PAST if n else T_CTX
                    act.activation(prob[:, s, n:n + w], ctx_ps[:, s, 0:w], ACT.Exp, bias=nmax,
                                   accum_out=sums[:, pos % 3, 1:2]).then_inc(exp_done, 1)

                def high_part(tile):
                    h, parity, pos = tile
                    s, inner = pos % 2, EDGES <= pos < EDGES + INNER
                    u = h * TILES + pos
                    n = kind(pos)[1]
                    act.wait_ge(pv_done, u + 1)
                    if n:
                        act.wait_ge(ta_done, h * (EDGES + INNER) + pos + 1)
                        act.copy(ph[:, s, 0:4, :], ta_ps[:, :, :]).then_inc(hi_a, 1)
                    act.wait_ge(tb_done, u + 1)
                    if inner:
                        act.copy(ph[0:GRID, s, 8, :], th_ps[0:GRID, 0:P])
                    b = 4 if n else 2
                    act.copy(ph[:, s, 4:4 + b, :], tb_ps[:, 0:b, :]).then_inc(hi_b, 1)

                def divide(tile):
                    h, parity, pos = tile
                    s, u = pos % 2, h * TILES + pos
                    if pos == 0:
                        act.wait_ge(stored[parity], (h - parity) * 8 + 16)
                    act.wait_ge(rden_done, u + 1)
                    act.wait_ge(o_read, u + 3)
                    act.activation(out[:, parity, kind(pos)[2] // P, :], osum[:, s, :], ACT.Copy,
                                   scale=rden[:, pos % 3:pos % 3 + 1]).then_inc(out_done, 1)

                def two_before(tile):
                    h, parity, pos = tile
                    if pos >= 2:
                        return h, parity, pos - 2
                    return None if isinstance(h, int) and h == 0 else (h - 1, 1 - parity, TILES - 2 + pos)

                def step(before, tile, after):
                    exps(tile)
                    high_part(tile)
                    if two_before(tile) is not None:
                        divide(two_before(tile))

                every_tile(act, step)
                for pos in (TILES - 2, TILES - 1):
                    divide((HEADS - 1, 1, pos))


def mix_phase(nc, y, x_all, w_out, ln1_g, ln1_b, mod, ident_in, x1, h2_t):
    N = T_ALL // P
    N_LAT = T_LAT // P
    HALVES = D // 512
    with ExitStack() as ctx:
        sb, ps, sem = phase_tools(nc, ctx)
        w = [sb(f"mx_w{h}", [P, KT, D], F32R) for h in (HI, LO)]
        stage = sb("mx_w_stage", [P, 2, D])
        yb = sb("mx_y", [P, 2, D])
        xb = sb("mx_x", [P, 2, D])
        yt = [sb(f"mx_yt{h}", [P, 2, KT, P], F32R) for h in (HI, LO)]
        res = sb("mx_res", [P, 2, D])
        x1b = sb("mx_x1", [P, 2, D])
        xn = sb("mx_xn", [P, 2, D])
        hst = sb("mx_h_stage", [P, 2, KT, P])
        gate = sb("mx_gate", [P, 2, D])
        ln_g = sb("mx_ln_g", [P, D])
        ln_b = sb("mx_ln_b", [P, D])
        shift = sb("mx_shift", [P, 2, KT])
        scale = sb("mx_scale", [P, 2, KT])
        scale1p = sb("mx_scale1p", [P, 2, KT])
        ident = sb("mx_ident", [P, P])
        stats = sb("mx_stats", [P, 2, 12])
        mv = sb("mx_mv", [P, 2, 2])
        veps = sb("mx_veps", [P, 2])
        rstd = sb("mx_rstd", [P, 2])
        waited = sb("mx_waited", [P, 2])
        minus_half = sb("mx_minus_half", [P, 1])
        eps = sb("mx_eps", [P, 1])
        acc = ps("mx_acc", [P, 2, D])
        yps = ps("mx_yps", [P, KT, P])
        hps = ps("mx_hps", [P, KT, P])

        consts_loaded, half_done, scale_done = sem("mx_consts_loaded"), sem("mx_half_done"), sem("mx_scale_done")
        w_staged = [sem(f"mx_w_staged{s}") for s in range(2)]
        w_hi, w_lo = sem("mx_w_hi"), sem("mx_w_lo")
        y_loaded = [sem(f"mx_y_loaded{s}") for s in range(2)]
        x_loaded = [sem(f"mx_x_loaded{s}") for s in range(2)]
        y_turned, y_hi, y_lo = sem("mx_y_turned"), sem("mx_y_hi"), sem("mx_y_lo")
        acc_done, gated, res_done = sem("mx_acc_done"), sem("mx_gated"), sem("mx_res_done")
        stats_done = [sem(f"mx_stats_done{n}") for n in range(2)]
        mv_done = [sem(f"mx_mv_done{n}") for n in range(2)]
        veps_done = [sem(f"mx_veps_done{n}") for n in range(2)]
        rstd_done = [sem(f"mx_rstd_done{n}") for n in range(2)]
        normed = [sem(f"mx_normed{n}") for n in range(2)]
        scaled, x1_done, h_turned, h_done = sem("mx_scaled"), sem("mx_x1_done"), sem("mx_h_turned"), sem("mx_h_done")
        x1_stored = [sem(f"mx_x1_stored{s}") for s in range(2)]
        h_stored = [sem(f"mx_h_stored{s}") for s in range(2)]
        N_CONSTS = 9

        w_tiles = w_out.rearrange("l (k p) n -> (l k) p n", p=P)
        tiles = lambda ap: ap.rearrange("(t p) d -> t p d", p=P)
        y_tiles, x_tiles, x1_tiles = tiles(y), tiles(x_all), tiles(x1)
        h_tiles = h2_t.rearrange("(k p) t -> p k t", p=P)
        use = lambda t, s: (t - s) * 8

        def every_tile(body):
            def loop(eng):
                body(0, 0, LAT)
                body(1, 1, LAT)
                with eng.Fori(0, (N_LAT - 2) // 2) as i:
                    for s in range(2):
                        body(i * 2 + (2 + s), s, LAT)
                for t in range(N_LAT, N):
                    body(t, t % 2, CTX)
            return loop

        last_tile = lambda t: isinstance(t, int) and t == N - 1
        first = lambda t, n: isinstance(t, int) and t < n

        with nc.Block() as block:
            @block.sync
            def _(sp):
                for s in range(2):
                    sp.sem_inc(x1_stored[s], 16)
                sp.dma_start(ident[:, :], ident_in).then_inc(consts_loaded, 16)
                for k in range(KT):
                    sp.wait_ge(w_lo, k + 1)
                    sp.dma_start(stage[:, k % 2, :], w_tiles[k]).then_inc(w_staged[k % 2], 16)
                    if k < 2:
                        sp.dma_start(yb[:, k, :], y_tiles[k]).then_inc(y_loaded[k], 16)
                with nc.allow_non_contiguous_dma(reason="modulation, channel on partition"):
                    for v in range(2):
                        for dst, what in ((shift, SHIFT2), (scale, SCALE2)):
                            sp.dma_start(dst[:, v, :], mod[v, what * D:(what + 1) * D].rearrange("(k p) -> p k", p=P)).then_inc(consts_loaded, 16)
                        sp.dma_start(gate[:, v, :], mod[v, GATE1 * D:(GATE1 + 1) * D].partition_broadcast(P)).then_inc(consts_loaded, 16)
                sp.dma_start(ln_g[:, :], ln1_g[0].partition_broadcast(P)).then_inc(consts_loaded, 16)
                sp.dma_start(ln_b[:, :], ln1_b[0].partition_broadcast(P)).then_inc(consts_loaded, 16)
                for t in range(2):
                    sp.dma_start(xb[:, t, :], x_tiles[t]).then_inc(x_loaded[t], 16)

                def store_x1(t, s):
                    sp.wait_ge(x1_done, t + 1)
                    sp.dma_start(x1_tiles[t], x1b[:, s, :]).then_inc(x1_stored[s], 16)

                def tile(t, s, vec):
                    if not isinstance(t, int) or t + 2 < N:
                        sp.wait_ge(y_turned, t + 1)
                        sp.dma_start(yb[:, s, :], y_tiles[t + 2]).then_inc(y_loaded[s], 16)
                    if not first(t, 1):
                        store_x1(t - 1, 1 - s)
                    if not isinstance(t, int) or t + 2 < N:
                        sp.wait_ge(res_done, t + 1)
                        sp.dma_start(xb[:, s, :], x_tiles[t + 2]).then_inc(x_loaded[s], 16)

                every_tile(tile)(sp)
                store_x1(N - 1, 1)
                for s in range(2):
                    sp.wait_ge(x1_stored[s], 16 * (N // 2 + 1))
                    sp.wait_ge(h_stored[s], 16 * (N // 2 + 1))

            @block.gpsimd
            def _(pool):
                pool.memset(minus_half[:, :], -0.5).then_inc(half_done, 1)
                pool.memset(eps[:, :], EPS).then_inc(half_done, 1)
                pool.wait_ge(half_done, 2)
                pool.wait_ge(consts_loaded, 16 * N_CONSTS)

                def make_rstd(t, n):
                    pool.wait_ge(mv_done[n], t + 1)
                    pool.tensor_tensor(veps[:, n:n + 1], mv[:, n, 1:2], eps[:, :], ALU.add).then_inc(veps_done[n], 1)
                    pool.wait_ge(veps_done[n], t + 1)
                    pool.tensor_tensor(rstd[:, n:n + 1], veps[:, n:n + 1], minus_half[:, :], ALU.pow).then_inc(rstd_done[n], 1)

                def affine(t, s):
                    pool.wait_ge(normed[0], t + 1)
                    pool.tensor_tensor(res[:, s, :], res[:, s, :], ln_g[:, :], ALU.mult).then_inc(scaled, 1)
                    pool.wait_ge(scaled, t + 1)
                    pool.wait_ge(x1_stored[s], use(t, s) + 16)
                    if not first(t, 2):
                        pool.wait_ge(normed[1], t - 1)
                    pool.tensor_tensor(x1b[:, s, :], res[:, s, :], ln_b[:, :], ALU.add).then_inc(x1_done, 1)

                def tile(t, s, vec):
                    make_rstd(t, 0)
                    if not first(t, 1):
                        make_rstd(t - 1, 1)
                    affine(t, s)

                every_tile(tile)(pool)
                make_rstd(N - 1, 1)

            @block.tensor
            def _(pe):
                pe.sem_inc(gated, 2)
                pe.wait_ge(consts_loaded, 16)

                def turn_y(t, s):
                    pe.wait_ge(y_loaded[s], use(t, s) + 16)
                    if not first(t, 1):
                        pe.wait_ge(y_lo, t)
                    for k in range(KT):
                        mm = pe.transpose(yps[:, k, :], yb[:, s, k * P:(k + 1) * P], ident[:, :])
                    mm.then_inc(y_turned, 1)

                def product(t, s):
                    pe.wait_ge(y_lo, t + 1)
                    pe.wait_ge(gated, t + 1)
                    for half in range(HALVES):
                        for k in range(KT):
                            if first(t, 1) and half == 0:
                                pe.wait_ge(w_lo, k + 3)
                            for a, b in PASSES:
                                mm = pe.matmul(acc[:, s, half * 512:(half + 1) * 512], yt[a][:, s, k, :],
                                               w[b][:, k, half * 512:(half + 1) * 512],
                                               start=(k, a, b) == (0, HI, HI), stop=(k, a, b) == (KT - 1, LO, HI))
                    mm.then_inc(acc_done, 1)

                def turn_h(t, s):
                    pe.wait_ge(normed[1], t + 1)
                    if not first(t, 1):
                        pe.wait_ge(h_done, t)
                    for k in range(KT):
                        mm = pe.transpose(hps[:, k, :], xn[:, s, k * P:(k + 1) * P], ident[:, :])
                    mm.then_inc(h_turned, 1)

                def tile(t, s, vec):
                    if not last_tile(t):
                        turn_y(t + 1, 1 - s)
                    product(t, s)
                    if not first(t, 2):
                        turn_h(t - 2, s)

                turn_y(0, 0)
                every_tile(tile)(pe)
                turn_h(N - 2, 0)
                turn_h(N - 1, 1)

            @block.scalar
            def _(act):
                for s in range(2):
                    act.sem_inc(h_stored[s], 16)
                for k in range(KT):
                    act.wait_ge(w_staged[k % 2], k // 2 * 16 + 16)
                    act.copy(w[HI][:, k, :], stage[:, k % 2, :]).then_inc(w_hi, 1)
                    if k == 1:
                        act.wait_ge(y_turned, 1)
                        act.copy(yt[HI][:, 0, :, :], yps[:, :, :]).then_inc(y_hi, 1)

                def round_y(t, s):
                    act.wait_ge(y_turned, t + 1)
                    if not first(t, 2):
                        act.wait_ge(acc_done, t - 1)
                    act.copy(yt[HI][:, s, :, :], yps[:, :, :]).then_inc(y_hi, 1)

                def modulate(t, s, vec):
                    act.wait_ge(h_turned, t + 1)
                    act.wait_ge(h_stored[s], use(t, s) + 16)
                    for k in range(KT):
                        last = act.activation(hst[:, s, k, :], hps[:, k, :], ACT.Identity,
                                              bias=shift[:, vec, k:k + 1], scale=scale1p[:, vec, k:k + 1])
                    last.then_inc(h_done, 1)
                    act.wait_ge(h_done, t + 1)
                    act.dma_start(h_tiles[:, :, bass.ds(t * P, P)], hst[:, s, :, :]).then_inc(h_stored[s], 16)

                def tile(t, s, vec):
                    if not last_tile(t):
                        round_y(t + 1, 1 - s)
                    if not first(t, 2):
                        modulate(t - 2, s, LAT)

                act.wait_ge(scale_done, 1)
                every_tile(tile)(act)
                modulate(N - 2, 0, CTX)
                modulate(N - 1, 1, CTX)

            @block.vector
            def _(dve):
                dve.sem_inc(w_lo, 2)

                def low_y(t, s):
                    dve.wait_ge(y_hi, t + 1)
                    dve.tensor_tensor(yt[LO][:, s, :, :], yps[:, :, :], yt[HI][:, s, :, :].bitcast(F32), ALU.subtract).then_inc(y_lo, 1)

                for k in range(KT):
                    dve.wait_ge(w_hi, k + 1)
                    dve.tensor_tensor(w[LO][:, k, :], stage[:, k % 2, :], w[HI][:, k, :].bitcast(F32), ALU.subtract).then_inc(w_lo, 1)
                    if k == 1:
                        low_y(0, 0)
                dve.wait_ge(consts_loaded, 16 * N_CONSTS)
                dve.tensor_scalar(scale1p[:, :, :], scale[:, :, :], 1.0, None, ALU.add).then_inc(scale_done, 1)

                def statistics(t, n, src):
                    for half in range(HALVES):
                        last = dve.bn_stats(stats[:, n, half * 6:half * 6 + 6], src[:, half * 512:(half + 1) * 512])
                    last.then_inc(stats_done[n], 1)
                    dve.wait_ge(stats_done[n], t + 1)
                    dve.tensor_copy(waited[:, n:n + 1], stats[:, n, 0:1])
                    dve.bn_aggr(mv[:, n, :], stats[:, n, :]).then_inc(mv_done[n], 1)

                def norm(t, n, dst, src):
                    dve.wait_ge(rstd_done[n], t + 1)
                    dve.tensor_scalar(dst, src, mv[:, n, 0:1], rstd[:, n:n + 1], ALU.subtract, ALU.mult).then_inc(normed[n], 1)

                def second_statistics(t, s):
                    dve.wait_ge(x1_done, t + 1)
                    statistics(t, 1, x1b[:, s, :])

                def second_norm(t, s):
                    if not first(t, 2):
                        dve.wait_ge(h_turned, t - 1)
                    norm(t, 1, xn[:, s, :], x1b[:, s, :])

                def tile(t, s, vec):
                    if not last_tile(t):
                        low_y(t + 1, 1 - s)
                    dve.wait_ge(acc_done, t + 1)
                    if not first(t, 2):
                        dve.wait_ge(x1_done, t - 1)
                    dve.tensor_tensor(res[:, s, :], acc[:, s, :], gate[:, vec, :], ALU.mult).then_inc(gated, 1)
                    dve.wait_ge(gated, t + 3)
                    dve.wait_ge(x_loaded[s], use(t, s) + 16)
                    dve.scalar_tensor_tensor(res[:, s, :], xb[:, s, :], ALPHA, res[:, s, :], ALU.mult, ALU.add).then_inc(res_done, 1)
                    dve.wait_ge(res_done, t + 1)
                    statistics(t, 0, res[:, s, :])
                    if not first(t, 1):
                        second_statistics(t - 1, 1 - s)
                    norm(t, 0, res[:, s, :], res[:, s, :])
                    if not first(t, 1):
                        second_norm(t - 1, 1 - s)

                every_tile(tile)(dve)
                second_statistics(N - 1, 1)
                second_norm(N - 1, 1)


def ffn_up_phase(nc, h2_t, w_gu, conv_w, conv_b, f_t):
    CHUNKS = [(c * 512, 512) for c in range(T_LAT // 512)] + [(T_LAT, T_CTX)]
    NC = len(CHUNKS)
    PIECE = 256
    H_PIECES = T_ALL // PIECE
    G_LEN = T_ALL + 4
    G_AT = [1 + at for at, _ in CHUNKS[:-1]] + [T_LAT + 3]
    ZEROS = (0, T_LAT + 1, T_LAT + 2, G_LEN - 1)
    BANK = (0, 1, 2, 3, 0)
    SLOT = (0, 1, 2, 0, 1)
    with ExitStack() as ctx:
        sb, ps, sem = phase_tools(nc, ctx)
        ht = [sb(f"fu_ht{h}", [P, KT, T_ALL], F32R) for h in (HI, LO)]
        w = [sb(f"fu_w{h}", [P, 2, KT, PIECE], F32R) for h in (HI, LO)]
        stage = sb("fu_stage", [P, 2, KT, PIECE])
        grow = sb("fu_g", [P, G_LEN])
        res = sb("fu_result", [P, 3, 512])
        cw = sb("fu_conv_w", [P, 3, FT])
        cb = sb("fu_conv_b", [P, FT])
        gps = ps("fu_gps", [P, 4, 512])
        ups = ps("fu_ups", [P, 4, 512])

        consts_loaded, zeroed = sem("fu_consts_loaded"), sem("fu_zeroed")
        staged = [sem(f"fu_staged{s}") for s in range(2)]
        part_hi, part_lo = sem("fu_part_hi"), sem("fu_part_lo")
        g_done, u_done, g_read, u_read = sem("fu_g_done"), sem("fu_u_done"), sem("fu_g_read"), sem("fu_u_read")
        tap = [sem(f"fu_tap{n}") for n in range(3)]
        silu_done = sem("fu_silu_done")
        stored = [sem(f"fu_stored{s}") for s in range(3)]
        USES = [SLOT.count(s) for s in range(3)]

        def uses(f, c):
            return f * USES[SLOT[c]] + SLOT[:c].count(SLOT[c])

        w_cols = w_gu.rearrange("l (k p) (h f c) -> (l h f) p k c", p=P, h=2, c=P)
        h_tiles = h2_t.rearrange("(k p) t -> p k t", p=P)
        piece_of = lambda f: H_PIECES + f
        h_pieces = lambda c: 1 + (CHUNKS[c][0] + CHUNKS[c][1]) // PIECE

        def every_tile(eng, body):
            body(0, 0)
            with eng.Fori(0, (FT - 2) // 2) as i:
                for s in range(2):
                    body(i * 2 + (1 + s), 1 - s)
            body(FT - 1, 1)

        def chunk_order(do_g, do_u):
            do_g(0)
            for c in range(NC):
                if c + 1 < NC:
                    do_g(c + 1)
                do_u(c)

        is_first = lambda f: isinstance(f, int) and f == 0
        is_last = lambda f: isinstance(f, int) and f == FT - 1

        with nc.Block() as block:
            @block.sync
            def _(sp):
                for s in range(3):
                    sp.sem_inc(stored[s], 16)

                def load_w(f, slot):
                    for h in range(2):
                        sp.dma_start(stage[:, slot, :, h * P:(h + 1) * P], w_cols[h * FT + f]).then_inc(staged[slot], 16)

                load_w(0, 0)
                for n in range(H_PIECES):
                    slot = (n + 1) % 2
                    if n:
                        sp.wait_ge(part_lo, n)
                    for h in range(2):
                        ks = slice(h * KT // 2, (h + 1) * KT // 2)
                        sp.dma_start(stage[:, slot, ks, :], h_tiles[:, ks, n * PIECE:(n + 1) * PIECE]).then_inc(staged[slot], 16)
                    if n == 1:
                        with nc.allow_non_contiguous_dma(reason="convolution weights, channel on partition"):
                            for tp in range(3):
                                sp.dma_start(cw[:, tp, :], conv_w[0, tp].rearrange("(f p) -> p f", p=P)).then_inc(consts_loaded, 16)
                            sp.dma_start(cb[:, :], conv_b[0].rearrange("(f p) -> p f", p=P)).then_inc(consts_loaded, 16)
                sp.wait_ge(part_lo, H_PIECES)
                load_w(1, (H_PIECES + 1) % 2)

                def tile(f, s):
                    for c, (at, n) in enumerate(CHUNKS):
                        sp.wait_ge(u_read, f * NC + c + 1)
                        sp.dma_start(f_t[bass.ds(f * P, P), at:at + n], res[:, SLOT[c], 0:n]).then_inc(stored[SLOT[c]], 16)
                        if c == 1 and not (isinstance(f, int) and f >= FT - 2):
                            sp.wait_ge(part_lo, f + (H_PIECES + 1))
                            load_w(f + 2, (H_PIECES + s) % 2)

                tile(0, 0)
                with sp.Fori(0, (FT - 4) // 2) as i:
                    for s in range(2):
                        tile(i * 2 + (1 + s), 1 - s)
                tile(FT - 3, 1)
                tile(FT - 2, 0)
                tile(FT - 1, 1)
                for s in range(3):
                    sp.wait_ge(stored[s], 16 * (FT * USES[s] + 1))

            @block.gpsimd
            def _(pool):
                for at in ZEROS:
                    pool.memset(grow[:, at:at + 1], 0.0).then_inc(zeroed, 1)

            @block.tensor
            def _(pe):
                def tile(f, s):
                    pe.wait_ge(part_lo, 1 if is_first(f) else f + (H_PIECES + 1))

                    def product(out, half, c):
                        at, n = CHUNKS[c]
                        for k in range(KT):
                            for a, b in PASSES:
                                mm = pe.matmul(out[:, BANK[c], 0:n], w[a][:, s, k, half * P:(half + 1) * P],
                                               ht[b][:, k, at:at + n],
                                               start=(k, a, b) == (0, HI, HI), stop=(k, a, b) == (KT - 1, LO, HI))
                        return mm

                    def g(c):
                        if is_first(f):
                            pe.wait_ge(part_lo, h_pieces(c))
                        if not (is_first(f) and c < 4):
                            pe.wait_ge(g_read, (f * NC + 1) if c == 4 else ((f - 1) * NC + (5 if c == 0 else c + 1)))
                        product(gps, 0, c).then_inc(g_done, 1)

                    def u(c):
                        if not (is_first(f) and c < 4):
                            pe.wait_ge(u_read, (f * NC + 1) if c == 4 else ((f - 1) * NC + (5 if c == 0 else c + 1)))
                        product(ups, 1, c).then_inc(u_done, 1)

                    chunk_order(g, u)

                every_tile(pe, tile)

            @block.scalar
            def _(act):
                def high(n, slot, dst):
                    act.wait_ge(staged[slot], (n - slot) * 16 + 32)
                    act.copy(dst, stage[:, slot, :, :]).then_inc(part_hi, 1)

                high(0, 0, w[HI][:, 0, :, :])
                for n in range(H_PIECES):
                    high(n + 1, (n + 1) % 2, ht[HI][:, :, n * PIECE:(n + 1) * PIECE])
                act.wait_ge(zeroed, len(ZEROS))

                def tile(f, s):
                    def g(c):
                        act.wait_ge(g_done, f * NC + c + 1)
                        if not is_first(f):
                            act.wait_ge(tap[2], (f - 1) * NC + min(c + 2, NC))
                        act.copy(grow[:, G_AT[c]:G_AT[c] + CHUNKS[c][1]], gps[:, BANK[c], 0:CHUNKS[c][1]]).then_inc(g_read, 1)

                    def u(c):
                        act.wait_ge(tap[2], f * NC + c + 1)
                        part = res[:, SLOT[c], 0:CHUNKS[c][1]]
                        act.activation(part, part, ACT.Silu).then_inc(silu_done, 1)
                        if c == 0 and not is_last(f):
                            if not is_first(f):
                                act.wait_ge(u_done, f * NC)
                            high(piece_of(1) + f, (H_PIECES + 1 + s) % 2, w[HI][:, 1 - s, :, :])

                    chunk_order(g, u)

                every_tile(act, tile)

            @block.vector
            def _(dve):
                def low(n, slot, dst, hi):
                    dve.wait_ge(part_hi, n + 1)
                    dve.tensor_tensor(dst, stage[:, slot, :, :], hi.bitcast(F32), ALU.subtract).then_inc(part_lo, 1)

                low(0, 0, w[LO][:, 0, :, :], w[HI][:, 0, :, :])
                for n in range(H_PIECES):
                    at = slice(n * PIECE, (n + 1) * PIECE)
                    low(n + 1, (n + 1) % 2, ht[LO][:, :, at], ht[HI][:, :, at])
                dve.wait_ge(consts_loaded, 64)
                dve.wait_ge(zeroed, len(ZEROS))

                def tile(f, s):
                    par = lambda ap: ap[:, bass.ds(f, 1)]

                    def conv(c):
                        u0 = f * NC + c + 1
                        n = CHUNKS[c][1]
                        dve.wait_ge(g_read, f * NC + (c + 2 if c < NC - 2 else c + 1))
                        dve.wait_ge(stored[SLOT[c]], (uses(f, c) + 1) * 16)
                        out = res[:, SLOT[c], 0:n]
                        src = lambda tp: grow[:, G_AT[c] + tp - 1:G_AT[c] + tp - 1 + n]
                        dve.tensor_scalar(out, src(0), par(cw[:, 0]), par(cb[:, :]), ALU.mult, ALU.add).then_inc(tap[0], 1)
                        for tp in (1, 2):
                            dve.wait_ge(tap[tp - 1], u0)
                            dve.scalar_tensor_tensor(out, src(tp), par(cw[:, tp]), out, ALU.mult, ALU.add).then_inc(tap[tp], 1)

                    def gate(c):
                        n = CHUNKS[c][1]
                        dve.wait_ge(u_done, f * NC + c + 1)
                        dve.wait_ge(silu_done, f * NC + c + 1)
                        out = res[:, SLOT[c], 0:n]
                        dve.tensor_tensor(out, out, ups[:, BANK[c], 0:n], ALU.mult).then_inc(u_read, 1)
                        if c == 0 and not is_last(f):
                            low(piece_of(1) + f, (H_PIECES + 1 + s) % 2, w[LO][:, 1 - s, :, :], w[HI][:, 1 - s, :, :])

                    conv(0)
                    for c in range(NC):
                        if c + 1 < NC:
                            conv(c + 1)
                        gate(c)

                every_tile(dve, tile)


def ffn_down_phase(nc, f_t, w_down, x1, ln2_g, ln2_b, mod, out_all):
    GT = 4
    GROUPS_LAT = T_LAT // (GT * P)
    CT = T_CTX // P
    TAILS = GT
    KEPT = 14
    assert KEPT % 2 == 0 and KEPT // 2 > TAILS
    with ExitStack() as ctx:
        sb, ps, sem = phase_tools(nc, ctx)
        fst = sb("fd_f_stage", [P, 2, GT * P])
        wst = sb("fd_w_stage", [P, 2, D])
        f = [sb(f"fd_f{h}", [P, 2, GT * P], F32R) for h in (HI, LO)]
        w = [sb(f"fd_w{h}", [P, KEPT + 2, D], F32R) for h in (HI, LO)]
        x = sb("fd_x1", [P, GT, D])
        res = sb("fd_res", [P, GT, D])
        out = sb("fd_out", [P, 2, D])
        gate = sb("fd_gate", [P, 2, D])
        ln_g = sb("fd_ln_g", [P, D])
        ln_b = sb("fd_ln_b", [P, D])
        stats = sb("fd_stats", [P, 12])
        mv = sb("fd_mv", [P, 2])
        veps = sb("fd_veps", [P, 1])
        rstd = sb("fd_rstd", [P, 1])
        waited = sb("fd_waited", [P, 1])
        minus_half = sb("fd_minus_half", [P, 1])
        eps = sb("fd_eps", [P, 1])
        acc = ps("fd_acc", [P, GT, D])

        consts_loaded, half_done = sem("fd_consts_loaded"), sem("fd_half_done")
        f_staged = [sem(f"fd_f_staged{s}") for s in range(2)]
        w_staged = [sem(f"fd_w_staged{s}") for s in range(2)]
        f_hi, f_lo, w_hi, w_lo = sem("fd_f_hi"), sem("fd_f_lo"), sem("fd_w_hi"), sem("fd_w_lo")
        step_done, acc_done, gated = sem("fd_step_done"), sem("fd_acc_done"), sem("fd_gated")
        x_loaded, res_done, stats_done, mv_done = sem("fd_x_loaded"), sem("fd_res_done"), sem("fd_stats_done"), sem("fd_mv_done")
        veps_done, rstd_done, normed, scaled, out_done = (
            sem("fd_veps_done"), sem("fd_rstd_done"), sem("fd_normed"), sem("fd_scaled"), sem("fd_out_done"))
        stored = [sem(f"fd_stored{s}") for s in range(2)]
        f_tiles = f_t.rearrange("(f p) t -> f p t", p=P)
        w_tiles = w_down.rearrange("l (f p) n -> (l f) p n", p=P)
        x_groups = x1[0:T_LAT, :].rearrange("(g t p) d -> g p t d", p=P, t=GT)
        x_ctx = x1[T_LAT:T_ALL, :].rearrange("(t p) d -> p t d", p=P)
        out_tiles = out_all.rearrange("(t p) d -> t p d", p=P)

        def every_step(eng, body, tail, store=lambda *a: None):
            def group(g, tiles, after_first):
                for t in range(KEPT // 2):
                    for s in range(2):
                        body(g, 2 * t + s, s, tiles)
                        if after_first and t < TAILS:
                            tail(g - 1, t, LAT, s)
                    if after_first and 1 <= t <= TAILS:
                        store(g - 1, t - 1)
                with eng.Fori(KEPT // 2, FT // 2 - 1) as i:
                    for s in range(2):
                        body(g, i * 2 + s, s, tiles)
                for s in range(2):
                    body(g, FT - 2 + s, s, tiles)

            group(0, GT, False)
            with eng.Fori(1, GROUPS_LAT) as g:
                group(g, GT, True)
            group(GROUPS_LAT, CT, True)
            for t in range(CT):
                for half in range(2):
                    tail(GROUPS_LAT, t, CTX, half)
                store(GROUPS_LAT, t)

        number = lambda g, t: g * GT + t
        kept = lambda st: isinstance(st, int) and st < KEPT
        loads_w = lambda g, st: is_first(g) or not kept(st)

        def pieces(g, st):
            return g * (FT - KEPT) + st

        def w_at(st, slot):
            return st if kept(st) else KEPT + slot

        is_step = lambda st, n: isinstance(st, int) and st == n
        is_first = lambda g: isinstance(g, int) and g == 0
        is_ctx = lambda g: isinstance(g, int) and g == GROUPS_LAT

        with nc.Block() as block:
            @block.sync
            def _(sp):
                for s in range(2):
                    sp.sem_inc(stored[s], 16)

                def load(g, st, slot, tiles):
                    n = tiles * P
                    if not (is_first(g) and isinstance(st, int) and st < 2):
                        sp.wait_ge(f_lo, g * FT + st - 1)
                    sp.dma_start(fst[:, slot, 0:n], f_tiles[st][:, bass.ds(g * (GT * P), n)]).then_inc(f_staged[slot], 16)
                    if loads_w(g, st):
                        if not (is_first(g) and isinstance(st, int) and st < 2):
                            sp.wait_ge(w_lo, pieces(g, st) - 1)
                        sp.dma_start(wst[:, slot, :], w_tiles[st]).then_inc(w_staged[slot], 16)
                    if is_first(g) and is_step(st, 1):
                        for v in range(2):
                            sp.dma_start(gate[:, v, :], mod[v, GATE2 * D:(GATE2 + 1) * D].partition_broadcast(P)).then_inc(consts_loaded, 16)
                        sp.dma_start(ln_g[:, :], ln2_g[0].partition_broadcast(P)).then_inc(consts_loaded, 16)
                        sp.dma_start(ln_b[:, :], ln2_b[0].partition_broadcast(P)).then_inc(consts_loaded, 16)
                    if is_step(st, FT - 2):
                        if not is_first(g):
                            sp.wait_ge(res_done, g * GT)
                        sp.dma_start(x[:, 0:tiles, :], x_ctx if is_ctx(g) else x_groups[g]).then_inc(x_loaded, 16)

                def store(g, t):
                    sp.wait_ge(out_done, number(g, t) + 1)
                    sp.dma_start(out_tiles[number(g, t)], out[:, t % 2, :]).then_inc(stored[t % 2], 16)

                every_step(sp, load, lambda *a: None, store)
                for s in range(2):
                    sp.wait_ge(stored[s], 16 * ((GROUPS_LAT * GT + CT) // 2 + 1))

            @block.scalar
            def _(act):
                def high(g, st, slot, tiles):
                    n = tiles * P
                    act.wait_ge(f_staged[slot], (g * FT + st - slot) * 8 + 16)
                    if not (is_first(g) and isinstance(st, int) and st < 2):
                        act.wait_ge(step_done, g * FT + st - 1)
                    act.copy(f[HI][:, slot, 0:n], fst[:, slot, 0:n]).then_inc(f_hi, 1)
                    if loads_w(g, st):
                        act.wait_ge(w_staged[slot], (pieces(g, st) - slot) * 8 + 16)
                        act.copy(w[HI][:, w_at(st, slot), :], wst[:, slot, :]).then_inc(w_hi, 1)

                every_step(act, high, lambda *a: None)

            @block.tensor
            def _(pe):
                def step(g, st, slot, tiles):
                    pe.wait_ge(f_lo, g * FT + st + 1)
                    if loads_w(g, st):
                        pe.wait_ge(w_lo, pieces(g, st) + 1)
                    last = is_step(st, FT - 1)
                    for t in range(tiles):
                        if is_step(st, 0) and not is_first(g):
                            pe.wait_ge(gated, number(g - 1, t) + 1)
                        for half in range(2):
                            at = slice(half * 512, (half + 1) * 512)
                            for a, b in PASSES:
                                mm = pe.matmul(acc[:, t, at], f[a][:, slot, t * P:(t + 1) * P], w[b][:, w_at(st, slot), at],
                                               start=is_step(st, 0) and (a, b) == (HI, HI), stop=last and (a, b) == (LO, HI))
                        if last and t < tiles - 1:
                            mm.then_inc(acc_done, 1)
                    mm.then_inc(step_done, 1)

                every_step(pe, step, lambda *a: None)

            @block.vector
            def _(dve):
                def gate_sums(g, tiles, vec):
                    for t in range(tiles):
                        if t < tiles - 1:
                            dve.wait_ge(acc_done, g * (GT - 1) + t + 1)
                        else:
                            dve.wait_ge(step_done, (g + 1) * FT)
                        dve.wait_ge(scaled, number(g, t) + 1)
                        dve.tensor_tensor(res[:, t, :], acc[:, t, :], gate[:, vec, :], ALU.mult).then_inc(gated, 1)

                def low(g, st, slot, tiles):
                    n = tiles * P
                    dve.wait_ge(f_hi, g * FT + st + 1)
                    dve.tensor_tensor(f[LO][:, slot, 0:n], fst[:, slot, 0:n], f[HI][:, slot, 0:n].bitcast(F32), ALU.subtract).then_inc(f_lo, 1)
                    if loads_w(g, st):
                        dve.wait_ge(w_hi, pieces(g, st) + 1)
                        at = w_at(st, slot)
                        dve.tensor_tensor(w[LO][:, at, :], wst[:, slot, :], w[HI][:, at, :].bitcast(F32), ALU.subtract).then_inc(w_lo, 1)
                    if is_step(st, 0) and not is_first(g):
                        gate_sums(g - 1, GT, LAT)
                    if is_ctx(g) and is_step(st, FT - 1):
                        gate_sums(g, CT, CTX)

                def tail(g, t, vec, half):
                    n = number(g, t)
                    if half == 0:
                        if t == 0:
                            dve.wait_ge(x_loaded, g * 16 + 16)
                        dve.wait_ge(gated, n + 1)
                        dve.scalar_tensor_tensor(res[:, t, :], x[:, t, :], ALPHA, res[:, t, :], ALU.mult, ALU.add).then_inc(res_done, 1)
                        dve.wait_ge(res_done, n + 1)
                        for h in range(2):
                            last = dve.bn_stats(stats[:, h * 6:h * 6 + 6], res[:, t, h * 512:(h + 1) * 512])
                        last.then_inc(stats_done, 1)
                        dve.wait_ge(stats_done, n + 1)
                        dve.tensor_copy(waited[:, :], stats[:, 0:1])
                        dve.bn_aggr(mv[:, :], stats[:, :]).then_inc(mv_done, 1)
                    else:
                        dve.wait_ge(rstd_done, n + 1)
                        dve.tensor_scalar(res[:, t, :], res[:, t, :], mv[:, 0:1], rstd[:, :], ALU.subtract, ALU.mult).then_inc(normed, 1)

                dve.wait_ge(consts_loaded, 64)
                every_step(dve, low, tail)

            @block.gpsimd
            def _(pool):
                pool.memset(minus_half[:, :], -0.5).then_inc(half_done, 1)
                pool.memset(eps[:, :], EPS).then_inc(half_done, 1)
                pool.wait_ge(half_done, 2)
                pool.sem_inc(scaled, GT)
                pool.wait_ge(consts_loaded, 64)

                def affine(g, t):
                    n, slot = number(g, t), t % 2
                    pool.wait_ge(mv_done, n + 1)
                    pool.tensor_tensor(veps[:, :], mv[:, 1:2], eps[:, :], ALU.add).then_inc(veps_done, 1)
                    pool.wait_ge(veps_done, n + 1)
                    pool.tensor_tensor(rstd[:, :], veps[:, :], minus_half[:, :], ALU.pow).then_inc(rstd_done, 1)
                    pool.wait_ge(normed, n + 1)
                    pool.tensor_tensor(res[:, t, :], res[:, t, :], ln_g[:, :], ALU.mult).then_inc(scaled, 1)
                    pool.wait_ge(scaled, n + GT + 1)
                    pool.wait_ge(stored[slot], (n - slot) * 8 + 16)
                    pool.tensor_tensor(out[:, slot, :], res[:, t, :], ln_b[:, :], ALU.add).then_inc(out_done, 1)

                with pool.Fori(0, GROUPS_LAT) as g:
                    for t in range(GT):
                        affine(g, t)
                for t in range(CT):
                    affine(GROUPS_LAT, t)


def shape_constants():
    import numpy as np

    def angles(rows, cols, n):
        return 2 * np.pi * (np.outer(rows, cols) % n) / n

    c64, s64 = np.zeros((P, P)), np.zeros((P, P))
    a = angles(np.arange(64), np.arange(64), 64)
    for h in (0, 64):
        c64[h:h + 64, h:h + 64] = np.cos(a) / 8
        s64[h:h + 64, h:h + 64] = -np.sin(a) / 8
    r = np.arange(512)
    a = angles(r, np.arange(4), T_LAT)
    twiddle = np.stack([np.cos(a), np.sin(a)], -1)
    a = angles(r, np.arange(512), 512)
    dft512 = np.stack([np.cos(a), np.sin(a)]) / np.sqrt(T_LAT)
    a = angles(np.arange(T_CTX), np.arange(T_CTX), T_CTX)
    dft256 = np.stack([np.cos(a), np.sin(a)]) / np.sqrt(T_CTX)
    col = np.arange(GRID)
    start = np.clip(col - 8, 0, GRID - 16)[:, None]
    col_mask = np.where((col >= start) & (col < start + 16), 0.0, MASKED)
    row_mask = np.zeros((2, GRID, 9, GRID))
    row_mask[0, :, 8] = MASKED
    row_mask[1, :, 0] = MASKED
    f = lambda v: np.ascontiguousarray(v, np.float32)
    return {"col_mask": f(np.tile(col_mask, (2, 1))), "row_mask": f(row_mask.reshape(P, 9 * GRID)), "ident": f(np.eye(P)), "dft_c64": f(c64), "dft_s64": f(s64), "twiddle": f(twiddle),
            "dft512": f(dft512), "dft256": f(dft256)}


def build_program(nc, x_all, conds, cache_k, cache_v, w_ada, b_ada, w_in, a_ws, a_bs, f_w, rpb, w_out, ln1_g, ln1_b,
                  w_gu, conv_w, conv_b, w_down, ln2_g, ln2_b,
                  ident, dft_c64, dft_s64, twiddle, dft512, dft256, col_mask, row_mask,
                  y_all, new_k, new_v):
    def scratch(name, shape, dt=F32):
        return nc.dram_tensor(name, shape, dt, kind="Internal").ap()

    mod = scratch("mod", [2, 6 * D])
    q_t = scratch("q_t", [2, D_C, T_ALL])
    k_t = scratch("k_t", [2, D_C, T_ALL + T_PAST])
    v_parts = scratch("v_parts", [T_ALL + T_PAST, 3 * D_C], BF16)
    chan_dft = scratch("chan_dft", [T_ALL, 2 * D_B])
    y = scratch("y_mixed", [T_ALL, D])
    rpb_pad = scratch("rpb_pad", [1, RPB_PAD + RPB + RPB_PAD])
    rel_bias = scratch("rel_bias", [GRID, HEADS * REL_ROWS, GRID])
    x1 = scratch("x1", [T_ALL, D])
    h2_t = scratch("h2_t", [D, T_ALL])
    f_t = scratch("f_t", [D_FF, T_ALL])

    with nc.cleanup_on_exit():
        rel_stored = modulation_phase(nc, conds, w_ada, b_ada, cache_k, cache_v, rpb, ident, mod, k_t, v_parts, rpb_pad, rel_bias)
        projection_phase(nc, x_all, w_in, a_ws, a_bs, f_w, ident, dft_c64, dft_s64,
                         mod, y, q_t, k_t, v_parts, chan_dft, new_k, new_v)
        fourier_phase(nc, chan_dft, twiddle, dft512, dft256, conds, w_ada, b_ada, mod, y)
        attention_phase(nc, q_t, k_t, v_parts, rel_bias, rel_stored, col_mask, row_mask, ident, y)
    mix_phase(nc, y, x_all, w_out, ln1_g, ln1_b, mod, ident, x1, h2_t)
    ffn_up_phase(nc, h2_t, w_gu, conv_w, conv_b, f_t)
    ffn_down_phase(nc, f_t, w_down, x1, ln2_g, ln2_b, mod, y_all)


WEIGHTS = ("cache_k", "cache_v", "w_ada", "b_ada", "w_in", "a_ws", "a_bs", "f_w", "rpb", "w_out", "ln1_g", "ln1_b",
           "w_gu", "conv_w", "conv_b", "w_down", "ln2_g", "ln2_b")
TABLES = ("ident", "dft_c64", "dft_s64", "twiddle", "dft512", "dft256", "col_mask", "row_mask")


def kernel(**inputs):
    import numpy as np
    import concourse.bacc as bacc
    from concourse.bass_utils import run_bass_kernel_spmd

    arrays = {"x_all": np.concatenate([inputs["x_sample"][0], inputs["x_prompt"][0]]),
              "conds": np.stack([inputs["c"][0], inputs["c_ctx"]])}
    arrays.update((name, np.ascontiguousarray(inputs[name])) for name in WEIGHTS)
    tables = shape_constants()
    arrays.update((name, tables[name]) for name in TABLES)
    outputs = {"y_all": (T_ALL, D), "new_k": (T_CTX, D_C), "new_v": (T_CTX, D_C)}

    nc = bacc.Bacc("TRN2", target_bir_lowering=False, num_devices=1)
    args = [nc.dram_tensor(f"in_{name}_dram", a.shape, mybir.dt.from_np(a.dtype), kind="ExternalInput").ap()
            for name, a in arrays.items()]
    args += [nc.dram_tensor(f"out_{name}_dram", shape, F32, kind="ExternalOutput").ap() for name, shape in outputs.items()]
    build_program(nc, *args)
    r = run_bass_kernel_spmd(nc, [{f"in_{name}_dram": a for name, a in arrays.items()}], core_ids=[0])
    y_all, new_k, new_v = (r.results[0][f"out_{name}_dram"] for name in outputs)
    cache_shape = (1, 1, T_CTX, HEADS, HD)
    return (y_all[T_LAT:].reshape(1, T_CTX, D), y_all[:T_LAT].reshape(1, T_LAT, D),
            new_k.reshape(cache_shape), new_v.reshape(cache_shape))
```

```python
from contextlib import ExitStack

import concourse.bass as bass
from concourse import mybir

F32 = mybir.dt.float32
F32R = mybir.dt.float32r
FP16 = mybir.dt.float16
BF16 = mybir.dt.bfloat16
ALU = mybir.AluOpType
ACT = mybir.ActivationFunctionType
AX_X = mybir.AxisListType.X

P = 128
D = 1024
KT = D // P
T_LAT, T_CTX, T_PAST = 2048, 256, 512
T_ALL = T_LAT + T_CTX
D_A, D_B, D_C = 256, 256, 512
HEADS, HD = 8, 64
A_HEADS = 4
GRID = 64
P_IN = 2 * D_A + D_B + 3 * D_C
COL_ZA, COL_ZB, COL_Q, COL_K, COL_V = 0, 512, 768, 1280, 1792
D_FF = 2816
REL_ROWS, REL_COLS = 15, 31
RPB = HEADS * REL_ROWS * REL_COLS
RPB_PAD = 64
MASKED = -1e30
FT = D_FF // P
ALPHA = 2.0 ** 0.25
EPS = 1e-6
HI, LO = 0, 1
ADA_COLS = 512
PASSES = ((HI, HI), (HI, LO), (LO, HI))
LAT, CTX = 0, 1
SHIFT1, SCALE1, GATE1, SHIFT2, SCALE2, GATE2 = range(6)


def phase_tools(nc, ctx):
    def sb(name, shape, dt=F32, side="left"):
        return ctx.enter_context(nc.sbuf_tensor(name, shape, dt, side=side))

    def ps(name, shape, dt=F32):
        return ctx.enter_context(nc.psum_tensor(name, shape, dt))

    def sem(name):
        return nc.alloc_semaphore(name)

    return sb, ps, sem


def ada_columns(w_ada):
    return w_ada.rearrange("l (k p) (n c) -> (l n) p k c", p=P, c=ADA_COLS)


def modulation_phase(nc, conds, w_ada, b_ada, w_in, rpb, mod, rpb_pad, w):
    with ExitStack() as ctx:
        sb, ps, sem = phase_tools(nc, ctx)
        N = 2 * D // ADA_COLS
        PIECES = 6
        WC = P_IN // PIECES
        wa = sb("ada_w", [P, 2, KT, ADA_COLS])
        cond = sb("ada_cond", [P, 2, KT])
        silu = sb("ada_silu", [P, KT, 2])
        bias = sb("ada_bias", [2, N, ADA_COLS])
        row = sb("ada_row", [2, N, ADA_COLS])
        zeros = sb("ada_zeros", [1, RPB_PAD])
        stage = sb("ada_w_in_stage", [P, PIECES, WC])
        acc = ps("ada_acc", [P, N, ADA_COLS])
        cond_loaded, bias_loaded, silu_done = sem("ada_cond_loaded"), sem("ada_bias_loaded"), sem("ada_silu_done")
        wa_loaded = [sem(f"ada_w_loaded{s}") for s in range(2)]
        acc_done, acc_read, stored = sem("ada_acc_done"), sem("ada_acc_read"), sem("ada_stored")
        zeroed, rpb_stored = sem("ada_zeroed"), sem("ada_rpb_stored")
        staged = [sem(f"ada_staged{n}") for n in range(PIECES)]
        w_hi, w_lo = sem("ada_w_in_hi"), sem("ada_w_in_lo")
        ada_cols = ada_columns(w_ada)
        w_tiles = w_in.rearrange("l (k p) n -> (l k) p n", p=P)

        with nc.Block() as block:
            @block.sync
            def _(sp):
                with nc.allow_non_contiguous_dma(reason="two conditioning vectors, channel on partition"):
                    for v in (LAT, CTX):
                        sp.dma_start(cond[:, v, :], conds[v].rearrange("(k p) -> p k", p=P)).then_inc(cond_loaded, 16)
                def load_w_in(k):
                    for n in range(PIECES):
                        sp.wait_ge(w_lo, k * PIECES + n + 1)
                        sp.dma_start(stage[:, n, :], w_tiles[k][:, n * WC:(n + 1) * WC]).then_inc(staged[n], 16)

                for n in range(N):
                    if n >= 2:
                        sp.wait_ge(acc_done, n - 1)
                    sp.dma_start(wa[:, n % 2], ada_cols[n]).then_inc(wa_loaded[n % 2], 16)
                    if n < 2:
                        sp.dma_start(bias[n:n + 1, :, :].rearrange("v n c -> v (n c)"), b_ada[:, 0:2 * D]).then_inc(bias_loaded, 16)
                    if n in (1, 2):
                        load_w_in(n - 1)
                sp.dma_start(rpb_pad[:, RPB_PAD:RPB_PAD + RPB], rpb.rearrange("l h r c -> l (h r c)")).then_inc(rpb_stored, 16)
                sp.wait_ge(zeroed, 1)
                for at in (0, RPB_PAD + RPB):
                    sp.dma_start(rpb_pad[:, at:at + RPB_PAD], zeros[:, :]).then_inc(rpb_stored, 16)
                with sp.Fori(2, KT) as k:
                    load_w_in(k)
                sp.wait_ge(acc_read, N)
                sp.dma_start(mod[:, 0:2 * D], row[:, :, :].rearrange("v n c -> v (n c)")).then_inc(stored, 16)
                sp.wait_ge(stored, 16)
                sp.wait_ge(rpb_stored, 48)

            @block.scalar
            def _(act):
                act.wait_ge(cond_loaded, 32)
                act.activation(silu[:, :, :].rearrange("p k v -> p v k"), cond[:, :, :], ACT.Silu).then_inc(silu_done, 1)
                with act.Fori(0, KT) as k:
                    for n in range(PIECES):
                        act.wait_ge(staged[n], k * 16 + 16)
                        act.copy(w[HI][:, k, n * WC:(n + 1) * WC], stage[:, n, :]).then_inc(w_hi, 1)

            @block.gpsimd
            def _(pool):
                pool.memset(zeros[:, :], 0.0).then_inc(zeroed, 1)

            @block.tensor
            def _(pe):
                pe.wait_ge(silu_done, 1)
                for n in range(N):
                    pe.wait_ge(wa_loaded[n % 2], (n // 2 + 1) * 16)
                    for k in range(KT):
                        mm = pe.matmul(acc[0:2, n], silu[:, k, :], wa[:, n % 2, k], start=k == 0, stop=k == KT - 1)
                    mm.then_inc(acc_done, 1)

            @block.vector
            def _(dve):
                dve.sem_inc(w_lo, PIECES)

                def low(k):
                    for n in range(PIECES):
                        dve.wait_ge(w_hi, k * PIECES + n + 1)
                        at = slice(n * WC, (n + 1) * WC)
                        dve.tensor_tensor(w[LO][:, k, at], stage[:, n, :], w[HI][:, k, at].bitcast(F32),
                                          ALU.subtract).then_inc(w_lo, 1)

                with dve.Fori(0, KT - 2) as k:
                    low(k)
                dve.wait_ge(bias_loaded, 32)
                for n in range(N):
                    dve.wait_ge(acc_done, n + 1)
                    dve.tensor_tensor(row[:, n, :], acc[0:2, n], bias[:, n, :], ALU.add).then_inc(acc_read, 1)
                for k in (KT - 2, KT - 1):
                    low(k)


def projection_phase(nc, x_all, w, a_ws, a_bs, f_w, ident_in, dft_c64, dft_s64,
                     mod, rpb_pad, rel_bias, y, q_t, k_t, v_parts, chan_dft, new_k, new_v):
    G_TOK = 256
    NT = G_TOK // P
    GROUPS = T_ALL // G_TOK
    UNITS, PSLOTS, STAGES = 9, 3, 6
    SUB = KT // 2
    with ExitStack() as ctx:
        sb, ps, sem = phase_tools(nc, ctx)
        ht = [sb(f"pj_ht{h}", [P, 2, KT, G_TOK], F32R) for h in (HI, LO)]
        x = sb("pj_x", [P, NT, D])
        hm = sb("pj_hm", [P, 2, G_TOK])
        st = sb("pj_out_stage", [P, 2, 512])
        st_lo = sb("pj_lo_stage", [P, 512])
        st_v = sb("pj_v_stage", [P, HEADS, 3, HD], BF16)
        zbt = sb("pj_zbt", [P, 2, G_TOK])
        zg = sb("pj_gelu", [P, NT, 2 * D_A])
        wst = sb("pj_wst", [P, A_HEADS, P])
        bd = sb("pj_bd", [P, 2, 2, P])
        ident = sb("pj_ident", [P, P])
        shift = sb("pj_shift", [P, 2, KT])
        scale = sb("pj_scale", [P, 2, KT])
        scale1p = sb("pj_scale1p", [P, 2, KT])
        bs = sb("pj_bs", [P, A_HEADS])
        stats = sb("pj_stats", [P, NT, 2, 6])
        mv = sb("pj_mv", [P, NT, 2])
        veps = sb("pj_veps", [P, NT])
        rstd = sb("pj_rstd", [P, NT])
        vstats = sb("pj_vstats", [P, 6])
        vmv = sb("pj_vmv", [P, 2])
        vveps = sb("pj_vveps", [P, 1])
        vrstd = sb("pj_vrstd", [P, 1])
        minus_half = sb("pj_minus_half", [P, 2])
        eps = sb("pj_eps", [P, 2])
        waited = sb("pj_waited", [P, 1])
        tps = ps("pj_tps", [P, 2, 2, G_TOK])
        gps = ps("pj_gps", [P, PSLOTS, 512])
        mixps = ps("pj_mixps", [P, A_HEADS, NT, HD])
        abps = ps("pj_abps", [P, 2, 512])

        consts_loaded, fw_zeroed, fw_loaded = sem("pj_consts_loaded"), sem("pj_fw_zeroed"), sem("pj_fw_loaded")
        setup_mm, setup_done, scale_done, half_done = (sem("pj_setup_mm"), sem("pj_setup_done"),
                                                       sem("pj_scale_done"), sem("pj_half_done"))
        x_loaded = sem("pj_x_loaded")
        stats_done, mv_done, veps_done, rstd_done, xn_done = (
            sem("pj_stats_done"), sem("pj_mv_done"), sem("pj_veps_done"), sem("pj_rstd_done"), sem("pj_xn_done"))
        tps_done, hm_done, h_hi, h_lo = sem("pj_tps_done"), sem("pj_hm_done"), sem("pj_h_hi"), sem("pj_h_lo")
        unit_done = sem("pj_unit_done")
        slot_read = [sem(f"pj_slot_read{s}") for s in range(PSLOTS)]
        qk_hi, v_hi, v_mid, v_done, raw_done = sem("pj_qk_hi"), sem("pj_v_hi"), sem("pj_v_mid"), sem("pj_v_done"), sem("pj_raw_done")
        lo_stored, v_stored, raw_stored = sem("pj_lo_stored"), sem("pj_v_stored"), sem("pj_raw_stored")
        vstats_done, vmv_done, vveps_done, vrstd_done, vn_done = (
            sem("pj_vstats_done"), sem("pj_vmv_done"), sem("pj_vveps_done"),
            sem("pj_vrstd_done"), sem("pj_vn_done"))
        mix_done, ya_done, ya_stored = sem("pj_mix_done"), sem("pj_ya_done"), sem("pj_ya_stored")
        ab_done = sem("pj_ab_done")
        ab_read = sem("pj_ab_read")
        st_stored = [sem(f"pj_st_stored{s}") for s in range(2)]
        rel_stored = sem("pj_rel_stored")
        N_CONSTS = 8

        x_groups = x_all.rearrange("(g t p) d -> g p t d", p=P, t=NT)
        tok = lambda g, t: bass.ds(g * G_TOK + t * P, P)
        grp = lambda g: bass.ds(g * G_TOK, G_TOK)
        qt_tiles = q_t.rearrange("x (m p) t -> x p m t", p=P)
        kt_tiles = k_t.rearrange("x (m p) t -> x p m t", p=P)
        fw2 = zg[:, 0]
        ws = hm
        v_rest = zg[:, 1]

        def every_group(eng, body):
            body(0, 0, True, LAT, False)
            with eng.Fori(0, (GROUPS - 3) // 2) as i:
                for s in range(2):
                    body(i * 2 + (1 + s), 1 - s, True, LAT, False)
            body(GROUPS - 2, 1, False, CTX, False)
            body(GROUPS - 1, 0, False, None, True)

        with nc.Block() as block:
            @block.sync
            def _(sp):
                sp.dma_start(x[:, :, :], x_groups[0]).then_inc(x_loaded, 16)
                for s in range(2):
                    sp.sem_inc(st_stored[s], 16)
                sp.sem_inc(lo_stored, 16)
                sp.sem_inc(v_stored, 16)
                with nc.allow_non_contiguous_dma(reason="modulation and biases, channel on partition"):
                    for v in range(2):
                        for dst, what in ((shift, SHIFT1), (scale, SCALE1)):
                            sp.dma_start(dst[:, v, :], mod[v, what * D:(what + 1) * D].rearrange("(k p) -> p k", p=P)).then_inc(consts_loaded, 16)
                    sp.dma_start(bs[:, :], a_bs.rearrange("l h p -> p (l h)")).then_inc(consts_loaded, 16)
                sp.dma_start(ident[:, :], ident_in).then_inc(consts_loaded, 16)
                sp.dma_start(zbt[:, 0, 0:P], dft_c64).then_inc(consts_loaded, 16)
                sp.dma_start(zbt[:, 1, 0:P], dft_s64).then_inc(consts_loaded, 16)
                sp.dma_start(ws[:, :, :].rearrange("p a (b q) -> p (a b) q", q=P), a_ws.rearrange("l h p q -> p (l h) q")).then_inc(fw_loaded, 16)
                sp.wait_ge(fw_zeroed, 1)
                for g in range(4):
                    pair, half = g // 2, g % 2
                    sp.dma_start(fw2[half * 64:half * 64 + 64, pair * P + half * 64:pair * P + half * 64 + 64],
                                 f_w[0, g]).then_inc(fw_loaded, 16)
                sp.wait_ge(tps_done, SUB)
                sp.dma_start(x[:, :, :], x_groups[1]).then_inc(x_loaded, 16)
                shifted = bass.AP(rpb_pad.tensor, RPB_PAD + REL_COLS // 2, [[REL_COLS, HEADS * REL_ROWS], [-1, GRID], [1, GRID]])
                sp.dma_start(rel_bias.rearrange("q r k -> r q k"), shifted).then_inc(rel_stored, 16)

                def group(g, s, next2, next1, is_ctx):
                    if next2:
                        sp.wait_ge(tps_done, (g + 2) * SUB)
                        sp.dma_start(x[:, :, :], x_groups[g + 2]).then_inc(x_loaded, 16)
                    staged = [0]

                    def stage():
                        staged[0] += 1
                        return (staged[0] - 1) % 2

                    def store_qk(dst, m, unit, n):
                        slot = stage()
                        sp.wait_ge(slot_read[unit % PSLOTS], g * (UNITS // PSLOTS) + unit // PSLOTS + 2)
                        view = lambda ap: ap.rearrange("p (m t) -> p m t", m=2)
                        sp.dma_start(dst[HI][:, m:m + 2, grp(g)], view(st[:, slot, :])).then_inc(st_stored[slot], 16)
                        sp.dma_start(dst[LO][:, m:m + 2, grp(g)], view(st_lo[:, :])).then_inc(lo_stored, 16)

                    def store_ab(t):
                        slot = stage()
                        sp.wait_ge(ab_read, g * NT + t + 1 + NT)
                        sp.dma_start(chan_dft[tok(g, t), :], st[:, slot, :]).then_inc(st_stored[slot], 16)

                    def store_ya(t):
                        sp.wait_ge(ya_done, g * NT + t + 2)
                        sp.dma_start(y[tok(g, t), 0:D_A], zg[:, t, 0:D_A]).then_inc(ya_stored, 16)

                    store_qk(qt_tiles, 0, 1, 0)
                    store_qk(qt_tiles, 2, 4, 1)
                    store_ya(0)
                    store_qk(kt_tiles, 0, 5, 2)
                    store_ya(1)
                    store_ab(0)
                    store_qk(kt_tiles, 2, 6, 3)
                    store_ab(1)
                    for t in range(NT):
                        sp.wait_ge(v_done, g * NT + t + 1)
                        sp.dma_start(v_parts[tok(g, t), :], st_v[:, :, :, :].rearrange("p h n d -> p (h n d)")).then_inc(v_stored, 16)
                    if is_ctx:
                        for n, (out, t) in enumerate(((new_v, 0), (new_v, 1), (new_k, 0), (new_k, 1))):
                            sp.wait_ge(raw_done, n + 1)
                            sp.dma_start(out[t * P:(t + 1) * P, :], x[:, t, (n // 2) * 512:(n // 2 + 1) * 512]).then_inc(raw_stored, 16)

                every_group(sp, group)
                for s in range(2):
                    sp.wait_ge(st_stored[s], 16 * (GROUPS * STAGES // 2 + 1))
                sp.wait_ge(rel_stored, 16)
                sp.wait_ge(lo_stored, 16 * (GROUPS * 4 + 1))
                sp.wait_ge(v_stored, 16 * (GROUPS * NT + 1))
                sp.wait_ge(raw_stored, 16 * 4)
                sp.wait_ge(ya_stored, 16 * GROUPS * NT)

            @block.gpsimd
            def _(pool):
                pool.memset(fw2[:, :], 0.0).then_inc(fw_zeroed, 1)
                pool.memset(minus_half[:, :], -0.5).then_inc(half_done, 1)
                pool.memset(eps[:, :], EPS).then_inc(half_done, 1)
                pool.wait_ge(half_done, 2)

                def row_rstd(n):
                    pool.wait_ge(mv_done, n * NT + NT)
                    pool.tensor_tensor(veps[:, :], mv[:, :, 1], eps[:, :], ALU.add).then_inc(veps_done, 1)
                    pool.wait_ge(veps_done, n + 1)
                    pool.tensor_tensor(rstd[:, :], veps[:, :], minus_half[:, :], ALU.pow).then_inc(rstd_done, 1)

                def gate_rstd(n):
                    pool.wait_ge(vmv_done, n + 1)
                    pool.tensor_tensor(vveps[:, :], vmv[:, 1:2], eps[:, 0:1], ALU.add).then_inc(vveps_done, 1)
                    pool.wait_ge(vveps_done, n + 1)
                    pool.tensor_tensor(vrstd[:, :], vveps[:, :], minus_half[:, 0:1], ALU.pow).then_inc(vrstd_done, 1)

                row_rstd(0)
                row_rstd(1)

                def group(g, s, next2, next1, is_ctx):
                    gate_rstd(g * NT)
                    if next2:
                        row_rstd(g + 2)
                    gate_rstd(g * NT + 1)

                every_group(pool, group)

            @block.scalar
            def _(act):
                for s in range(PSLOTS):
                    act.sem_inc(slot_read[s], 1)
                act.sem_inc(ab_read, NT)
                def round_h(n, s, j, used=None):
                    if used is not None:
                        act.wait_ge(unit_done, used * UNITS)
                    act.wait_ge(hm_done, n * SUB * 2 + 2 * j + 2)
                    act.copy(ht[HI][:, s, 2 * j:2 * j + 2, :], hm[:, :, :]).then_inc(h_hi, 1)

                for j in range(SUB):
                    round_h(0, 0, j)

                def group(g, s, next2, next1, is_ctx):
                    if next1 is not None:
                        for j in range(SUB):
                            round_h(g + 1, 1 - s, j, used=g)
                    unit, staged = [0], [0]

                    def product():
                        unit[0] += 1
                        act.wait_ge(unit_done, g * UNITS + unit[0])
                        return (unit[0] - 1) % PSLOTS

                    def stage():
                        slot, use = staged[0] % 2, staged[0] // 2
                        staged[0] += 1
                        act.wait_ge(st_stored[slot], (g * (STAGES // 2) + use + 1) * 16)
                        return st[:, slot, :]

                    def gelu(t):
                        n = product()
                        if not (isinstance(g, int) and g == 0):
                            if t == 0:
                                act.wait_ge(ya_stored, g * (NT * 16))
                            else:
                                act.wait_ge(v_done, g * NT)
                        act.activation(zg[:, t, :], gps[:, n, :], ACT.Gelu_apprx_tanh).then_inc(slot_read[n], 1)

                    def round_qk(times=1.0):
                        n = product()
                        act.activation(stage().bitcast(F32R), gps[:, n, :], ACT.Copy, scale=times).then_inc(qk_hi, 1)

                    def ab_to_stage(t):
                        act.wait_ge(ab_done, g * NT + t + 1 + NT)
                        act.copy(stage(), abps[:, t, :]).then_inc(ab_read, 1)

                    gelu(0)
                    round_qk(HD ** -0.5)
                    n = product()
                    act.wait_ge(ab_done, g * NT + NT)
                    act.copy(zbt[:, :, :].rearrange("p m t -> p (m t)"), gps[:, n, :]).then_inc(slot_read[n], 1)
                    gelu(1)
                    round_qk(HD ** -0.5)
                    round_qk()
                    ab_to_stage(0)
                    round_qk()
                    ab_to_stage(1)
                    for t in range(NT):
                        n = product()
                        act.wait_ge(v_stored, (g * NT + t + 1) * 16)
                        if is_ctx:
                            act.copy(x[:, t, 0:512], gps[:, n, :]).then_inc(raw_done, 1)
                        act.copy(st_v[:, :, 0, :], gps[:, n, :].rearrange("p (h d) -> p h d", h=HEADS)).then_inc(v_hi, 1)
                    if is_ctx:
                        for t in range(NT):
                            n = product()
                            act.copy(x[:, t, 512:1024], gps[:, n, :]).then_inc(raw_done, 1)

                act.wait_ge(setup_mm, 2)
                every_group(act, group)

            @block.tensor
            def _(pe):
                pe.sem_inc(ab_done, NT)
                pe.wait_ge(consts_loaded, 16 * N_CONSTS)
                pe.wait_ge(fw_loaded, 16 * 5)
                for h in range(A_HEADS):
                    mm = pe.transpose(gps[:, 0, h * P:(h + 1) * P], ws[:, h // 2, (h % 2) * P:(h % 2 + 1) * P], ident[:, :])
                mm.then_inc(setup_mm, 1)
                for m in range(2):
                    for ri in range(2):
                        mm = pe.matmul(gps[:, 1, (2 * m + ri) * P:(2 * m + ri + 1) * P], zbt[:, ri, 0:P],
                                       fw2[:, m * P:(m + 1) * P], start=True, stop=True)
                mm.then_inc(setup_mm, 1)
                pe.wait_ge(setup_done, 2)

                def transposes(n, j):
                    if not (isinstance(n, int) and n == 0 and j < 2):
                        pe.wait_ge(hm_done, (n * SUB + j - 2) * 2 + 2)
                    for kk in range(2):
                        for t in range(NT):
                            k = 2 * j + kk
                            mm = pe.transpose(tps[:, j % 2, kk, t * P:(t + 1) * P], x[:, t, k * P:(k + 1) * P], ident[:, :])
                    mm.then_inc(tps_done, 1)

                pe.wait_ge(xn_done, NT)
                for j in range(SUB):
                    transposes(0, j)

                def group(g, s, next2, next1, is_ctx):
                    def turn_next(js):
                        if next1 is not None:
                            if 0 in js:
                                pe.wait_ge(xn_done, (g + 1) * NT + NT)
                            for j in js:
                                transposes(g + 1, j)

                    unit = [0]

                    def product():
                        pe.wait_ge(slot_read[unit[0] % PSLOTS], g * (UNITS // PSLOTS) + unit[0] // PSLOTS + 1)
                        unit[0] += 1
                        return gps[:, (unit[0] - 1) % PSLOTS, :]

                    def rows(t, col):
                        out = product()
                        for k in range(KT):
                            for a, b in PASSES:
                                mm = pe.matmul(out, ht[a][:, s, k, t * P:(t + 1) * P], w[b][:, k, col:col + 512],
                                               start=(k, a, b) == (0, HI, HI), stop=(k, a, b) == (KT - 1, LO, HI))
                        mm.then_inc(unit_done, 1)

                    def channels(col):
                        out = product()
                        for m in range(2):
                            for k in range(KT):
                                for a, b in PASSES:
                                    mm = pe.matmul(out[:, m * G_TOK:(m + 1) * G_TOK],
                                                   w[a][:, k, col + m * P:col + (m + 1) * P], ht[b][:, s, k, :],
                                                   start=(k, a, b) == (0, HI, HI), stop=(k, a, b) == (KT - 1, LO, HI))
                        mm.then_inc(unit_done, 1)

                    def mix():
                        pe.wait_ge(vn_done, (g + 1) * NT)
                        pe.wait_ge(ya_done, g * NT + 1)
                        for h in range(A_HEADS):
                            mm = pe.matmul(mixps[:, h, :, :], wst[:, h, :],
                                           zg[:, :, D_A + h * HD:D_A + (h + 1) * HD], start=True, stop=True)
                        mm.then_inc(mix_done, 1)

                    def channel_dft(t):
                        if t == 0:
                            pe.wait_ge(slot_read[2], g * (UNITS // PSLOTS) + 2)
                        pe.wait_ge(ab_read, g * NT + t + 1)
                        for m in range(2):
                            mm = pe.matmul(abps[:, t, m * 256:(m + 1) * 256], zbt[:, m, t * P:(t + 1) * P],
                                           bd[:, m, :, :].rearrange("p r c -> p (r c)"), start=True, stop=True)
                        mm.then_inc(ab_done, 1)

                    if isinstance(g, int) and g == 0:
                        pe.wait_ge(h_lo, SUB)
                        rows(0, COL_ZA)
                        turn_next((0, 1))
                        channels(COL_Q)
                        turn_next((2, 3))
                    else:
                        turn_next((0, 1))
                        rows(0, COL_ZA)
                        turn_next((2, 3))
                        channels(COL_Q)
                    channels(COL_ZB)
                    rows(1, COL_ZA)
                    channels(COL_Q + 256)
                    mix()
                    channels(COL_K)
                    channel_dft(0)
                    channels(COL_K + 256)
                    channel_dft(1)
                    for t in range(NT):
                        rows(t, COL_V)
                    if is_ctx:
                        for t in range(NT):
                            rows(t, COL_K)

                every_group(pe, group)

            @block.vector
            def _(dve):
                dve.sem_inc(ya_done, 1)
                def norm_x(n):
                    dve.wait_ge(x_loaded, n * 16 + 16)
                    for t in range(NT):
                        for half in range(2):
                            last = dve.bn_stats(stats[:, t, half, :], x[:, t, half * 512:(half + 1) * 512])
                    last.then_inc(stats_done, 1)
                    dve.wait_ge(stats_done, n + 1)
                    dve.tensor_copy(waited[:, :], stats[:, 0, 0, 0:1])
                    for t in range(NT):
                        dve.bn_aggr(mv[:, t, :], stats[:, t, :, :].rearrange("p a b -> p (a b)")).then_inc(mv_done, 1)
                    dve.wait_ge(rstd_done, n + 1)
                    for t in range(NT):
                        dve.tensor_scalar(x[:, t, :], x[:, t, :], mv[:, t, 0:1], rstd[:, t:t + 1],
                                          ALU.subtract, ALU.mult).then_inc(xn_done, 1)

                def modulate(n, s, vec, used=None):
                    if used is not None:
                        dve.wait_ge(unit_done, used * UNITS)
                    for j in range(SUB):
                        dve.wait_ge(tps_done, n * SUB + j + 1)
                        dve.wait_ge(h_lo, n * SUB + j)
                        for kk in range(2):
                            k = 2 * j + kk
                            dve.tensor_scalar(hm[:, kk, :], tps[:, j % 2, kk, :], scale1p[:, vec, k:k + 1],
                                              shift[:, vec, k:k + 1], ALU.mult, ALU.add).then_inc(hm_done, 1)
                        dve.wait_ge(h_hi, n * SUB + j + 1)
                        dve.tensor_tensor(ht[LO][:, s, 2 * j:2 * j + 2, :], hm[:, :, :],
                                          ht[HI][:, s, 2 * j:2 * j + 2, :].bitcast(F32), ALU.subtract).then_inc(h_lo, 1)

                norm_x(0)
                dve.wait_ge(consts_loaded, 16 * N_CONSTS)
                dve.tensor_scalar(scale1p[:, :, :], scale[:, :, :], 1.0, None, ALU.add).then_inc(scale_done, 1)
                dve.wait_ge(setup_mm, 2)
                dve.tensor_copy(wst[:, :, :].rearrange("p h q -> p (h q)"), gps[:, 0, :]).then_inc(setup_done, 1)
                dve.tensor_copy(bd[:, :, :, :].rearrange("p m r c -> p (m r c)"), gps[:, 1, :]).then_inc(setup_done, 1)
                dve.wait_ge(scale_done, 1)
                modulate(0, 0, LAT)
                norm_x(1)

                def group(g, s, next2, next1, is_ctx):
                    if next1 is not None:
                        modulate(g + 1, 1 - s, next1, used=g)

                    def gate_norm(t):
                        n = g * NT + t
                        dve.wait_ge(slot_read[0], g * (UNITS // PSLOTS) + t + 2)
                        dve.bn_stats(vstats[:, :], zg[:, t, D_A:2 * D_A]).then_inc(vstats_done, 1)
                        dve.wait_ge(vstats_done, n + 1)
                        dve.tensor_copy(waited[:, :], vstats[:, 0:1])
                        dve.bn_aggr(vmv[:, :], vstats[:, :]).then_inc(vmv_done, 1)
                        dve.wait_ge(vrstd_done, n + 1)
                        dve.tensor_scalar(zg[:, t, D_A:2 * D_A], zg[:, t, D_A:2 * D_A], vmv[:, 0:1], vrstd[:, :],
                                          ALU.subtract, ALU.mult).then_inc(vn_done, 1)

                    def gate(t):
                        n = g * NT + t
                        dve.wait_ge(mix_done, g + 1)
                        for h in range(A_HEADS):
                            at = slice(h * HD, (h + 1) * HD)
                            last = dve.scalar_tensor_tensor(zg[:, t, at], mixps[:, h, t, :], bs[:, h:h + 1], zg[:, t, at], ALU.add, ALU.mult)
                        last.then_inc(ya_done, 1)

                    def low_qk(n, unit, times=1.0):
                        slot = unit % PSLOTS
                        dve.wait_ge(qk_hi, g * 4 + n + 1)
                        dve.wait_ge(lo_stored, (g * 4 + n + 1) * 16)
                        hi = st[:, (0, 1, 0, 0)[n], :]
                        dve.scalar_tensor_tensor(st_lo[:, :].bitcast(F32R), gps[:, slot, :], times, hi,
                                                 ALU.mult, ALU.subtract).then_inc(slot_read[slot], 1)

                    def v_tail(t, unit):
                        n = g * NT + t
                        slot = unit % PSLOTS
                        heads = lambda ap: ap.rearrange("p (h d) -> p h d", h=HEADS)
                        if t == 0:
                            dve.wait_ge(ya_stored, (g + 1) * (NT * 16))
                        dve.wait_ge(v_hi, n + 1)
                        dve.tensor_tensor(heads(v_rest[:, :]), heads(gps[:, slot, :]), st_v[:, :, 0, :], ALU.subtract).then_inc(slot_read[slot], 1)
                        dve.wait_ge(slot_read[slot], g * (UNITS // PSLOTS) + unit // PSLOTS + 2)
                        dve.tensor_copy(st_v[:, :, 1, :], heads(v_rest[:, :])).then_inc(v_mid, 1)
                        dve.wait_ge(v_mid, n + 1)
                        dve.tensor_tensor(st_v[:, :, 2, :], heads(v_rest[:, :]), st_v[:, :, 1, :], ALU.subtract).then_inc(v_done, 1)

                    gate_norm(0)
                    low_qk(0, 1, HD ** -0.5)
                    if next2:
                        norm_x(g + 2)
                    gate_norm(1)
                    low_qk(1, 4, HD ** -0.5)
                    gate(0)
                    low_qk(2, 5)
                    gate(1)
                    low_qk(3, 6)
                    v_tail(0, 7)
                    v_tail(1, 8)

                every_group(dve, group)


def fourier_phase(nc, chan_dft, twiddle_in, dft512_in, dft256_in, conds, w_ada, b_ada, cache_k, cache_v, ident_in,
                  mod, k_t, v_parts, y):
    R = 4
    with ExitStack() as ctx:
        sb, ps, sem = phase_tools(nc, ctx)
        tw = sb("fo_tw", [P, R, R, 2])
        table = [sb(f"fo_table{h}", [P, 2, R, 512], F32R) for h in (HI, LO)]
        w = sb("fo_w", [P, 2, KT, ADA_COLS])
        table_in = w[:, 1].rearrange("p (r i) m -> p r i m", r=2)
        table_flat = table_in.rearrange("p r i m -> p (r i m)")
        cond = sb("fo_cond", [P, 2, KT])
        silu = sb("fo_silu", [P, KT, 2])
        bias = sb("fo_bias", [2, 2, ADA_COLS])
        row = sb("fo_row", [2, 2, ADA_COLS])
        x = sb("fo_x", [P, 4 * R, 512])
        ctab = x[:, 0:2, :].rearrange("p r (i k) -> p r i k", i=2)
        xc = x[:, 2:4, :]
        ident = sb("fo_ident", [P, P])
        kc = sb("fo_kc", [P, D_C])
        kct = [sb(f"fo_kct{h}", [P, D_C // P, P]) for h in (HI, LO)]
        vc = sb("fo_vc", [P, HEADS, HD])
        vparts = sb("fo_vparts", [P, HEADS, 3, HD], BF16)
        sums = sb("fo_sums", [P, 2, 2, 512])
        yj = sb("fo_y", [P, 2, R, 256])
        prod = sb("fo_prod", [P, 2, 256])
        ys = [sb(f"fo_ys{h}", [P, R, 2, R, 256], F32R) for h in (HI, LO)]
        out = sb("fo_out", [P, 4, 2, 256])
        acc = ps("fo_acc", [P, 4, 512])
        ada_acc = ps("fo_ada_acc", [P, 2, ADA_COLS])
        kps = ps("fo_kps", [P, D_C // P, P])
        ident_loaded, kc_loaded, kc_turned, kc_hi, kc_lo, kc_stored = (
            sem("fo_ident_loaded"), sem("fo_kc_loaded"), sem("fo_kc_turned"), sem("fo_kc_hi"), sem("fo_kc_lo"), sem("fo_kc_stored"))
        vc_loaded, vc_step, vc_stored = sem("fo_vc_loaded"), sem("fo_vc_step"), sem("fo_vc_stored")
        VC_STEPS = 5
        PAST_TILES = T_PAST // P
        tables_loaded, x_loaded = sem("fo_tables_loaded"), [sem(f"fo_x_loaded{i}") for i in range(R)]
        xc_loaded = sem("fo_xc_loaded")
        table_hi, table_lo = sem("fo_table_hi"), sem("fo_table_lo")
        sums_done, bfly_done, prod_done, tw_done = sem("fo_sums_done"), sem("fo_bfly_done"), sem("fo_prod_done"), sem("fo_tw_done")
        y_hi, y_lo = sem("fo_y_hi"), sem("fo_y_lo")
        acc_done, acc_read = sem("fo_acc_done"), sem("fo_acc_read")
        stored = [sem(f"fo_stored{s}") for s in range(4)]
        ctx_stored = sem("fo_ctx_stored")
        cond_loaded, silu_done = sem("fo_cond_loaded"), sem("fo_silu_done")
        w_loaded = [sem(f"fo_w_loaded{s}") for s in range(2)]
        bias_loaded = [sem(f"fo_bias_loaded{s}") for s in range(2)]
        ada_done, ada_read = sem("fo_ada_done"), sem("fo_ada_read")
        row_stored = [sem(f"fo_row_stored{s}") for s in range(2)]
        FIRST, CHUNKS = 2 * D // ADA_COLS, 4 * D // ADA_COLS
        w_cols = ada_columns(w_ada)
        UNITS = 8

        k_rows = cache_k.rearrange("b l (n p) h d -> (b l n) p (h d)", p=P)
        v_rows = cache_v.rearrange("b l (n p) h d -> (b l n) p h d", p=P)
        y_lat = y[0:T_LAT, D_A:D_A + D_B].rearrange("(m p j) c -> m p j c", p=P, j=R)
        SPLITS = R

        with nc.Block() as block:
            @block.sync
            def _(sp):
                xs = chan_dft[0:T_LAT, :].rearrange("(q i p) c -> i p q c", p=P, i=R)

                def load_past(t):
                    if t:
                        sp.wait_ge(kc_turned, t)
                    sp.dma_start(kc[:, :], k_rows[t]).then_inc(kc_loaded, 16)
                    if t:
                        sp.wait_ge(vc_step, t * VC_STEPS)
                    sp.dma_start(vc[:, :, :], v_rows[t]).then_inc(vc_loaded, 16)

                def store_past(t):
                    at = slice(T_ALL + t * P, T_ALL + (t + 1) * P)
                    sp.wait_ge(kc_lo, t + 1)
                    for part in (HI, LO):
                        sp.dma_start(k_t[part, :, at].rearrange("(m p) t -> p m t", p=P), kct[part][:, :, :]).then_inc(kc_stored, 16)
                    sp.wait_ge(vc_step, (t + 1) * VC_STEPS)
                    sp.dma_start(v_parts[at, :], vparts[:, :, :, :].rearrange("p h k d -> p (h k d)")).then_inc(vc_stored, 16)

                def store_unit(u):
                    jp, m = u // R, u % R
                    sp.wait_ge(acc_read, 4 + u + 1)
                    sp.dma_start(y_lat[m, :, 2 * jp:2 * jp + 2, :], out[:, u % 4, :, :]).then_inc(stored[u % 4], 16)

                with nc.allow_non_contiguous_dma(reason="two conditioning vectors, channel on partition"):
                    for v in (LAT, CTX):
                        sp.dma_start(cond[:, v, :], conds[v].rearrange("(k p) -> p k", p=P)).then_inc(cond_loaded, 16)

                def load_chunk(c):
                    slot, col = c % 2, (FIRST + c) * ADA_COLS
                    if c >= 2:
                        sp.wait_ge(ada_done, c - 1)
                    sp.dma_start(w[:, slot], w_cols[FIRST + c]).then_inc(w_loaded[slot], 16)
                    if c >= 2:
                        sp.wait_ge(ada_read, c - 1)
                    for v in range(2):
                        sp.dma_start(bias[v:v + 1, slot, :], b_ada[:, col:col + ADA_COLS]).then_inc(bias_loaded[slot], 16)

                def store_chunk(c):
                    col = (FIRST + c) * ADA_COLS
                    sp.wait_ge(ada_read, c + 1)
                    sp.dma_start(mod[:, col:col + ADA_COLS], row[:, c % 2, :]).then_inc(row_stored[c % 2], 16)

                sp.dma_start(tw[:, :, :, :], twiddle_in.rearrange("(i p) j r -> p i j r", p=P)).then_inc(tables_loaded, 16)
                for i in range(R):
                    sp.dma_start(x[:, i * R:(i + 1) * R, :], xs[i]).then_inc(x_loaded[i], 16)
                    if i == 0:
                        sp.dma_start(table_in, dft512_in.rearrange("r (i p) m -> p r i m", p=P)).then_inc(tables_loaded, 16)
                        load_chunk(0)
                        sp.dma_start(ident[:, :], ident_in).then_inc(ident_loaded, 16)
                        load_past(0)
                sp.wait_ge(table_lo, 1)
                load_chunk(1)
                for c in range(2, CHUNKS):
                    load_chunk(c)
                    store_chunk(c - 2)
                    if c in (4, 5):
                        store_unit(2 * c - 8)
                        store_unit(2 * c - 7)
                    if c >= CHUNKS - 2:
                        load_past(c - CHUNKS + 3)
                        store_past(c - CHUNKS + 2)
                    if c == 5:
                        sp.wait_ge(bfly_done, 8 * R)
                        sp.dma_start(ctab, dft256_in.rearrange("r (i p) m -> p r i m", p=P)).then_inc(xc_loaded, 16)
                        sp.dma_start(xc, chan_dft[T_LAT:T_ALL, :].rearrange("(i p) c -> p i c", p=P)).then_inc(xc_loaded, 16)
                load_past(3)
                store_past(2)
                store_unit(4)
                store_unit(5)
                store_chunk(CHUNKS - 2)
                store_past(3)
                store_unit(6)
                store_chunk(CHUNKS - 1)
                store_unit(7)
                for t in range(2):
                    sp.wait_ge(acc_read, 4 + UNITS + t + 1)
                    sp.dma_start(y[T_LAT + t * P:T_LAT + (t + 1) * P, D_A:D_A + D_B], out[:, t, 0, :]).then_inc(ctx_stored, 16)
                for s in range(4):
                    sp.wait_ge(stored[s], UNITS // 4 * 16)
                for s in range(2):
                    sp.wait_ge(row_stored[s], CHUNKS // 2 * 16)
                sp.wait_ge(kc_stored, PAST_TILES * 32)
                sp.wait_ge(vc_stored, PAST_TILES * 16)
                sp.wait_ge(ctx_stored, 32)

            @block.scalar
            def _(act):
                act.sem_inc(acc_read, 4)
                act.wait_ge(tables_loaded, 32)
                act.copy(table[HI][:, :, :, :].rearrange("p r i m -> p (r i m)"), table_flat).then_inc(table_hi, 1)
                act.wait_ge(cond_loaded, 32)
                act.activation(silu[:, :, :].rearrange("p k v -> p v k"), cond[:, :, :], ACT.Silu).then_inc(silu_done, 1)
                for i in range(R):
                    act.wait_ge(bfly_done, 8 * (i + 1))
                    act.wait_ge(tw_done, 3 * 4 * (i + 1))
                    act.copy(ys[HI][:, i].rearrange("p r j c -> p (r j c)"), yj[:, :, :, :].rearrange("p r j c -> p (r j c)")).then_inc(y_hi, 1)
                for u in range(UNITS + 2):
                    if R <= u < R + PAST_TILES:
                        t = u - R
                        act.wait_ge(kc_turned, t + 1)
                        if t:
                            act.wait_ge(kc_stored, t * 32)
                        act.copy(kct[HI][:, :, :].bitcast(F32R), kps[:, :, :]).then_inc(kc_hi, 1)
                    act.wait_ge(acc_done, u + 1)
                    if u >= 4:
                        act.wait_ge(stored[u % 4], u // 4 * 16)
                    if u < UNITS:
                        act.copy(out[:, u % 4, :, :].rearrange("p j c -> p (j c)"), acc[:, u % 4, :]).then_inc(acc_read, 1)
                    else:
                        act.copy(out[:, u % 4, 0, :], acc[:, u % 4, 0:256]).then_inc(acc_read, 1)

            @block.vector
            def _(dve):
                def add_bias(c):
                    dve.wait_ge(ada_done, c + 1)
                    dve.wait_ge(bias_loaded[c % 2], (c // 2 + 1) * 32)
                    if c >= 2:
                        dve.wait_ge(row_stored[c % 2], c // 2 * 16)
                    dve.tensor_tensor(row[:, c % 2, :], ada_acc[0:2, c % 2, :], bias[:, c % 2, :], ALU.add).then_inc(ada_read, 1)

                for i in range(R):
                    xi = x[:, i * R:(i + 1) * R, :]
                    dve.wait_ge(x_loaded[i], 16)
                    for odd in range(2):
                        for diff in range(2):
                            dve.tensor_tensor(sums[:, odd, diff, :], xi[:, odd, :], xi[:, odd + 2, :],
                                              ALU.subtract if diff else ALU.add).then_inc(sums_done, 1)
                    dve.wait_ge(sums_done, 4 * (i + 1))
                    part = lambda odd, diff, ri: sums[:, odd, diff, :].rearrange("p (h r c) -> p r h c", h=2, r=2)[:, ri]
                    y_of = lambda ri, j: yj[:, ri, j, :].rearrange("p (h c) -> p h c", h=2)
                    for ri in range(2):
                        for j in (0, 2):
                            dve.tensor_tensor(y_of(ri, j), part(0, 0, ri), part(1, 0, ri),
                                              ALU.subtract if j else ALU.add).then_inc(bfly_done, 1)
                    for ri in range(2):
                        for j in (1, 3):
                            op = ALU.add if (ri == 0) == (j == 1) else ALU.subtract
                            dve.tensor_tensor(y_of(ri, j), part(0, 1, ri), part(1, 1, 1 - ri), op).then_inc(bfly_done, 1)
                    if i == 0:
                        dve.wait_ge(tables_loaded, 32)
                    dve.wait_ge(bfly_done, 8 * (i + 1))
                    for j in range(1, R):
                        n = (i * 3 + j - 1)
                        cos, sin = tw[:, i, j, 0:1], tw[:, i, j, 1:2]
                        if n:
                            dve.wait_ge(tw_done, 4 * n)
                        dve.tensor_scalar(prod[:, 0, :], yj[:, 1, j, :], sin, None, ALU.mult).then_inc(prod_done, 1)
                        dve.tensor_scalar(prod[:, 1, :], yj[:, 0, j, :], sin, None, ALU.mult).then_inc(prod_done, 1)
                        dve.wait_ge(prod_done, 2 * n + 2)
                        dve.scalar_tensor_tensor(yj[:, 0, j, :], yj[:, 0, j, :], cos, prod[:, 0, :],
                                                 ALU.mult, ALU.add).then_inc(tw_done, 2)
                        dve.scalar_tensor_tensor(yj[:, 1, j, :], yj[:, 1, j, :], cos, prod[:, 1, :],
                                                 ALU.mult, ALU.subtract).then_inc(tw_done, 2)
                    if i == 0:
                        dve.wait_ge(table_hi, 1)
                        dve.tensor_tensor(table[LO][:, :, :, :].rearrange("p r i m -> p (r i m)"), table_flat,
                                          table[HI][:, :, :, :].rearrange("p r i m -> p (r i m)").bitcast(F32), ALU.subtract).then_inc(table_lo, 1)
                    dve.wait_ge(y_hi, i + 1)
                    dve.tensor_tensor(ys[LO][:, i].rearrange("p r j c -> p (r j c)"), yj[:, :, :, :].rearrange("p r j c -> p (r j c)"),
                                      ys[HI][:, i].rearrange("p r j c -> p (r j c)").bitcast(F32), ALU.subtract).then_inc(y_lo, 1)
                    if i >= 1:
                        add_bias(i - 1)
                for c in range(R - 1, CHUNKS):
                    add_bias(c)
                    t = c - (CHUNKS - PAST_TILES)
                    if t >= 0:
                        dve.wait_ge(kc_hi, t + 1)
                        dve.tensor_tensor(kct[LO][:, :, :].bitcast(F32R), kps[:, :, :], kct[HI][:, :, :], ALU.subtract).then_inc(kc_lo, 1)

            @block.gpsimd
            def _(pool):
                for t in range(PAST_TILES):
                    for n in range(3):
                        if n == 0:
                            pool.wait_ge(vc_loaded, (t + 1) * 16)
                            if t:
                                pool.wait_ge(vc_stored, t * 16)
                        else:
                            pool.wait_ge(vc_step, t * VC_STEPS + 2 * n)
                        pool.tensor_copy(vparts[:, :, n, :], vc[:, :, :]).then_inc(vc_step, 1)
                        if n < 2:
                            pool.wait_ge(vc_step, t * VC_STEPS + 2 * n + 1)
                            pool.tensor_tensor(vc[:, :, :], vc[:, :, :], vparts[:, :, n, :], ALU.subtract).then_inc(vc_step, 1)

            @block.tensor
            def _(pe):
                def ada_product(c):
                    if c == 0:
                        pe.wait_ge(silu_done, 1)
                    pe.wait_ge(w_loaded[c % 2], (c // 2 + 1) * 16)
                    if c >= 2:
                        pe.wait_ge(ada_read, c - 1)
                    for k in range(KT):
                        mm = pe.matmul(ada_acc[0:2, c % 2], silu[:, k, :], w[:, c % 2, k], start=k == 0, stop=k == KT - 1)
                    mm.then_inc(ada_done, 1)

                ada_product(0)
                pe.wait_ge(table_lo, 1)
                def terms(jp, m, i):
                    for ri in range(2):
                        for a, b in PASSES:
                            mm = pe.matmul(acc[:, m, :], table[a][:, ri, i, m * P:(m + 1) * P],
                                           ys[b][:, i, ri, 2 * jp:2 * jp + 2, :].rearrange("p j c -> p (j c)"),
                                           start=(i, ri, a, b) == (0, 0, HI, HI), stop=(i, ri, a, b) == (R - 1, 1, LO, HI))
                    if i == R - 1:
                        mm.then_inc(acc_done, 1)

                def turn_past(t):
                    if t == 0:
                        pe.wait_ge(ident_loaded, 16)
                    pe.wait_ge(kc_loaded, (t + 1) * 16)
                    if t:
                        pe.wait_ge(kc_lo, t)
                    for m in range(D_C // P):
                        mm = pe.transpose(kps[:, m, :], kc[:, m * P:(m + 1) * P], ident[:, :])
                    mm.then_inc(kc_turned, 1)

                for i in range(R):
                    pe.wait_ge(y_lo, i + 1)
                    for m in range(R):
                        if i == 0:
                            pe.wait_ge(acc_read, m + 1)
                        terms(0, m, i)
                    ada_product(i + 1)
                turn_past(0)
                for m in range(R):
                    pe.wait_ge(acc_read, R + m + 1)
                    for i in range(R):
                        terms(1, m, i)
                    if m < R - 1:
                        ada_product(R + m + 1)
                        turn_past(m + 1)
                pe.wait_ge(xc_loaded, 32)
                for t in range(2):
                    pe.wait_ge(acc_read, UNITS + t + 1)
                    for h in range(2):
                        for n, (i, ri) in enumerate(((0, 0), (0, 1), (1, 0), (1, 1))):
                            mm = pe.matmul(acc[:, t, h * P:(h + 1) * P], ctab[:, ri, i, t * P:(t + 1) * P],
                                           xc[:, i, (2 * h + ri) * P:(2 * h + ri + 1) * P], start=n == 0, stop=n == 3)
                    mm.then_inc(acc_done, 1)


class OutOperands:

    def __init__(self, nc, ctx, w_out):
        sb, _, sem = phase_tools(nc, ctx)
        self.w = [sb(f"out_w{h}", [P, KT, D], F32R, side="right") for h in (HI, LO)]
        self.stage = sb("out_w_stage", [P, 2, D], side="right")
        self.tiles = w_out.rearrange("l (k p) n -> (l k) p n", p=P)
        self.staged = [sem(f"out_w_staged{s}") for s in range(2)]
        self.w_hi, self.w_lo = sem("out_w_hi"), sem("out_w_lo")


def attention_phase(nc, q_t, k_t, v_parts, rel_bias, col_mask_in, row_mask_in, ident_in, y, wo):
    TILES, EDGES, INNER = 18, 4, 12
    EDGE_T = (0, 1, 14, 15)
    WIN, WIN_IN = 8 * GRID, 9 * GRID
    KCOLS = T_ALL + T_PAST
    VT = KCOLS // P
    VT_CTX, VT_PAST = T_LAT // P, T_ALL // P
    E_ROWS = 14
    with ExitStack() as ctx:
        sb, ps, sem = phase_tools(nc, ctx)
        ident = sb("at_ident", [P, P])
        col_mask = sb("at_col_mask", [P, GRID])
        row_mask = sb("at_row_mask", [P, WIN_IN])
        qs = sb("at_q", [P, 2, T_ALL], F32R)
        bin_ = sb("at_bias_in", [P, E_ROWS, GRID])
        k = [sb(f"at_k{h}", [P, 2, KCOLS], F32R) for h in (HI, LO)]
        vp = sb("at_v_parts", [P, 2, VT, 3, HD], BF16)
        ebias = sb("at_edge_bias", [P, 2, E_ROWS, GRID])
        ibias = sb("at_inner_bias", [P, 2, WIN_IN])
        sl = sb("at_local_scores", [P, 2, WIN_IN])
        prob = sb("at_prob", [P, 2, WIN_IN + T_PAST])
        ph = sb("at_prob_hi", [P, 2, 9, P], FP16)
        pl = sb("at_prob_lo", [P, 2, 9, P], FP16)
        ncmax = sb("at_neg_context_max", [P, 2])
        lmax = sb("at_local_max", [P, 2])
        nmx = sb("at_neg_max", [P, 2])
        sums = sb("at_sums", [P, 3, 2])
        den = sb("at_den", [P, 3])
        rden = sb("at_rden", [P, 3])
        minus_one = sb("at_minus_one", [P, 1])
        osum = sb("at_osum", [P, 2, HD])
        out = sb("at_out", [P, 2, TILES, HD])
        loc_ps = ps("at_loc_ps", [P, 2, 512])
        ctx_ps = ps("at_ctx_ps", [P, 2, 512])
        ta_ps = ps("at_ta_ps", [P, 4, P])
        tb_ps = ps("at_tb_ps", [P, 4, P])
        th_ps = ps("at_th_ps", [P, 512])
        o_ps = ps("at_o_ps", [P, 2, 256])

        consts_loaded, minus_one_done = sem("at_consts_loaded"), sem("at_minus_one_done")
        qk_loaded = [sem(f"at_qk_loaded{s}") for s in range(2)]
        first_loaded, second_loaded, context_loaded = sem("at_first_loaded"), sem("at_second_loaded"), sem("at_context_loaded")
        v_loaded = [sem(f"at_v_loaded{s}") for s in range(2)]
        bias_loaded, ebias_done, bias_ready = sem("at_bias_loaded"), sem("at_ebias_done"), sem("at_bias_ready")
        qk_done = sem("at_qk_done")
        cmax_done, smax_done, nmax_done, exp_done = sem("at_cmax_done"), sem("at_smax_done"), sem("at_nmax_done"), sem("at_exp_done")
        exp_local_done, lo_a = sem("at_exp_local_done"), sem("at_lo_a")
        ta_done, tb_done, hi_a, hi_b, lo_done = sem("at_ta_done"), sem("at_tb_done"), sem("at_hi_a"), sem("at_hi_b"), sem("at_lo_done")
        pv_done, den_done, rden_done, o_read, out_done = (
            sem("at_pv_done"), sem("at_den_done"), sem("at_rden_done"), sem("at_o_read"), sem("at_out_done"))
        stored = [sem(f"at_stored{s}") for s in range(2)]

        v_tiles = v_parts.rearrange("(n p) c -> p n c", p=P)
        y_tiles = y.rearrange("(n p) c -> p n c", p=P)
        DMAS_QK = 6
        BIAS_POS = 11

        def kind(pos):
            if EDGES <= pos < EDGES + INNER:
                return (pos - EDGES) * P, WIN_IN, (pos - EDGES + 2) * P
            if pos < EDGES:
                return (0 if pos < 2 else T_LAT - WIN), WIN, EDGE_T[pos] * P
            return None, 0, T_LAT + (pos - EDGES - INNER) * P

        def every_tile(eng, body):
            def one_head(h, parity, first, last):
                for p in range(TILES):
                    before = (h, parity, p - 1) if p else (None if first else (h - 1, 1 - parity, TILES - 1))
                    after = (h, parity, p + 1) if p < TILES - 1 else (None if last else (h + 1, 1 - parity, 0))
                    body(before, (h, parity, p), after)

            one_head(0, 0, True, False)
            with eng.Fori(0, (HEADS - 2) // 2) as i:
                for s in range(2):
                    one_head(i * 2 + (1 + s), 1 - s, False, False)
            one_head(HEADS - 1, 1, False, True)

        with nc.Block() as block:
            @block.sync
            def _(sp):
                sp.sem_inc(stored[0], 16)
                sp.sem_inc(stored[1], 16)
                sp.dma_start(ident[:, :], ident_in).then_inc(consts_loaded, 16)
                sp.dma_start(col_mask[:, :], col_mask_in).then_inc(consts_loaded, 16)
                sp.dma_start(row_mask[:, :], row_mask_in).then_inc(consts_loaded, 16)

                def load_qk(h, parity, done, k_cols, q_cols):
                    rows = bass.ds(h * HD, HD)
                    for half in range(2):
                        at = slice(half * HD, (half + 1) * HD)
                        for cols in k_cols:
                            for part in (HI, LO):
                                sp.dma_start(k[part][at, parity, cols].bitcast(F32), k_t[part, rows, cols]).then_inc(done, 16)
                        sp.dma_start(qs[at, parity, q_cols].bitcast(F32), q_t[half, rows, q_cols]).then_inc(done, 16)

                def load_v(h, parity):
                    sp.dma_start(vp[:, parity].rearrange("p t n d -> p t (n d)"),
                                 v_tiles[:, :, bass.ds(h * (3 * HD), 3 * HD)]).then_inc(v_loaded[parity], 16)

                def load_bias(h):
                    for half in range(2):
                        src = rel_bias[:, bass.ds(h * REL_ROWS + (1 - half), E_ROWS), :]
                        sp.dma_start(bin_[half * HD:(half + 1) * HD, :, :], src).then_inc(bias_loaded, 16)

                load_qk(0, 0, first_loaded, (slice(0, WIN), slice(T_ALL, KCOLS)), slice(0, 2 * P))
                load_bias(0)
                load_qk(0, 0, second_loaded, (slice(T_LAT - WIN, T_LAT),), slice(T_LAT - 2 * P, T_LAT))
                load_v(0, 0)
                load_qk(0, 0, qk_loaded[0], (slice(WIN, T_LAT - WIN),), slice(2 * P, T_LAT - 2 * P))
                load_qk(0, 0, context_loaded, (slice(T_LAT, T_ALL),), slice(T_LAT, T_ALL))

                def one_head(h, parity, last):
                    if not last:
                        sp.wait_ge(pv_done, h * TILES + 2)
                        load_qk(h + 1, 1 - parity, qk_loaded[1 - parity], (slice(0, KCOLS),), slice(0, T_ALL))
                        load_v(h + 1, 1 - parity)
                        sp.wait_ge(bias_ready, h + 1)
                        load_bias(h + 1)
                    sp.wait_ge(wo.w_lo, h + 1)
                    sp.dma_start(wo.stage[:, parity, :], wo.tiles[h]).then_inc(wo.staged[parity], 16)
                    sp.wait_ge(out_done, (h + 1) * TILES)
                    sp.dma_start(y_tiles[:, :, bass.ds(h * HD + (D_A + D_B), HD)], out[:, parity]).then_inc(stored[parity], 16)

                with sp.Fori(0, HEADS // 2 - 1) as i:
                    for s in range(2):
                        one_head(i * 2 + s, s, False)
                one_head(HEADS - 2, 0, False)
                one_head(HEADS - 1, 1, True)
                for s in range(2):
                    sp.wait_ge(stored[s], 16 * (HEADS // 2 + 1))

            @block.gpsimd
            def _(pool):
                pool.memset(minus_one[:, :], -1.0).then_inc(minus_one_done, 1)
                pool.wait_ge(minus_one_done, 1)
                pool.wait_ge(consts_loaded, 48)

                def edge_bias(h, parity):
                    pool.wait_ge(bias_loaded, (h + 1) * 32)
                    pool.tensor_tensor(ebias[:, parity], bin_[:, :, :],
                                       col_mask[:, :].unsqueeze(1).to_broadcast([P, E_ROWS, GRID]), ALU.add).then_inc(ebias_done, 1)

                def inner_bias(h, parity):
                    pool.wait_ge(ebias_done, h + 1)
                    pool.tensor_tensor(ibias[:, parity, :], ebias[:, parity, 2:11, :].rearrange("p e c -> p (e c)"),
                                       row_mask[:, :], ALU.add).then_inc(bias_ready, 1)

                def step(before, tile, after):
                    h, parity, pos = tile
                    u, n = h * TILES + pos, pos % 3
                    pool.wait_ge(exp_done, u + 3)
                    if kind(pos)[1]:
                        pool.tensor_tensor(den[:, n:n + 1], sums[:, n, 0:1], sums[:, n, 1:2], ALU.add).then_inc(den_done, 1)
                        pool.wait_ge(den_done, h * (EDGES + INNER) + pos + 1)
                        pool.tensor_tensor(rden[:, n:n + 1], den[:, n:n + 1], minus_one[:, :], ALU.pow).then_inc(rden_done, 1)
                    else:
                        pool.tensor_tensor(rden[:, n:n + 1], sums[:, n, 1:2], minus_one[:, :], ALU.pow).then_inc(rden_done, 1)
                    if not (isinstance(h, int) and h == HEADS - 1):
                        if pos == BIAS_POS:
                            edge_bias(h + 1, 1 - parity)
                        if pos == BIAS_POS + 3:
                            inner_bias(h + 1, 1 - parity)

                edge_bias(0, 0)
                inner_bias(0, 0)
                every_tile(pool, step)

            @block.tensor
            def _(pe):
                pe.sem_inc(qk_done, 2)
                pe.sem_inc(pv_done, 2)
                pe.wait_ge(consts_loaded, 48)

                def head_uses(h, parity):
                    return (h - parity) // 2 + 1 if isinstance(h, int) else ((h - parity) >> 1) + 1

                def qk(tile):
                    h, parity, pos = tile
                    s, inner = pos % 2, EDGES <= pos < EDGES + INNER
                    u = h * TILES + pos
                    if isinstance(h, int) and h == 0:
                        if pos == 0:
                            pe.wait_ge(first_loaded, 160)
                        if pos == 2:
                            pe.wait_ge(second_loaded, 96)
                        if pos == EDGES:
                            pe.wait_ge(qk_loaded[0], 16 * DMAS_QK)
                        if pos == EDGES + INNER:
                            pe.wait_ge(context_loaded, 96)
                    elif pos == 0:
                        pe.wait_ge(qk_loaded[parity], head_uses(h, parity) * (16 * DMAS_QK))
                    pe.wait_ge(nmax_done, u)
                    pe.wait_ge(exp_done, u + 1)
                    key0, n, token = kind(pos)
                    q = qs[:, parity, token:token + P]
                    for c in range(2 if n else 0):
                        w = n // 2
                        for b in (HI, LO):
                            pe.matmul(loc_ps[:, c, 0:w], q, k[b][:, parity, key0 + c * w:key0 + (c + 1) * w],
                                      start=b == HI, stop=b == LO)
                    col, w = (T_ALL, T_PAST) if n else (T_LAT, T_CTX)
                    for b in (HI, LO):
                        mm = pe.matmul(ctx_ps[:, s, 0:w], q, k[b][:, parity, col:col + w], start=b == HI, stop=b == LO)
                    mm.then_inc(qk_done, 1)

                def turn(tile):
                    h, parity, pos = tile
                    s, inner = pos % 2, EDGES <= pos < EDGES + INNER
                    u = h * TILES + pos
                    n = kind(pos)[1]
                    if n:
                        n_loc = h * (EDGES + INNER) + pos
                        pe.wait_ge(exp_local_done, n_loc + 1)
                        if not (isinstance(h, int) and h == 0 and pos == 0):
                            pe.wait_ge(lo_a, n_loc)
                        for b in range(4):
                            mm = pe.transpose(ta_ps[:, b, :], prob[:, s, b * P:(b + 1) * P], ident[:, :])
                        mm.then_inc(ta_done, 1)
                    pe.wait_ge(exp_done, u + 3)
                    pe.wait_ge(lo_done, u)
                    for b in range(4 if n else 2):
                        if inner and b == 1:
                            pe.transpose(th_ps[0:GRID, 0:P], prob[:, s, 4 * P:4 * P + GRID], ident[:, :])
                        mm = pe.transpose(tb_ps[:, b, :], prob[:, s, n + b * P:n + (b + 1) * P], ident[:, :])
                    mm.then_inc(tb_done, 1)

                def pv(tile):
                    h, parity, pos = tile
                    s, inner = pos % 2, EDGES <= pos < EDGES + INNER
                    u = h * TILES + pos
                    if pos == 0:
                        pe.wait_ge(v_loaded[parity], head_uses(h, parity) * 16)
                    pe.wait_ge(lo_done, u + 1)
                    pe.wait_ge(o_read, u + 2)
                    key0, n, _ = kind(pos)
                    vt = key0 // P if n else None
                    blocks = [(b, vt + b, P) for b in range(4)] if n else []
                    if inner:
                        blocks.append((8, vt + 4, GRID))
                    blocks += [(4 + b, (VT_PAST if n else VT_CTX) + b, P) for b in range(4 if n else 2)]
                    for i, (b, v, rows) in enumerate(blocks):
                        for part, width in ((ph, 3), (pl, 2)):
                            mm = pe.matmul(o_ps[:, s, 0:width * HD], part[0:rows, s, b, :],
                                           vp[0:rows, parity, v, 0:width, :].rearrange("p n d -> p (n d)"),
                                           start=i == 0 and width == 3, stop=i == len(blocks) - 1 and width == 2)
                    mm.then_inc(pv_done, 1)

                def step(before, tile, after):
                    if after is not None:
                        qk(after)
                    turn(tile)
                    if before is not None:
                        pv(before)

                qk((0, 0, 0))
                every_tile(pe, step)
                pv((HEADS - 1, 1, TILES - 1))

            @block.vector
            def _(dve):
                dve.sem_inc(o_read, 2)
                dve.sem_inc(wo.w_lo, 2)
                dve.wait_ge(consts_loaded, 48)

                def row_max(tile):
                    h, parity, pos = tile
                    s, inner = pos % 2, EDGES <= pos < EDGES + INNER
                    u = h * TILES + pos
                    key0, n, _ = kind(pos)
                    if pos == 0:
                        dve.wait_ge(bias_ready, h + 1)
                    dve.wait_ge(qk_done, u + 3)
                    w = T_PAST if n else T_CTX
                    if n:
                        if inner:
                            bias = ibias[:, parity, :]
                        else:
                            e0 = (0 if pos < 2 else GRID // 2 - 8) - 2 * EDGE_T[pos] + 7 - 1
                            bias = ebias[:, parity, e0:e0 + 8, :].rearrange("p e c -> p (e c)")
                    dve.tensor_reduce(ncmax[:, s:s + 1], ctx_ps[:, s, 0:w], AX_X, ALU.max, negate=True).then_inc(cmax_done if n else nmax_done, 1)
                    if n:
                        dve.tensor_tensor_reduce(sl[:, s, 0:n].rearrange("p (a c) -> p a c", a=2), loc_ps[:, :, 0:n // 2],
                                                 bias.rearrange("p (a c) -> p a c", a=2), 1.0, 2 * MASKED,
                                                 ALU.add, ALU.max, lmax[:, s:s + 1]).then_inc(smax_done, 1)
                        dve.wait_ge(smax_done, h * (EDGES + INNER) + pos + 1)
                        dve.scalar_tensor_tensor(nmx[:, s:s + 1], lmax[:, s:s + 1], -1.0, ncmax[:, s:s + 1],
                                                 ALU.mult, ALU.min).then_inc(nmax_done, 1)

                def low_part(tile):
                    h, parity, pos = tile
                    s, inner = pos % 2, EDGES <= pos < EDGES + INNER
                    u = h * TILES + pos
                    n = kind(pos)[1]
                    if n:
                        dve.wait_ge(hi_a, h * (EDGES + INNER) + pos + 1)
                        dve.tensor_tensor(pl[:, s, 0:4, :], ta_ps[:, :, :], ph[:, s, 0:4, :], ALU.subtract).then_inc(lo_a, 1)
                    dve.wait_ge(hi_b, u + 1)
                    if inner:
                        dve.tensor_tensor(pl[0:GRID, s, 8, :], th_ps[0:GRID, 0:P], ph[0:GRID, s, 8, :], ALU.subtract)
                    b = 4 if n else 2
                    dve.tensor_tensor(pl[:, s, 4:4 + b, :], tb_ps[:, 0:b, :], ph[:, s, 4:4 + b, :], ALU.subtract).then_inc(lo_done, 1)

                def finish(tile):
                    h, parity, pos = tile
                    s, inner = pos % 2, EDGES <= pos < EDGES + INNER
                    u = h * TILES + pos
                    dve.wait_ge(pv_done, u + 3)
                    dve.tensor_reduce(osum[:, s, :], o_ps[:, s, 0:3 * HD].rearrange("p (n d) -> p d n", n=3), AX_X, ALU.add).then_inc(o_read, 1)

                def step(before, tile, after):
                    if after is not None:
                        row_max(after)
                    low_part(tile)
                    if before is not None:
                        finish(before)
                    h, parity, pos = tile
                    if pos == TILES - 1:
                        dve.wait_ge(wo.w_hi, h + 1)
                        dve.tensor_tensor(wo.w[LO][:, h, :], wo.stage[:, parity, :], wo.w[HI][:, h, :].bitcast(F32),
                                          ALU.subtract).then_inc(wo.w_lo, 1)

                row_max((0, 0, 0))
                every_tile(dve, step)
                dve.wait_ge(out_done, HEADS * TILES - 2)
                finish((HEADS - 1, 1, TILES - 1))

            @block.scalar
            def _(act):
                act.sem_inc(exp_done, 2)
                act.wait_ge(consts_loaded, 48)

                def exps(tile):
                    h, parity, pos = tile
                    s, inner = pos % 2, EDGES <= pos < EDGES + INNER
                    u = h * TILES + pos
                    n = kind(pos)[1]
                    act.wait_ge(nmax_done, u + 1)
                    nmax = (nmx if n else ncmax)[:, s:s + 1]
                    if n:
                        act.activation(prob[:, s, 0:n], sl[:, s, 0:n], ACT.Exp, bias=nmax,
                                       accum_out=sums[:, pos % 3, 0:1]).then_inc(exp_local_done, 1)
                    w = T_PAST if n else T_CTX
                    act.activation(prob[:, s, n:n + w], ctx_ps[:, s, 0:w], ACT.Exp, bias=nmax,
                                   accum_out=sums[:, pos % 3, 1:2]).then_inc(exp_done, 1)

                def high_part(tile):
                    h, parity, pos = tile
                    s, inner = pos % 2, EDGES <= pos < EDGES + INNER
                    u = h * TILES + pos
                    n = kind(pos)[1]
                    act.wait_ge(pv_done, u + 1)
                    if n:
                        act.wait_ge(ta_done, h * (EDGES + INNER) + pos + 1)
                        act.copy(ph[:, s, 0:4, :], ta_ps[:, :, :]).then_inc(hi_a, 1)
                    act.wait_ge(tb_done, u + 1)
                    if inner:
                        act.copy(ph[0:GRID, s, 8, :], th_ps[0:GRID, 0:P])
                    b = 4 if n else 2
                    act.copy(ph[:, s, 4:4 + b, :], tb_ps[:, 0:b, :]).then_inc(hi_b, 1)

                def divide(tile):
                    h, parity, pos = tile
                    s, u = pos % 2, h * TILES + pos
                    if pos == 0:
                        act.wait_ge(stored[parity], (h - parity) * 8 + 16)
                    act.wait_ge(rden_done, u + 1)
                    act.wait_ge(o_read, u + 3)
                    act.activation(out[:, parity, kind(pos)[2] // P, :], osum[:, s, :], ACT.Copy,
                                   scale=rden[:, pos % 3:pos % 3 + 1]).then_inc(out_done, 1)

                def two_before(tile):
                    h, parity, pos = tile
                    if pos >= 2:
                        return h, parity, pos - 2
                    return None if isinstance(h, int) and h == 0 else (h - 1, 1 - parity, TILES - 2 + pos)

                def step(before, tile, after):
                    h, parity, pos = tile
                    if pos == TILES - 2:
                        act.wait_ge(wo.staged[parity], (h - parity) * 8 + 16)
                    exps(tile)
                    high_part(tile)
                    if pos == TILES - 2:
                        act.copy(wo.w[HI][:, h, :], wo.stage[:, parity, :]).then_inc(wo.w_hi, 1)
                    if two_before(tile) is not None:
                        divide(two_before(tile))

                every_tile(act, step)
                for pos in (TILES - 2, TILES - 1):
                    divide((HEADS - 1, 1, pos))


class UpOperands:
    PIECE = 256

    def __init__(self, nc, ctx, h2_t, w_gu):
        sb, _, sem = phase_tools(nc, ctx)
        self.w = [sb(f"up_w{h}", [P, 2, KT, self.PIECE], F32R) for h in (HI, LO)]
        self.stage = sb("up_stage", [P, 2, KT, self.PIECE])
        self.staged = [sem(f"up_staged{s}") for s in range(2)]
        self.part_hi, self.part_lo = sem("up_part_hi"), sem("up_part_lo")
        self.w_cols = w_gu.rearrange("l (k p) (h f c) -> (l h f) p k c", p=P, h=2, c=P)
        self.h_tiles = h2_t.rearrange("(k p) t -> p k t", p=P)

    def load_w(self, eng, f, slot):
        for h in range(2):
            eng.dma_start(self.stage[:, slot, :, h * P:(h + 1) * P], self.w_cols[h * FT + f]).then_inc(self.staged[slot], 16)

    def load_h(self, eng, n, slot):
        for h in range(2):
            ks = slice(h * KT // 2, (h + 1) * KT // 2)
            eng.dma_start(self.stage[:, slot, ks, :],
                          self.h_tiles[:, ks, n * self.PIECE:(n + 1) * self.PIECE]).then_inc(self.staged[slot], 16)

    def high(self, act, n, slot, dst):
        act.wait_ge(self.staged[slot], (n - slot) * 16 + 32)
        act.copy(dst, self.stage[:, slot, :, :]).then_inc(self.part_hi, 1)

    def low(self, dve, n, slot, dst, hi):
        dve.wait_ge(self.part_hi, n + 1)
        dve.tensor_tensor(dst, self.stage[:, slot, :, :], hi.bitcast(F32), ALU.subtract).then_inc(self.part_lo, 1)


def mix_phase(nc, y, x_all, w, ln1_g, ln1_b, mod, ident_in, x1, h2_t, up):
    N = T_ALL // P
    N_LAT = T_LAT // P
    HALVES = D // 512
    with ExitStack() as ctx:
        sb, ps, sem = phase_tools(nc, ctx)
        yb = sb("mx_y", [P, 2, D])
        xb = sb("mx_x", [P, 2, D])
        yt = [sb(f"mx_yt{h}", [P, 2, KT, P], F32R) for h in (HI, LO)]
        res = sb("mx_res", [P, 2, D])
        x1b = sb("mx_x1", [P, 2, D])
        xn = sb("mx_xn", [P, 2, D])
        hst = sb("mx_h_stage", [P, 2, KT, P])
        gate = sb("mx_gate", [P, 2, D])
        ln_g = sb("mx_ln_g", [P, D])
        ln_b = sb("mx_ln_b", [P, D])
        shift = sb("mx_shift", [P, 2, KT])
        scale = sb("mx_scale", [P, 2, KT])
        scale1p = sb("mx_scale1p", [P, 2, KT])
        ident = sb("mx_ident", [P, P])
        stats = sb("mx_stats", [P, 2, 12])
        mv = sb("mx_mv", [P, 2, 2])
        veps = sb("mx_veps", [P, 2])
        rstd = sb("mx_rstd", [P, 2])
        waited = sb("mx_waited", [P, 2])
        minus_half = sb("mx_minus_half", [P, 1])
        eps = sb("mx_eps", [P, 1])
        acc = ps("mx_acc", [P, 2, D])
        yps = ps("mx_yps", [P, KT, P])
        hps = ps("mx_hps", [P, KT, P])

        consts_loaded, half_done, scale_done = sem("mx_consts_loaded"), sem("mx_half_done"), sem("mx_scale_done")
        y_loaded = [sem(f"mx_y_loaded{s}") for s in range(2)]
        x_loaded = [sem(f"mx_x_loaded{s}") for s in range(2)]
        y_turned, y_hi, y_lo = sem("mx_y_turned"), sem("mx_y_hi"), sem("mx_y_lo")
        acc_done, gated, res_done = sem("mx_acc_done"), sem("mx_gated"), sem("mx_res_done")
        stats_done = [sem(f"mx_stats_done{n}") for n in range(2)]
        mv_done = [sem(f"mx_mv_done{n}") for n in range(2)]
        veps_done = [sem(f"mx_veps_done{n}") for n in range(2)]
        rstd_done = [sem(f"mx_rstd_done{n}") for n in range(2)]
        normed, scaled, x1_done, h_turned, h_done = sem("mx_normed"), sem("mx_scaled"), sem("mx_x1_done"), sem("mx_h_turned"), sem("mx_h_done")
        x1_stored = [sem(f"mx_x1_stored{s}") for s in range(2)]
        h_stored = [sem(f"mx_h_stored{s}") for s in range(2)]
        N_CONSTS = 9

        tiles = lambda ap: ap.rearrange("(t p) d -> t p d", p=P)
        y_tiles, x_tiles, x1_tiles = tiles(y), tiles(x_all), tiles(x1)
        h_tiles = h2_t.rearrange("(k p) t -> p k t", p=P)
        use = lambda t, s: (t - s) * 8

        def every_tile(body, after_second=lambda: None):
            def loop(eng):
                body(0, 0, LAT)
                body(1, 1, LAT)
                after_second()
                with eng.Fori(0, (N_LAT - 2) // 2) as i:
                    for s in range(2):
                        body(i * 2 + (2 + s), s, LAT)
                for t in range(N_LAT, N):
                    body(t, t % 2, CTX)
            return loop

        last_tile = lambda t: isinstance(t, int) and t == N - 1
        first = lambda t, n: isinstance(t, int) and t < n

        with nc.Block() as block:
            @block.sync
            def _(sp):
                for s in range(2):
                    sp.sem_inc(x1_stored[s], 16)
                sp.dma_start(ident[:, :], ident_in).then_inc(consts_loaded, 16)
                for t in range(2):
                    sp.dma_start(yb[:, t, :], y_tiles[t]).then_inc(y_loaded[t], 16)
                with nc.allow_non_contiguous_dma(reason="modulation, channel on partition"):
                    for v in range(2):
                        for dst, what in ((shift, SHIFT2), (scale, SCALE2)):
                            sp.dma_start(dst[:, v, :], mod[v, what * D:(what + 1) * D].rearrange("(k p) -> p k", p=P)).then_inc(consts_loaded, 16)
                        sp.dma_start(gate[:, v, :], mod[v, GATE1 * D:(GATE1 + 1) * D].partition_broadcast(P)).then_inc(consts_loaded, 16)
                sp.dma_start(ln_g[:, :], ln1_g[0].partition_broadcast(P)).then_inc(consts_loaded, 16)
                sp.dma_start(ln_b[:, :], ln1_b[0].partition_broadcast(P)).then_inc(consts_loaded, 16)
                for t in range(2):
                    sp.dma_start(xb[:, t, :], x_tiles[t]).then_inc(x_loaded[t], 16)

                def store_x1(t, s):
                    sp.wait_ge(x1_done, t + 1)
                    sp.dma_start(x1_tiles[t], x1b[:, s, :]).then_inc(x1_stored[s], 16)

                def tile(t, s, vec):
                    if not isinstance(t, int) or t + 2 < N:
                        sp.wait_ge(y_turned, t + 1)
                        sp.dma_start(yb[:, s, :], y_tiles[t + 2]).then_inc(y_loaded[s], 16)
                    if not first(t, 1):
                        store_x1(t - 1, 1 - s)
                    if not isinstance(t, int) or t + 2 < N:
                        sp.wait_ge(res_done, t + 1)
                        sp.dma_start(xb[:, s, :], x_tiles[t + 2]).then_inc(x_loaded[s], 16)

                up.load_w(sp, 0, 0)
                every_tile(tile)(sp)
                for s in range(2):
                    sp.wait_ge(h_stored[s], 48)
                up.load_h(sp, 0, 1)
                sp.wait_ge(up.part_lo, 1)
                up.load_h(sp, 1, 0)
                store_x1(N - 1, 1)
                for s in range(2):
                    sp.wait_ge(x1_stored[s], 16 * (N // 2 + 1))
                    sp.wait_ge(h_stored[s], 16 * (N // 2 + 1))

            @block.gpsimd
            def _(pool):
                pool.memset(minus_half[:, :], -0.5).then_inc(half_done, 1)
                pool.memset(eps[:, :], EPS).then_inc(half_done, 1)
                pool.wait_ge(half_done, 2)

                def make_rstd(t, n):
                    pool.wait_ge(mv_done[n], t + 1)
                    pool.tensor_tensor(veps[:, n:n + 1], mv[:, n, 1:2], eps[:, :], ALU.add).then_inc(veps_done[n], 1)
                    pool.wait_ge(veps_done[n], t + 1)
                    pool.tensor_tensor(rstd[:, n:n + 1], veps[:, n:n + 1], minus_half[:, :], ALU.pow).then_inc(rstd_done[n], 1)

                def tile(t, s, vec):
                    make_rstd(t, 0)
                    if not first(t, 1):
                        make_rstd(t - 1, 1)

                every_tile(tile)(pool)
                make_rstd(N - 1, 1)

            @block.tensor
            def _(pe):
                pe.sem_inc(gated, 2)
                pe.wait_ge(consts_loaded, 16)

                def turn_y(t, s):
                    pe.wait_ge(y_loaded[s], use(t, s) + 16)
                    if not first(t, 1):
                        pe.wait_ge(y_lo, t)
                    for k in range(KT):
                        mm = pe.transpose(yps[:, k, :], yb[:, s, k * P:(k + 1) * P], ident[:, :])
                    mm.then_inc(y_turned, 1)

                def product(t, s):
                    pe.wait_ge(y_lo, t + 1)
                    pe.wait_ge(gated, t + 1)
                    for half in range(HALVES):
                        for k in range(KT):
                            for a, b in PASSES:
                                mm = pe.matmul(acc[:, s, half * 512:(half + 1) * 512], yt[a][:, s, k, :],
                                               w[b][:, k, half * 512:(half + 1) * 512],
                                               start=(k, a, b) == (0, HI, HI), stop=(k, a, b) == (KT - 1, LO, HI))
                    mm.then_inc(acc_done, 1)

                def turn_h(t, s):
                    pe.wait_ge(normed, t + 1)
                    if not first(t, 1):
                        pe.wait_ge(h_done, t)
                    for k in range(KT):
                        mm = pe.transpose(hps[:, k, :], xn[:, s, k * P:(k + 1) * P], ident[:, :])
                    mm.then_inc(h_turned, 1)

                def tile(t, s, vec):
                    if not last_tile(t):
                        turn_y(t + 1, 1 - s)
                    product(t, s)
                    if not first(t, 2):
                        turn_h(t - 2, s)

                turn_y(0, 0)
                every_tile(tile)(pe)
                turn_h(N - 2, 0)
                turn_h(N - 1, 1)

            @block.scalar
            def _(act):
                for s in range(2):
                    act.sem_inc(h_stored[s], 16)
                act.wait_ge(y_turned, 1)
                act.copy(yt[HI][:, 0, :, :], yps[:, :, :]).then_inc(y_hi, 1)

                def round_y(t, s):
                    act.wait_ge(y_turned, t + 1)
                    if not first(t, 2):
                        act.wait_ge(acc_done, t - 1)
                    act.copy(yt[HI][:, s, :, :], yps[:, :, :]).then_inc(y_hi, 1)

                def modulate(t, s, vec):
                    act.wait_ge(h_turned, t + 1)
                    act.wait_ge(h_stored[s], use(t, s) + 16)
                    for k in range(KT):
                        last = act.activation(hst[:, s, k, :], hps[:, k, :], ACT.Identity,
                                              bias=shift[:, vec, k:k + 1], scale=scale1p[:, vec, k:k + 1])
                    last.then_inc(h_done, 1)
                    act.wait_ge(h_done, t + 1)
                    act.dma_start(h_tiles[:, :, bass.ds(t * P, P)], hst[:, s, :, :]).then_inc(h_stored[s], 16)

                def tile(t, s, vec):
                    if not last_tile(t):
                        round_y(t + 1, 1 - s)
                    if not first(t, 2):
                        modulate(t - 2, s, LAT)

                act.wait_ge(scale_done, 1)
                every_tile(tile, lambda: up.high(act, 0, 0, up.w[HI][:, 0, :, :]))(act)
                modulate(N - 2, 0, CTX)
                modulate(N - 1, 1, CTX)

            @block.vector
            def _(dve):
                def low_y(t, s):
                    dve.wait_ge(y_hi, t + 1)
                    dve.tensor_tensor(yt[LO][:, s, :, :], yps[:, :, :], yt[HI][:, s, :, :].bitcast(F32), ALU.subtract).then_inc(y_lo, 1)

                low_y(0, 0)
                dve.wait_ge(consts_loaded, 16 * N_CONSTS)
                dve.tensor_scalar(scale1p[:, :, :], scale[:, :, :], 1.0, None, ALU.add).then_inc(scale_done, 1)

                def statistics(t, n, src):
                    for half in range(HALVES):
                        last = dve.bn_stats(stats[:, n, half * 6:half * 6 + 6], src[:, half * 512:(half + 1) * 512])
                    last.then_inc(stats_done[n], 1)
                    dve.wait_ge(stats_done[n], t + 1)
                    dve.tensor_copy(waited[:, n:n + 1], stats[:, n, 0:1])
                    dve.bn_aggr(mv[:, n, :], stats[:, n, :]).then_inc(mv_done[n], 1)

                def affine_norm(t, s):
                    dve.wait_ge(mv_done[0], t + 1)
                    dve.scalar_tensor_tensor(res[:, s, :], res[:, s, :], mv[:, 0, 0:1], ln_g[:, :], ALU.subtract, ALU.mult).then_inc(scaled, 1)
                    dve.wait_ge(scaled, t + 1)
                    dve.wait_ge(rstd_done[0], t + 1)
                    dve.wait_ge(x1_stored[s], use(t, s) + 16)
                    dve.scalar_tensor_tensor(x1b[:, s, :], res[:, s, :], rstd[:, 0:1], ln_b[:, :], ALU.mult, ALU.add).then_inc(x1_done, 1)

                def second_statistics(t, s):
                    dve.wait_ge(x1_done, t + 1)
                    statistics(t, 1, x1b[:, s, :])

                def second_norm(t, s):
                    if not first(t, 2):
                        dve.wait_ge(h_turned, t - 1)
                    dve.wait_ge(rstd_done[1], t + 1)
                    dve.tensor_scalar(xn[:, s, :], x1b[:, s, :], mv[:, 1, 0:1], rstd[:, 1:2], ALU.subtract, ALU.mult).then_inc(normed, 1)

                def tile(t, s, vec):
                    if not last_tile(t):
                        low_y(t + 1, 1 - s)
                    dve.wait_ge(acc_done, t + 1)
                    dve.tensor_tensor(res[:, s, :], acc[:, s, :], gate[:, vec, :], ALU.mult).then_inc(gated, 1)
                    dve.wait_ge(gated, t + 3)
                    dve.wait_ge(x_loaded[s], use(t, s) + 16)
                    dve.scalar_tensor_tensor(res[:, s, :], xb[:, s, :], ALPHA, res[:, s, :], ALU.mult, ALU.add).then_inc(res_done, 1)
                    dve.wait_ge(res_done, t + 1)
                    statistics(t, 0, res[:, s, :])
                    if not first(t, 1):
                        second_statistics(t - 1, 1 - s)
                    affine_norm(t, s)
                    if not first(t, 1):
                        second_norm(t - 1, 1 - s)

                every_tile(tile, lambda: up.low(dve, 0, 0, up.w[LO][:, 0, :, :], up.w[HI][:, 0, :, :]))(dve)
                second_statistics(N - 1, 1)
                second_norm(N - 1, 1)


def ffn_up_phase(nc, up, conv_w, conv_b, f_t):
    CHUNKS = [(c * 512, 512) for c in range(T_LAT // 512)] + [(T_LAT, T_CTX)]
    NC = len(CHUNKS)
    PIECE = up.PIECE
    H_PIECES = T_ALL // PIECE
    G_LEN = T_ALL + 4
    G_AT = [1 + at for at, _ in CHUNKS[:-1]] + [T_LAT + 3]
    ZEROS = (0, T_LAT + 1, T_LAT + 2, G_LEN - 1)
    BANK = (0, 1, 2, 3, 0)
    SLOT = (0, 1, 2, 0, 1)
    with ExitStack() as ctx:
        sb, ps, sem = phase_tools(nc, ctx)
        ht = [sb(f"fu_ht{h}", [P, KT, T_ALL], F32R) for h in (HI, LO)]
        w, part_lo = up.w, up.part_lo
        grow = sb("fu_g", [P, G_LEN])
        res = sb("fu_result", [P, 3, 512])
        cw = sb("fu_conv_w", [P, 3, FT])
        cb = sb("fu_conv_b", [P, FT])
        gps = ps("fu_gps", [P, 4, 512])
        ups = ps("fu_ups", [P, 4, 512])

        consts_loaded, zeroed = sem("fu_consts_loaded"), sem("fu_zeroed")
        g_done, u_done, g_read, u_read = sem("fu_g_done"), sem("fu_u_done"), sem("fu_g_read"), sem("fu_u_read")
        tap = [sem(f"fu_tap{n}") for n in range(3)]
        silu_done = sem("fu_silu_done")
        stored = [sem(f"fu_stored{s}") for s in range(3)]
        USES = [SLOT.count(s) for s in range(3)]

        def uses(f, c):
            return f * USES[SLOT[c]] + SLOT[:c].count(SLOT[c])

        piece_of = lambda f: H_PIECES + f
        h_pieces = lambda c: 1 + (CHUNKS[c][0] + CHUNKS[c][1]) // PIECE

        def every_tile(eng, body):
            body(0, 0)
            with eng.Fori(0, (FT - 2) // 2) as i:
                for s in range(2):
                    body(i * 2 + (1 + s), 1 - s)
            body(FT - 1, 1)

        def chunk_order(do_g, do_u):
            do_g(0)
            for c in range(NC):
                if c + 1 < NC:
                    do_g(c + 1)
                do_u(c)

        is_first = lambda f: isinstance(f, int) and f == 0
        is_last = lambda f: isinstance(f, int) and f == FT - 1

        with nc.Block() as block:
            @block.sync
            def _(sp):
                for s in range(3):
                    sp.sem_inc(stored[s], 16)

                for n in range(2, H_PIECES):
                    slot = (n + 1) % 2
                    sp.wait_ge(part_lo, n)
                    up.load_h(sp, n, slot)
                    if n == H_PIECES - 2:
                        with nc.allow_non_contiguous_dma(reason="convolution weights, channel on partition"):
                            for tp in range(3):
                                sp.dma_start(cw[:, tp, :], conv_w[0, tp].rearrange("(f p) -> p f", p=P)).then_inc(consts_loaded, 16)
                            sp.dma_start(cb[:, :], conv_b[0].rearrange("(f p) -> p f", p=P)).then_inc(consts_loaded, 16)
                sp.wait_ge(part_lo, H_PIECES)
                up.load_w(sp, 1, (H_PIECES + 1) % 2)

                def tile(f, s):
                    for c, (at, n) in enumerate(CHUNKS):
                        sp.wait_ge(u_read, f * NC + c + 1)
                        sp.dma_start(f_t[bass.ds(f * P, P), at:at + n], res[:, SLOT[c], 0:n]).then_inc(stored[SLOT[c]], 16)
                        if c == 1 and not (isinstance(f, int) and f >= FT - 2):
                            sp.wait_ge(part_lo, f + (H_PIECES + 1))
                            up.load_w(sp, f + 2, (H_PIECES + s) % 2)

                tile(0, 0)
                with sp.Fori(0, (FT - 4) // 2) as i:
                    for s in range(2):
                        tile(i * 2 + (1 + s), 1 - s)
                tile(FT - 3, 1)
                tile(FT - 2, 0)
                tile(FT - 1, 1)
                for s in range(3):
                    sp.wait_ge(stored[s], 16 * (FT * USES[s] + 1))

            @block.gpsimd
            def _(pool):
                for at in ZEROS:
                    pool.memset(grow[:, at:at + 1], 0.0).then_inc(zeroed, 1)

            @block.tensor
            def _(pe):
                def tile(f, s):
                    pe.wait_ge(part_lo, 1 if is_first(f) else f + (H_PIECES + 1))

                    def product(out, half, c):
                        at, n = CHUNKS[c]
                        for k in range(KT):
                            for a, b in PASSES:
                                mm = pe.matmul(out[:, BANK[c], 0:n], w[a][:, s, k, half * P:(half + 1) * P],
                                               ht[b][:, k, at:at + n],
                                               start=(k, a, b) == (0, HI, HI), stop=(k, a, b) == (KT - 1, LO, HI))
                        return mm

                    def g(c):
                        if is_first(f):
                            pe.wait_ge(part_lo, h_pieces(c))
                        if not (is_first(f) and c < 4):
                            pe.wait_ge(g_read, (f * NC + 1) if c == 4 else ((f - 1) * NC + (5 if c == 0 else c + 1)))
                        product(gps, 0, c).then_inc(g_done, 1)

                    def u(c):
                        if not (is_first(f) and c < 4):
                            pe.wait_ge(u_read, (f * NC + 1) if c == 4 else ((f - 1) * NC + (5 if c == 0 else c + 1)))
                        product(ups, 1, c).then_inc(u_done, 1)

                    chunk_order(g, u)

                every_tile(pe, tile)

            @block.scalar
            def _(act):
                for n in range(H_PIECES):
                    up.high(act, n + 1, (n + 1) % 2, ht[HI][:, :, n * PIECE:(n + 1) * PIECE])
                act.wait_ge(zeroed, len(ZEROS))

                def tile(f, s):
                    def g(c):
                        act.wait_ge(g_done, f * NC + c + 1)
                        if not is_first(f):
                            act.wait_ge(tap[2], (f - 1) * NC + min(c + 2, NC))
                        act.copy(grow[:, G_AT[c]:G_AT[c] + CHUNKS[c][1]], gps[:, BANK[c], 0:CHUNKS[c][1]]).then_inc(g_read, 1)

                    def u(c):
                        act.wait_ge(tap[2], f * NC + c + 1)
                        part = res[:, SLOT[c], 0:CHUNKS[c][1]]
                        act.activation(part, part, ACT.Silu).then_inc(silu_done, 1)
                        if c == 0 and not is_last(f):
                            if not is_first(f):
                                act.wait_ge(u_done, f * NC)
                            up.high(act, piece_of(1) + f, (H_PIECES + 1 + s) % 2, w[HI][:, 1 - s, :, :])

                    chunk_order(g, u)

                every_tile(act, tile)

            @block.vector
            def _(dve):
                for n in range(H_PIECES):
                    at = slice(n * PIECE, (n + 1) * PIECE)
                    up.low(dve, n + 1, (n + 1) % 2, ht[LO][:, :, at], ht[HI][:, :, at])
                dve.wait_ge(consts_loaded, 64)
                dve.wait_ge(zeroed, len(ZEROS))

                def tile(f, s):
                    par = lambda ap: ap[:, bass.ds(f, 1)]

                    def conv(c):
                        u0 = f * NC + c + 1
                        n = CHUNKS[c][1]
                        dve.wait_ge(g_read, f * NC + (c + 2 if c < NC - 2 else c + 1))
                        dve.wait_ge(stored[SLOT[c]], (uses(f, c) + 1) * 16)
                        out = res[:, SLOT[c], 0:n]
                        src = lambda tp: grow[:, G_AT[c] + tp - 1:G_AT[c] + tp - 1 + n]
                        dve.tensor_scalar(out, src(0), par(cw[:, 0]), par(cb[:, :]), ALU.mult, ALU.add).then_inc(tap[0], 1)
                        for tp in (1, 2):
                            dve.wait_ge(tap[tp - 1], u0)
                            dve.scalar_tensor_tensor(out, src(tp), par(cw[:, tp]), out, ALU.mult, ALU.add).then_inc(tap[tp], 1)

                    def gate(c):
                        n = CHUNKS[c][1]
                        dve.wait_ge(u_done, f * NC + c + 1)
                        dve.wait_ge(silu_done, f * NC + c + 1)
                        out = res[:, SLOT[c], 0:n]
                        dve.tensor_tensor(out, out, ups[:, BANK[c], 0:n], ALU.mult).then_inc(u_read, 1)
                        if c == 0 and not is_last(f):
                            up.low(dve, piece_of(1) + f, (H_PIECES + 1 + s) % 2, w[LO][:, 1 - s, :, :], w[HI][:, 1 - s, :, :])

                    conv(0)
                    for c in range(NC):
                        if c + 1 < NC:
                            conv(c + 1)
                        gate(c)

                every_tile(dve, tile)


def ffn_down_phase(nc, f_t, w_down, x1, ln2_g, ln2_b, mod, out_all):
    GT = 4
    GROUPS_LAT = T_LAT // (GT * P)
    CT = T_CTX // P
    TAILS = GT
    KEPT = 14
    assert KEPT % 2 == 0 and KEPT // 2 > TAILS
    with ExitStack() as ctx:
        sb, ps, sem = phase_tools(nc, ctx)
        fst = sb("fd_f_stage", [P, 2, GT * P])
        wst = sb("fd_w_stage", [P, 2, D])
        f = [sb(f"fd_f{h}", [P, 2, GT * P], F32R) for h in (HI, LO)]
        w = [sb(f"fd_w{h}", [P, KEPT + 2, D], F32R) for h in (HI, LO)]
        x = sb("fd_x1", [P, GT, D])
        res = sb("fd_res", [P, GT, D])
        out = sb("fd_out", [P, 2, D])
        gate = sb("fd_gate", [P, 2, D])
        ln_g = sb("fd_ln_g", [P, D])
        ln_b = sb("fd_ln_b", [P, D])
        stats = sb("fd_stats", [P, 12])
        mv = sb("fd_mv", [P, 2])
        veps = sb("fd_veps", [P, 1])
        rstd = sb("fd_rstd", [P, 1])
        waited = sb("fd_waited", [P, 1])
        minus_half = sb("fd_minus_half", [P, 1])
        eps = sb("fd_eps", [P, 1])
        acc = ps("fd_acc", [P, GT, D])

        consts_loaded, half_done = sem("fd_consts_loaded"), sem("fd_half_done")
        f_staged = [sem(f"fd_f_staged{s}") for s in range(2)]
        w_staged = [sem(f"fd_w_staged{s}") for s in range(2)]
        f_hi, f_lo, w_hi, w_lo = sem("fd_f_hi"), sem("fd_f_lo"), sem("fd_w_hi"), sem("fd_w_lo")
        step_done, acc_done, gated = sem("fd_step_done"), sem("fd_acc_done"), sem("fd_gated")
        x_loaded, res_done, stats_done, mv_done = sem("fd_x_loaded"), sem("fd_res_done"), sem("fd_stats_done"), sem("fd_mv_done")
        veps_done, rstd_done, normed, scaled, out_done = (
            sem("fd_veps_done"), sem("fd_rstd_done"), sem("fd_normed"), sem("fd_scaled"), sem("fd_out_done"))
        stored = [sem(f"fd_stored{s}") for s in range(2)]
        f_tiles = f_t.rearrange("(f p) t -> f p t", p=P)
        w_tiles = w_down.rearrange("l (f p) n -> (l f) p n", p=P)
        x_groups = x1[0:T_LAT, :].rearrange("(g t p) d -> g p t d", p=P, t=GT)
        x_ctx = x1[T_LAT:T_ALL, :].rearrange("(t p) d -> p t d", p=P)
        out_tiles = out_all.rearrange("(t p) d -> t p d", p=P)

        def every_step(eng, body, tail, store=lambda *a: None):
            def group(g, tiles, after_first):
                for t in range(KEPT // 2):
                    for s in range(2):
                        body(g, 2 * t + s, s, tiles)
                        if after_first and t < TAILS:
                            tail(g - 1, t, LAT, s)
                    if after_first and 1 <= t <= TAILS:
                        store(g - 1, t - 1)
                with eng.Fori(KEPT // 2, FT // 2 - 1) as i:
                    for s in range(2):
                        body(g, i * 2 + s, s, tiles)
                for s in range(2):
                    body(g, FT - 2 + s, s, tiles)

            group(0, GT, False)
            with eng.Fori(1, GROUPS_LAT) as g:
                group(g, GT, True)
            group(GROUPS_LAT, CT, True)
            for t in range(CT):
                for half in range(2):
                    tail(GROUPS_LAT, t, CTX, half)
                store(GROUPS_LAT, t)

        number = lambda g, t: g * GT + t
        kept = lambda st: isinstance(st, int) and st < KEPT
        loads_w = lambda g, st: is_first(g) or not kept(st)

        def pieces(g, st):
            return g * (FT - KEPT) + st

        def w_at(st, slot):
            return st if kept(st) else KEPT + slot

        is_step = lambda st, n: isinstance(st, int) and st == n
        is_first = lambda g: isinstance(g, int) and g == 0
        is_ctx = lambda g: isinstance(g, int) and g == GROUPS_LAT

        with nc.Block() as block:
            @block.sync
            def _(sp):
                for s in range(2):
                    sp.sem_inc(stored[s], 16)

                def load(g, st, slot, tiles):
                    n = tiles * P
                    if not (is_first(g) and isinstance(st, int) and st < 2):
                        sp.wait_ge(f_lo, g * FT + st - 1)
                    sp.dma_start(fst[:, slot, 0:n], f_tiles[st][:, bass.ds(g * (GT * P), n)]).then_inc(f_staged[slot], 16)
                    if loads_w(g, st):
                        if not (is_first(g) and isinstance(st, int) and st < 2):
                            sp.wait_ge(w_lo, pieces(g, st) - 1)
                        sp.dma_start(wst[:, slot, :], w_tiles[st]).then_inc(w_staged[slot], 16)
                    if is_first(g) and is_step(st, 1):
                        for v in range(2):
                            sp.dma_start(gate[:, v, :], mod[v, GATE2 * D:(GATE2 + 1) * D].partition_broadcast(P)).then_inc(consts_loaded, 16)
                        sp.dma_start(ln_g[:, :], ln2_g[0].partition_broadcast(P)).then_inc(consts_loaded, 16)
                        sp.dma_start(ln_b[:, :], ln2_b[0].partition_broadcast(P)).then_inc(consts_loaded, 16)
                    if is_step(st, FT - 2):
                        if not is_first(g):
                            sp.wait_ge(res_done, g * GT)
                        sp.dma_start(x[:, 0:tiles, :], x_ctx if is_ctx(g) else x_groups[g]).then_inc(x_loaded, 16)

                def store(g, t):
                    sp.wait_ge(out_done, number(g, t) + 1)
                    sp.dma_start(out_tiles[number(g, t)], out[:, t % 2, :]).then_inc(stored[t % 2], 16)

                every_step(sp, load, lambda *a: None, store)
                for s in range(2):
                    sp.wait_ge(stored[s], 16 * ((GROUPS_LAT * GT + CT) // 2 + 1))

            @block.scalar
            def _(act):
                def high(g, st, slot, tiles):
                    n = tiles * P
                    act.wait_ge(f_staged[slot], (g * FT + st - slot) * 8 + 16)
                    if not (is_first(g) and isinstance(st, int) and st < 2):
                        act.wait_ge(step_done, g * FT + st - 1)
                    act.copy(f[HI][:, slot, 0:n], fst[:, slot, 0:n]).then_inc(f_hi, 1)
                    if loads_w(g, st):
                        act.wait_ge(w_staged[slot], (pieces(g, st) - slot) * 8 + 16)
                        act.copy(w[HI][:, w_at(st, slot), :], wst[:, slot, :]).then_inc(w_hi, 1)

                every_step(act, high, lambda *a: None)

            @block.tensor
            def _(pe):
                def step(g, st, slot, tiles):
                    pe.wait_ge(f_lo, g * FT + st + 1)
                    if loads_w(g, st):
                        pe.wait_ge(w_lo, pieces(g, st) + 1)
                    last = is_step(st, FT - 1)
                    for t in range(tiles):
                        if is_step(st, 0) and not is_first(g):
                            pe.wait_ge(gated, number(g - 1, t) + 1)
                        for half in range(2):
                            at = slice(half * 512, (half + 1) * 512)
                            for a, b in PASSES:
                                mm = pe.matmul(acc[:, t, at], f[a][:, slot, t * P:(t + 1) * P], w[b][:, w_at(st, slot), at],
                                               start=is_step(st, 0) and (a, b) == (HI, HI), stop=last and (a, b) == (LO, HI))
                        if last and t < tiles - 1:
                            mm.then_inc(acc_done, 1)
                    mm.then_inc(step_done, 1)

                every_step(pe, step, lambda *a: None)

            @block.vector
            def _(dve):
                def gate_sums(g, tiles, vec):
                    dve.wait_ge(consts_loaded, 64)
                    for t in range(tiles):
                        if t < tiles - 1:
                            dve.wait_ge(acc_done, g * (GT - 1) + t + 1)
                        else:
                            dve.wait_ge(step_done, (g + 1) * FT)
                        dve.wait_ge(scaled, number(g, t) + 1)
                        dve.tensor_tensor(res[:, t, :], acc[:, t, :], gate[:, vec, :], ALU.mult).then_inc(gated, 1)

                def low(g, st, slot, tiles):
                    n = tiles * P
                    dve.wait_ge(f_hi, g * FT + st + 1)
                    dve.tensor_tensor(f[LO][:, slot, 0:n], fst[:, slot, 0:n], f[HI][:, slot, 0:n].bitcast(F32), ALU.subtract).then_inc(f_lo, 1)
                    if loads_w(g, st):
                        dve.wait_ge(w_hi, pieces(g, st) + 1)
                        at = w_at(st, slot)
                        dve.tensor_tensor(w[LO][:, at, :], wst[:, slot, :], w[HI][:, at, :].bitcast(F32), ALU.subtract).then_inc(w_lo, 1)
                    if is_step(st, 0) and not is_first(g):
                        gate_sums(g - 1, GT, LAT)
                    if is_ctx(g) and is_step(st, FT - 1):
                        gate_sums(g, CT, CTX)

                def tail(g, t, vec, half):
                    n = number(g, t)
                    if half == 0:
                        if t == 0:
                            dve.wait_ge(x_loaded, g * 16 + 16)
                        dve.wait_ge(gated, n + 1)
                        dve.scalar_tensor_tensor(res[:, t, :], x[:, t, :], ALPHA, res[:, t, :], ALU.mult, ALU.add).then_inc(res_done, 1)
                        dve.wait_ge(res_done, n + 1)
                        for h in range(2):
                            last = dve.bn_stats(stats[:, h * 6:h * 6 + 6], res[:, t, h * 512:(h + 1) * 512])
                        last.then_inc(stats_done, 1)
                        dve.wait_ge(stats_done, n + 1)
                        dve.tensor_copy(waited[:, :], stats[:, 0:1])
                        dve.bn_aggr(mv[:, :], stats[:, :]).then_inc(mv_done, 1)
                    elif is_ctx(g):
                        dve.wait_ge(mv_done, n + 1)
                        dve.scalar_tensor_tensor(res[:, t, :], res[:, t, :], mv[:, 0:1], ln_g[:, :], ALU.subtract, ALU.mult).then_inc(normed, 1)
                        dve.wait_ge(normed, n + 1)
                        dve.wait_ge(rstd_done, n + 1)
                        dve.wait_ge(stored[t % 2], (n - t % 2) * 8 + 16)
                        dve.scalar_tensor_tensor(out[:, t % 2, :], res[:, t, :], rstd[:, :], ln_b[:, :], ALU.mult, ALU.add).then_inc(out_done, 1)
                    else:
                        dve.wait_ge(rstd_done, n + 1)
                        dve.tensor_scalar(res[:, t, :], res[:, t, :], mv[:, 0:1], rstd[:, :], ALU.subtract, ALU.mult).then_inc(normed, 1)

                every_step(dve, low, tail)

            @block.gpsimd
            def _(pool):
                pool.memset(minus_half[:, :], -0.5).then_inc(half_done, 1)
                pool.memset(eps[:, :], EPS).then_inc(half_done, 1)
                pool.wait_ge(half_done, 2)
                pool.sem_inc(scaled, GT)
                pool.wait_ge(consts_loaded, 64)

                def make_rstd(n):
                    pool.wait_ge(mv_done, n + 1)
                    pool.tensor_tensor(veps[:, :], mv[:, 1:2], eps[:, :], ALU.add).then_inc(veps_done, 1)
                    pool.wait_ge(veps_done, n + 1)
                    pool.tensor_tensor(rstd[:, :], veps[:, :], minus_half[:, :], ALU.pow).then_inc(rstd_done, 1)

                def affine(g, t):
                    n, slot = number(g, t), t % 2
                    pool.wait_ge(normed, n + 1)
                    pool.tensor_tensor(res[:, t, :], res[:, t, :], ln_g[:, :], ALU.mult).then_inc(scaled, 1)
                    pool.wait_ge(scaled, n + GT + 1)
                    pool.wait_ge(stored[slot], (n - slot) * 8 + 16)
                    pool.tensor_tensor(out[:, slot, :], res[:, t, :], ln_b[:, :], ALU.add).then_inc(out_done, 1)

                with pool.Fori(0, GROUPS_LAT) as g:
                    for t in range(GT):
                        make_rstd(number(g, t))
                        affine(g, t)
                for t in range(CT):
                    make_rstd(number(GROUPS_LAT, t))


def shape_constants():
    import numpy as np

    def angles(rows, cols, n):
        return 2 * np.pi * (np.outer(rows, cols) % n) / n

    c64, s64 = np.zeros((P, P)), np.zeros((P, P))
    a = angles(np.arange(64), np.arange(64), 64)
    for h in (0, 64):
        c64[h:h + 64, h:h + 64] = np.cos(a) / 8
        s64[h:h + 64, h:h + 64] = -np.sin(a) / 8
    r = np.arange(512)
    a = angles(r, np.arange(4), T_LAT)
    twiddle = np.stack([np.cos(a), np.sin(a)], -1)
    a = angles(r, np.arange(512), 512)
    dft512 = np.stack([np.cos(a), np.sin(a)]) / np.sqrt(T_LAT)
    a = angles(np.arange(T_CTX), np.arange(T_CTX), T_CTX)
    dft256 = np.stack([np.cos(a), np.sin(a)]) / np.sqrt(T_CTX)
    col = np.arange(GRID)
    start = np.clip(col - 8, 0, GRID - 16)[:, None]
    col_mask = np.where((col >= start) & (col < start + 16), 0.0, MASKED)
    row_mask = np.zeros((2, GRID, 9, GRID))
    row_mask[0, :, 8] = MASKED
    row_mask[1, :, 0] = MASKED
    f = lambda v: np.ascontiguousarray(v, np.float32)
    return {"ident": f(np.eye(P)), "dft_c64": f(c64), "dft_s64": f(s64), "twiddle": f(twiddle),
            "dft512": f(dft512), "dft256": f(dft256),
            "col_mask": f(np.tile(col_mask, (2, 1))), "row_mask": f(row_mask.reshape(P, 9 * GRID))}


def build_program(nc, x_all, conds, cache_k, cache_v, w_ada, b_ada, w_in, a_ws, a_bs, f_w, rpb, w_out, ln1_g, ln1_b,
                  w_gu, conv_w, conv_b, w_down, ln2_g, ln2_b,
                  ident, dft_c64, dft_s64, twiddle, dft512, dft256, col_mask, row_mask,
                  y_all, new_k, new_v):
    def scratch(name, shape, dt=F32):
        return nc.dram_tensor(name, shape, dt, kind="Internal").ap()

    mod = scratch("mod", [2, 6 * D])
    q_t = scratch("q_t", [2, D_C, T_ALL])
    k_t = scratch("k_t", [2, D_C, T_ALL + T_PAST])
    v_parts = scratch("v_parts", [T_ALL + T_PAST, 3 * D_C], BF16)
    chan_dft = scratch("chan_dft", [T_ALL, 2 * D_B])
    y = scratch("y_mixed", [T_ALL, D])
    rpb_pad = scratch("rpb_pad", [1, RPB_PAD + RPB + RPB_PAD])
    rel_bias = scratch("rel_bias", [GRID, HEADS * REL_ROWS, GRID])
    x1 = scratch("x1", [T_ALL, D])
    h2_t = scratch("h2_t", [D, T_ALL])
    f_t = scratch("f_t", [D_FF, T_ALL])

    with nc.cleanup_on_exit():
        with ExitStack() as ctx:
            w = [ctx.enter_context(nc.sbuf_tensor(f"w_in{h}", [P, KT, P_IN], F32R)) for h in (HI, LO)]
            modulation_phase(nc, conds, w_ada, b_ada, w_in, rpb, mod, rpb_pad, w)
            projection_phase(nc, x_all, w, a_ws, a_bs, f_w, ident, dft_c64, dft_s64,
                             mod, rpb_pad, rel_bias, y, q_t, k_t, v_parts, chan_dft, new_k, new_v)
        fourier_phase(nc, chan_dft, twiddle, dft512, dft256, conds, w_ada, b_ada, cache_k, cache_v, ident,
                      mod, k_t, v_parts, y)
    with ExitStack() as up_ctx:
        with ExitStack() as out_ctx:
            wo = OutOperands(nc, out_ctx, w_out)
            attention_phase(nc, q_t, k_t, v_parts, rel_bias, col_mask, row_mask, ident, y, wo)
            up = UpOperands(nc, up_ctx, h2_t, w_gu)
            mix_phase(nc, y, x_all, wo.w, ln1_g, ln1_b, mod, ident, x1, h2_t, up)
        ffn_up_phase(nc, up, conv_w, conv_b, f_t)
    ffn_down_phase(nc, f_t, w_down, x1, ln2_g, ln2_b, mod, y_all)


WEIGHTS = ("cache_k", "cache_v", "w_ada", "b_ada", "w_in", "a_ws", "a_bs", "f_w", "rpb", "w_out", "ln1_g", "ln1_b",
           "w_gu", "conv_w", "conv_b", "w_down", "ln2_g", "ln2_b")
TABLES = ("ident", "dft_c64", "dft_s64", "twiddle", "dft512", "dft256", "col_mask", "row_mask")


def kernel(**inputs):
    import numpy as np
    import concourse.bacc as bacc
    from concourse.bass_utils import run_bass_kernel_spmd

    arrays = {"x_all": np.concatenate([inputs["x_sample"][0], inputs["x_prompt"][0]]),
              "conds": np.stack([inputs["c"][0], inputs["c_ctx"]])}
    arrays.update((name, np.ascontiguousarray(inputs[name])) for name in WEIGHTS)
    tables = shape_constants()
    arrays.update((name, tables[name]) for name in TABLES)
    outputs = {"y_all": (T_ALL, D), "new_k": (T_CTX, D_C), "new_v": (T_CTX, D_C)}

    nc = bacc.Bacc("TRN2", target_bir_lowering=False, num_devices=1)
    args = [nc.dram_tensor(f"in_{name}_dram", a.shape, mybir.dt.from_np(a.dtype), kind="ExternalInput").ap()
            for name, a in arrays.items()]
    args += [nc.dram_tensor(f"out_{name}_dram", shape, F32, kind="ExternalOutput").ap() for name, shape in outputs.items()]
    build_program(nc, *args)
    r = run_bass_kernel_spmd(nc, [{f"in_{name}_dram": a for name, a in arrays.items()}], core_ids=[0])
    y_all, new_k, new_v = (r.results[0][f"out_{name}_dram"] for name in outputs)
    cache_shape = (1, 1, T_CTX, HEADS, HD)
    return (y_all[T_LAT:].reshape(1, T_CTX, D), y_all[:T_LAT].reshape(1, T_LAT, D),
            new_k.reshape(cache_shape), new_v.reshape(cache_shape))
```
